# Optimizing a Trainium2 kernel written in Bass

```python
import math
import jax, jax.numpy as jnp
from jax import lax
import numpy as np

D_MODEL = 1024
BATCH = 1
SEQ = 512
DEPTH = 1
DEC_BATCH = 1
DEC_SEQ = 64
PAST_LEN = 512

CHUNK = 64
Q_BLOCK = 128
EPS = 1e-6
SSM_HEADS = 16
SSM_HEAD_DIM = 64
SSM_INNER = SSM_HEADS * SSM_HEAD_DIM
SSM_GROUPS = 2
SSM_STATE = 128
CONV_W = 4
CONV_DIM = SSM_INNER + 2 * SSM_GROUPS * SSM_STATE
SB_HEADS = 8
SB_HEAD_DIM = 64
SB_INNER = SB_HEADS * SB_HEAD_DIM
MEM_LEN = 256
MEM_HEADS = 4
MEM_HEAD_DIM = D_MODEL // MEM_HEADS
MOE_GROUPS = 4
EXPERTS_PER_GROUP = 4
N_EXPERTS = MOE_GROUPS * EXPERTS_PER_GROUP
TOP_K_INNER = 2
D_FF_EXPERT = 512
IN_SIZES = (SSM_INNER, CONV_DIM, SSM_HEADS, SB_INNER, SB_INNER, SB_INNER, D_MODEL, D_MODEL)
IN_COLS = sum(IN_SIZES)

kernel_name = "hybrid_ssd_stickbreak_hmoe_stream_step"

def rmsnorm(x, g):
    xf = x.astype(jnp.float32)
    r = lax.rsqrt(jnp.mean(xf * xf, axis=-1, keepdims=True) + EPS)
    return (xf * r).astype(x.dtype) * g

def split_cols(proj):
    idx = np.cumsum(np.array(IN_SIZES))[:-1].tolist()
    return jnp.split(proj, idx, axis=-1)

def ssd_chunked(xh, dt, a, bm, cm, h0):
    f32 = jnp.float32
    bsz, L, H, P = xh.shape
    c = min(CHUNK, L)
    nc = L // c
    rep = H // SSM_GROUPS
    xf = xh.astype(f32).reshape(bsz, nc, c, H, P)
    bf = jnp.repeat(bm.astype(f32), rep, axis=2).reshape(bsz, nc, c, H, SSM_STATE)
    cf = jnp.repeat(cm.astype(f32), rep, axis=2).reshape(bsz, nc, c, H, SSM_STATE)
    dtc = dt.astype(f32).reshape(bsz, nc, c, H)
    cum = jnp.cumsum(dtc * a, axis=2)
    tri = jnp.tril(jnp.ones((c, c), dtype=bool))
    seg = cum[:, :, :, None, :] - cum[:, :, None, :, :]
    decay = jnp.exp(jnp.where(tri[None, None, :, :, None], seg, -jnp.inf))
    xdt = xf * dtc[..., None]
    cb = jnp.einsum('bzthn,bzshn->bztsh', cf, bf)
    y_intra = jnp.einsum('bztsh,bzshp->bzthp', cb * decay, xdt)
    to_end = jnp.exp(cum[:, :, -1:, :] - cum)
    states = jnp.einsum('bzshn,bzshp->bzhpn', bf, xdt * to_end[..., None])
    chunk_decay = jnp.exp(cum[:, :, -1, :])

    def carry_step(hc, inp):
        s_z, d_z = inp
        return hc * d_z[:, :, None, None] + s_z, hc

    h_last, h_in = lax.scan(carry_step, h0.astype(f32),
                            (jnp.moveaxis(states, 1, 0), jnp.moveaxis(chunk_decay, 1, 0)))
    h_in = jnp.moveaxis(h_in, 0, 1)
    y_inter = jnp.einsum('bzthn,bzhpn->bzthp', cf * jnp.exp(cum)[..., None], h_in)
    y = (y_intra + y_inter).reshape(bsz, L, H, P)
    return y.astype(xh.dtype), h_last.astype(h0.dtype)

def stick_breaking(q, k_all, v_all, q_offset):
    f32 = jnp.float32
    bsz, L, H, d = q.shape
    blk = min(Q_BLOCK, L)
    nb = L // blk
    k_pos = jnp.arange(k_all.shape[1], dtype=jnp.int32)
    scale = SB_HEAD_DIM ** -0.5

    def one_block(args):
        qb, i = args
        q_pos = q_offset + i * blk + jnp.arange(blk, dtype=jnp.int32)
        z = jnp.einsum('bqhd,bkhd->bhqk', qb, k_all).astype(f32) * scale
        causal = k_pos[None, :] < q_pos[:, None]
        log_keep = jnp.where(causal, jax.nn.log_sigmoid(-z), 0.0)
        after = lax.cumsum(log_keep, axis=3, reverse=True) - log_keep
        w = jnp.where(causal, jnp.exp(jax.nn.log_sigmoid(z) + after), 0.0)
        return jnp.einsum('bhqk,bkhd->bqhd', w.astype(v_all.dtype), v_all)

    qb = jnp.moveaxis(q.reshape(bsz, nb, blk, H, d), 1, 0)
    o = lax.map(one_block, (qb, jnp.arange(nb, dtype=jnp.int32)))
    return jnp.moveaxis(o, 0, 1).reshape(bsz, L, H, d)

def mixer_block(x, conv_ctx, ssm_h0, past_k, past_v, norm_mix, w_in, conv_w, conv_b, dt_bias,
                a_log, d_skip, ssm_norm, w_ssm_br, w_sb_br, w_out):
    bsz, L, _ = x.shape
    h = rmsnorm(x, norm_mix)
    z, xbc_raw, dt_raw, q, k, v, gl_ssm, gl_sb = split_cols(h @ w_in)
    xbc_all = jnp.concatenate([conv_ctx, xbc_raw], axis=1)
    new_conv = xbc_all[:, -(CONV_W - 1):]
    conv = conv_b
    for j in range(CONV_W):
        conv = conv + xbc_all[:, j:j + L] * conv_w[j]
    xbc = jax.nn.silu(conv)
    xs, bm, cm = jnp.split(xbc, [SSM_INNER, SSM_INNER + SSM_GROUPS * SSM_STATE], axis=-1)
    xh = xs.reshape(bsz, L, SSM_HEADS, SSM_HEAD_DIM)
    bm = bm.reshape(bsz, L, SSM_GROUPS, SSM_STATE)
    cm = cm.reshape(bsz, L, SSM_GROUPS, SSM_STATE)
    dt = jax.nn.softplus((dt_raw + dt_bias).astype(jnp.float32))
    a = -jnp.exp(a_log.astype(jnp.float32))
    y, h_last = ssd_chunked(xh, dt, a, bm, cm, ssm_h0)
    y = (y + d_skip[:, None] * xh).reshape(bsz, L, SSM_INNER)
    y_ssm = rmsnorm(y * jax.nn.silu(z), ssm_norm) @ w_ssm_br
    qh = q.reshape(bsz, L, SB_HEADS, SB_HEAD_DIM)
    kh = k.reshape(bsz, L, SB_HEADS, SB_HEAD_DIM)
    vh = v.reshape(bsz, L, SB_HEADS, SB_HEAD_DIM)
    if past_k is None:
        k_all, v_all, off = kh, vh, 0
    else:
        k_all = jnp.concatenate([past_k, kh], axis=1)
        v_all = jnp.concatenate([past_v, vh], axis=1)
        off = past_k.shape[1]
    y_sb = stick_breaking(qh, k_all, v_all, off).reshape(bsz, L, SB_INNER) @ w_sb_br
    merged = jax.nn.sigmoid(gl_ssm) * y_ssm + jax.nn.sigmoid(gl_sb) * y_sb
    return x + merged @ w_out, new_conv, h_last, kh, vh

def memory_kv(mem, norm_mem_kv, w_mem_kv):
    bsz, M, _ = mem.shape
    k, v = jnp.split(rmsnorm(mem, norm_mem_kv) @ w_mem_kv, 2, axis=-1)
    return (k.reshape(bsz, M, MEM_HEADS, MEM_HEAD_DIM), v.reshape(bsz, M, MEM_HEADS, MEM_HEAD_DIM))

def memory_block(x, mk, mv, norm_mem_q, w_mem_q, w_mem_o):
    bsz, L, _ = x.shape
    q = (rmsnorm(x, norm_mem_q) @ w_mem_q).reshape(bsz, L, MEM_HEADS, MEM_HEAD_DIM)
    s = jnp.einsum('bqhd,bkhd->bhqk', q, mk).astype(jnp.float32) * (MEM_HEAD_DIM ** -0.5)
    p = jax.nn.softmax(s, axis=-1).astype(mv.dtype)
    o = jnp.einsum('bhqk,bkhd->bqhd', p, mv).reshape(bsz, L, D_MODEL)
    return x + o @ w_mem_o

def hier_moe(x, norm_ffn, w_group_router, w_expert_router, w_gate_e, w_up_e, w_down_e):
    bsz, L, _ = x.shape
    h = rmsnorm(x, norm_ffn).reshape(bsz * L, D_MODEL)
    p_group = jax.nn.softmax((h @ w_group_router).astype(jnp.float32), axis=-1)
    p_sel, g_sel = lax.top_k(p_group, 1)
    le = (h @ w_expert_router).astype(jnp.float32).reshape(-1, MOE_GROUPS, EXPERTS_PER_GROUP)
    le_sel = jnp.take_along_axis(le, g_sel[:, :, None], axis=1)[:, 0]
    top_v, top_i = lax.top_k(le_sel, TOP_K_INNER)
    gate = jax.nn.softmax(top_v, axis=-1) * p_sel
    eid = g_sel * EXPERTS_PER_GROUP + top_i
    dense_w = jnp.sum(jax.nn.one_hot(eid, N_EXPERTS, dtype=jnp.float32) * gate[..., None], axis=1)
    dense_w = dense_w.astype(h.dtype)
    out = jnp.zeros_like(h)
    for e in range(N_EXPERTS):
        he = jax.nn.silu(h @ w_gate_e[e]) * (h @ w_up_e[e])
        out = out + dense_w[:, e:e + 1] * (he @ w_down_e[e])
    return x + out.reshape(bsz, L, D_MODEL)

def setup_inputs(seed: int = 0) -> dict:
    key = jax.random.key(seed)
    ks = jax.random.split(key, 40)
    f32 = jnp.float32
    nrm = lambda k, shape, s: jax.random.normal(k, shape, f32) * s
    gain = lambda k, shape: 1.0 + 0.01 * jax.random.normal(k, shape, f32)
    dt0 = jnp.exp(jax.random.uniform(ks[20], (DEPTH, SSM_HEADS), f32) * (math.log(0.1) - math.log(0.001)) + math.log(0.001))
    return {
        "x_prompt": nrm(ks[0], (BATCH, SEQ, D_MODEL), 1.0),
        "x_sample": nrm(ks[1], (DEC_BATCH, DEC_SEQ, D_MODEL), 1.0),
        "cache_sb_k": nrm(ks[2], (DEPTH, DEC_BATCH, PAST_LEN, SB_HEADS, SB_HEAD_DIM), 1.0),
        "cache_sb_v": nrm(ks[3], (DEPTH, DEC_BATCH, PAST_LEN, SB_HEADS, SB_HEAD_DIM), 1.0),
        "state_ssm": nrm(ks[4], (DEPTH, DEC_BATCH, SSM_HEADS, SSM_HEAD_DIM, SSM_STATE), 0.5),
        "state_conv": nrm(ks[5], (DEPTH, DEC_BATCH, CONV_W - 1, CONV_DIM), 1.0),
        "cache_mem_k": nrm(ks[6], (DEPTH, DEC_BATCH, MEM_LEN, MEM_HEADS, MEM_HEAD_DIM), 1.0),
        "cache_mem_v": nrm(ks[7], (DEPTH, DEC_BATCH, MEM_LEN, MEM_HEADS, MEM_HEAD_DIM), 1.0),
        "mem_prompt": nrm(ks[8], (BATCH, MEM_LEN, D_MODEL), 1.0),
        "norm_mix": gain(ks[9], (DEPTH, D_MODEL)),
        "w_in": nrm(ks[10], (DEPTH, D_MODEL, IN_COLS), D_MODEL ** -0.5),
        "conv_w": nrm(ks[11], (DEPTH, CONV_W, CONV_DIM), CONV_W ** -0.5),
        "conv_b": nrm(ks[12], (DEPTH, CONV_DIM), 0.01),
        "dt_bias": dt0 + jnp.log(-jnp.expm1(-dt0)),
        "a_log": jnp.log(jax.random.uniform(ks[13], (DEPTH, SSM_HEADS), f32, 1.0, 16.0)),
        "d_skip": gain(ks[14], (DEPTH, SSM_HEADS)),
        "ssm_norm": gain(ks[15], (DEPTH, SSM_INNER)),
        "w_ssm_br": nrm(ks[16], (DEPTH, SSM_INNER, D_MODEL), SSM_INNER ** -0.5),
        "w_sb_br": nrm(ks[17], (DEPTH, SB_INNER, D_MODEL), SB_INNER ** -0.5),
        "w_out": nrm(ks[18], (DEPTH, D_MODEL, D_MODEL), D_MODEL ** -0.5),
        "norm_mem_q": gain(ks[19], (DEPTH, D_MODEL)),
        "norm_mem_kv": gain(ks[21], (DEPTH, D_MODEL)),
        "w_mem_q": nrm(ks[22], (DEPTH, D_MODEL, D_MODEL), D_MODEL ** -0.5),
        "w_mem_kv": nrm(ks[23], (DEPTH, D_MODEL, 2 * D_MODEL), D_MODEL ** -0.5),
        "w_mem_o": nrm(ks[24], (DEPTH, D_MODEL, D_MODEL), D_MODEL ** -0.5),
        "norm_ffn": gain(ks[25], (DEPTH, D_MODEL)),
        "w_group_router": nrm(ks[26], (DEPTH, D_MODEL, MOE_GROUPS), D_MODEL ** -0.5),
        "w_expert_router": nrm(ks[27], (DEPTH, D_MODEL, N_EXPERTS), D_MODEL ** -0.5),
        "w_gate_e": nrm(ks[28], (DEPTH, N_EXPERTS, D_MODEL, D_FF_EXPERT), D_MODEL ** -0.5),
        "w_up_e": nrm(ks[29], (DEPTH, N_EXPERTS, D_MODEL, D_FF_EXPERT), D_MODEL ** -0.5),
        "w_down_e": nrm(ks[30], (DEPTH, N_EXPERTS, D_FF_EXPERT, D_MODEL), D_FF_EXPERT ** -0.5),
        "norm_final": gain(ks[31], (D_MODEL,)),
    }

def reference(x_prompt, x_sample, cache_sb_k, cache_sb_v, state_ssm, state_conv, cache_mem_k,
              cache_mem_v, mem_prompt, norm_mix, w_in, conv_w, conv_b, dt_bias, a_log, d_skip,
              ssm_norm, w_ssm_br, w_sb_br, w_out, norm_mem_q, norm_mem_kv, w_mem_q, w_mem_kv,
              w_mem_o, norm_ffn, w_group_router, w_expert_router, w_gate_e, w_up_e, w_down_e,
              norm_final):
    xp, xs = x_prompt, x_sample
    bp = xp.shape[0]
    skp, svp, ssp, scp, mkp, mvp = [], [], [], [], [], []
    sks, svs, sss, scs = [], [], [], []
    for l in range(DEPTH):
        mw = (norm_mix[l], w_in[l], conv_w[l], conv_b[l], dt_bias[l], a_log[l], d_skip[l],
              ssm_norm[l], w_ssm_br[l], w_sb_br[l], w_out[l])
        mq = (norm_mem_q[l], w_mem_q[l], w_mem_o[l])
        fw = (norm_ffn[l], w_group_router[l], w_expert_router[l], w_gate_e[l], w_up_e[l], w_down_e[l])
        conv0 = jnp.zeros((bp, CONV_W - 1, CONV_DIM), xp.dtype)
        h0 = jnp.zeros((bp, SSM_HEADS, SSM_HEAD_DIM, SSM_STATE), xp.dtype)
        xp, conv_p, ssm_p, k_p, v_p = mixer_block(xp, conv0, h0, None, None, *mw)
        mk_p, mv_p = memory_kv(mem_prompt, norm_mem_kv[l], w_mem_kv[l])
        xp = memory_block(xp, mk_p, mv_p, *mq)
        xp = hier_moe(xp, *fw)
        skp.append(k_p); svp.append(v_p); ssp.append(ssm_p); scp.append(conv_p)
        mkp.append(mk_p); mvp.append(mv_p)
        xs, conv_s, ssm_s, k_s, v_s = mixer_block(xs, state_conv[l], state_ssm[l], cache_sb_k[l],
                                                  cache_sb_v[l], *mw)
        xs = memory_block(xs, cache_mem_k[l], cache_mem_v[l], *mq)
        xs = hier_moe(xs, *fw)
        sks.append(k_s); svs.append(v_s); sss.append(ssm_s); scs.append(conv_s)
    y_prompt = rmsnorm(xp, norm_final)
    y_sample = rmsnorm(xs, norm_final)
    return (y_prompt, y_sample, jnp.stack(skp), jnp.stack(svp), jnp.stack(ssp), jnp.stack(scp),
            jnp.stack(mkp), jnp.stack(mvp), jnp.stack(sks), jnp.stack(svs), jnp.stack(sss),
            jnp.stack(scs))


_drawn_inputs = setup_inputs


def setup_inputs(seed=0):
    import zlib

    import numpy as np

    out = dict(_drawn_inputs(seed))
    spreads = {}
    factors = {'cache_sb_k': 2.729,
     'norm_mix': 3.288,
     'conv_b': 4.029,
     'd_skip': 41.576,
     'ssm_norm': 4.95,
     'norm_mem_q': 8.0,
     'norm_mem_kv': 5.496,
     'norm_ffn': 3.131,
     'norm_final': 33.502}
    for name, (base, spread) in spreads.items():
        noise = np.random.default_rng([zlib.crc32(name.encode()), seed]).standard_normal(out[name].shape)
        drawn = base * np.exp(spread * noise) if base else spread * noise
        out[name] = __import__('jax').numpy.asarray(drawn.astype(out[name].dtype))
    for name, factor in factors.items():
        out[name] = (out[name] * factor).astype(out[name].dtype)
    return out
```

```python
from contextlib import ExitStack

import numpy as np
import concourse.bass as bass
from concourse import mybir

F32 = mybir.dt.float32
U32 = mybir.dt.uint32
ACT = mybir.ActivationFunctionType
ALU = mybir.AluOpType
AX = mybir.AxisListType

P = 128
D = 1024
KD = D // P
LP, LS = 512, 64
T = LP + LS
CH = [(0, 128), (128, 128), (256, 128), (384, 128), (512, 64)]
NC_ = len(CH)
PAST = 512
NH, HD, NS = 16, 64, 128
SBH = 8
MH, MHD, ML = 4, 256, 256
NE, FF, TOPG, EPG = 16, 512, 4, 4
CONV_C = 12
EPS = 1e-6
TS = NC_ * P
CAP = NC_ * P
BIG = 1.0e30
C_Z, C_X, C_DT, C_Q, C_K, C_V, C_GS, C_GB = 0, 1024, 2560, 2576, 3088, 3600, 4112, 5136
NRING = 3
NMRING = 6
NXG = 4


class Arena:

    def __init__(self, t, words):
        self.t, self.words, self.at = t, words, 0

    def mark(self):
        return self.at

    def back(self, at):
        self.at = at

    def view(self, *shape):
        n = int(np.prod(shape))
        a = self.t[:, self.at:self.at + n]
        self.at += n
        assert self.at <= self.words, (self.at, self.words)
        if len(shape) == 1:
            return a
        names = "abcd"[:len(shape)]
        return a.rearrange("p (%s) -> p %s" % (" ".join(names), " ".join(names)),
                           **{c: s for c, s in zip(names[:-1], shape[:-1])})


def bc(ap, shape):
    return ap.to_broadcast(list(shape))


def encoder_step(nc, I, O):
    ctx = ExitStack()
    with ctx:
        sem_names = []

        def sem(name):
            assert name not in sem_names
            sem_names.append(name)
            return ctx.enter_context(nc.semaphore(name))

        WORDS = 53200
        arena_t = ctx.enter_context(nc.sbuf_tensor("arena", [P, WORDS], F32))
        A = Arena(arena_t, WORDS)
        ps = ctx.enter_context(nc.psum_tensor("ps", [P, 8 * 512], F32))
        bank = lambda b, n=1: ps[:, b * 512:(b + n) * 512]
        hn_rows = nc.dram_tensor("hn_rows", [T, D], F32, kind="Internal").ap()
        y_rows = nc.dram_tensor("y_rows", [NE * CAP, D], F32, kind="Internal").ap()

        X = A.view(NC_, D)
        HT = A.view(KD, T)
        IDENT = A.view(P)
        TSUF = A.view(P)
        TINC = A.view(P)
        TSTR = A.view(P)
        ONES = A.view(P)
        VT = A.view(100)
        CTXT = A.view(36)
        SS = A.view(24)
        RL = A.view(24)
        RI = A.view(24)
        DP = A.view(8)
        CST = A.view(4)
        HCOL = A.view(4)
        G_MIX, G_MKV, G_SSM, G_MQ, G_FFN = (VT[:, 8 * i:8 * i + 8] for i in range(5))
        CB = VT[:, 40:52]
        CW = VT[:, 52:100].rearrange("p (j c) -> p j c", j=4)
        WR = A.view(KD, 20)
        RING = [A.view(4096) for _ in range(NRING)]
        base = A.mark()

        XN = [A.view(D) for _ in range(2)]
        SQ = A.view(D)
        MT = A.view(KD, ML)
        YSBT = A.view(4, T)
        mix = A.mark()

        VEC = A.view(P)
        CTXR = A.view(P)
        KR = A.view(NC_, 512)
        VR = A.view(NC_, 512)
        PVR = A.view(4, 512)
        QT = A.view(4, T)
        KTA = A.view(4, 9 * P)
        att = A.mark()
        MR = A.view(2, D)
        PKR = A.view(4, 512)
        A.back(att)
        ZSB = [A.view(1280) for _ in range(3)]
        LB = [A.view(1280) for _ in range(2)]
        A.back(mix)

        XC = A.view(CONV_C, TS)
        ZS = A.view(KD, T)
        ssd = A.mark()
        XR = [A.view(584) for _ in range(3)]
        CV = [A.view(580) for _ in range(2)]
        UD, AD = A.view(T), A.view(T)
        TAIL = A.view(2, 3, CONV_C)
        TAILR = A.view(2, P)
        WDT = A.view(KD, NH)
        DTA, RST = A.view(TS), A.view(TS)
        ssd2 = A.mark()
        A.back(ssd)
        SEG = [A.view(8, P) for _ in range(2)]
        T1 = [A.view(4, P) for _ in range(2)]
        DX = A.view(4, P)
        assert A.at <= ssd + 3 * 584 + 2 * 580 + 2 * T
        HS = A.view(2, 2, 512)
        assert A.at <= ssd2
        A.back(ssd2)
        DTT, CUM, ECM = (A.view(TS) for _ in range(3))
        SELP = A.view(NH, HD)
        DIAG = A.view(NC_, NH)
        CR, DR, TE, CD, WRW = (A.view(NC_, NH) for _ in range(5))
        H0R = HO = A.view(8, P)
        A.back(base)
        XD = [A.view(512) for _ in range(2)]
        XW = [A.view(512) for _ in range(2)]
        BROW = [A.view(P) for _ in range(2)]
        CBM = [A.view(P) for _ in range(2)]
        ECS = A.view(512)
        assert A.at <= base + 3 * D
        A.back(mix)

        MG = A.view(KD, T)
        RB = A.view(T)
        GS = [A.view(T) for _ in range(2)]
        assert A.at <= mix + CONV_C * TS
        A.back(ssd)
        GB = [A.view(T) for _ in range(2)]
        M1 = [A.view(T) for _ in range(2)]
        SQT = [A.view(T) for _ in range(2)]
        A.back(mix)

        A.back(mix - 4 * T)
        OT = A.view(KD, T)
        QM = A.view(KD, T)
        MKV = A.view(2, 2 * D)
        MC = A.view(2, 2, D)
        late = A.mark()
        KM = A.view(2, KD, ML)
        PX = [A.view(ML) for _ in range(2)]
        PT = [A.view(2, T) for _ in range(2)]
        NM = A.view(20)
        RS = A.view(20)
        RR = A.view(20)
        A.back(late)
        XNR = A.view(NC_, D)

        A.back(base)
        RING2 = [A.view(4096) for _ in range(NMRING - NRING)]
        MSLOT = RING + RING2
        XG = [A.view(D) for _ in range(NXG)]
        GT = [A.view(KD, P) for _ in range(2)]
        SG = [A.view(FF) for _ in range(2)]
        HE = [A.view(FF) for _ in range(2)]
        HET = [A.view(4, P) for _ in range(2)]
        A.back(late)
        assert A.at >= base + 3 * 4096 + NXG * D + 2048 + 3 * 1024
        A.view(NC_, D)
        YO = [A.view(D) for _ in range(2)]
        A.back(late)
        NF = A.view(D)
        GM = [A.view(NC_, P) for _ in range(2)]
        IOTA = A.view(P)
        ECAP = A.view(NE)
        W4 = A.view(4)
        TW = A.view(NC_, NE, 2)
        LG = A.view(NC_, 20)
        MX, SM, PSEL, MA, MB, EX, DEN, GA, GB_, RF = (A.view(NC_) for _ in range(10))
        E4, EQ, OHG, LSEL, OH1, L2, OH2 = (A.view(NC_, 4) for _ in range(7))
        TMP, S1, S2, MK, DW, POSP, POSM, TMP2 = (A.view(NC_, NE) for _ in range(8))
        R1F, R2F = A.view(NC_), A.view(NC_)
        R12 = A.view(2, NC_)
        SLOT = A.view(NE, 2)
        IDX = A.view(NE)
        CNT = A.view(NE)
        FLAG = A.view(2)
        PC = A.view(NC_)
        TWO = A.view(NC_, 2)
        SLOTO = A.view(2)
        IDXO = A.view(1)
        assert A.at <= late + NC_ * D
        x_loaded = [sem(f"x_loaded{i}") for i in range(NC_)]
        mem_loaded = [sem(f"mem_loaded{i}") for i in range(2)]
        vec_loaded = sem("vec_loaded")
        past_loaded = sem("past_loaded")
        cols_loaded = sem("cols_loaded")
        ring_loaded = [sem(f"ring_loaded{i}") for i in range(NRING)]
        state_loaded = sem("state_loaded")
        memc_loaded = sem("memc_loaded")
        out_stored = sem("out_stored")
        late_stored = sem("late_stored")
        const0 = sem("const0")
        consts = sem("consts")
        vec_psum = sem("vec_psum")
        vec_ready = sem("vec_ready")
        sel_ready = sem("sel_ready")
        dp_psum = sem("dp_psum")
        ss_ready, rl_ready, ri_ready, xn_ready, tp_psum, ht_ready = (
            sem(n) for n in ("ss_ready", "rl_ready", "ri_ready", "xn_ready", "tp_psum", "ht_ready"))
        N_A, N_G, N_I, N_F = 0, 7, 12, 17
        kv_psum, kv_rows = sem("kv_psum"), sem("kv_rows")
        q_psum, q_ready = sem("q_psum"), sem("q_ready")
        kt_psum, kt_ready = sem("kt_psum"), sem("kt_ready")
        z_psum, z_abs, z_copied, z_exp, l_ready = (sem(n) for n in ("z_psum", "z_abs", "z_copied", "z_exp", "l_ready"))
        sp_raw, sp_ready, s_psum, u_ready, w_raw, w_ready, pv_psum, ysb_ready = (
            sem(n) for n in ("sp_raw", "sp_ready", "s_psum", "u_ready", "w_raw", "w_ready", "pv_psum", "ysb_ready"))

        w_in = I["w_in"][0].rearrange("(k p) n -> p k n", p=P)

        def cols(w, c0, n):
            return w.rearrange("(k p) n -> p k n", p=P)[:, :, c0:c0 + n]

        def tile8(slot):
            return RING[slot].rearrange("p (k n) -> p k n", k=KD)

        def mtile(slot):
            return RING[slot][:, 0:28 * P].rearrange("p (k n) -> p k n", k=28)

        loads = []
        for c in (C_K, C_V, C_Q, C_X, C_X + 512, C_X + 1024, C_Z, C_Z + 512):
            loads.append([(tile8, w_in[:, :, c:c + 512])])
        W_K, W_V, W_Q, W_X, W_Z = 0, 1, 2, 3, 6
        W_M = len(loads)
        for c in range(KD):
            loads.append([
                (lambda s: mtile(s)[:, 0:8, :], w_in[:, :, C_GS + c * P:C_GS + (c + 1) * P]),
                (lambda s: mtile(s)[:, 8:16, :], w_in[:, :, C_GB + c * P:C_GB + (c + 1) * P]),
                (lambda s: mtile(s)[:, 16:24, :], cols(I["w_ssm_br"][0], c * P, P)),
                (lambda s: mtile(s)[:, 24:28, :], cols(I["w_sb_br"][0], c * P, P)),
            ])
        W_O = len(loads)
        for c in range(2):
            loads.append([(tile8, cols(I["w_out"][0], 512 * c, 512))])
        W_KV = len(loads)
        for c in range(4):
            loads.append([(tile8, cols(I["w_mem_kv"][0], 512 * c, 512))])
        W_MQ = len(loads)
        for c in range(2):
            loads.append([(tile8, cols(I["w_mem_q"][0], 512 * c, 512))])
        W_MO = len(loads)
        for c in range(2):
            loads.append([(tile8, cols(I["w_mem_o"][0], 512 * c, 512))])
        landed, tot = [], [0] * NRING
        for n, parts in enumerate(loads):
            tot[n % NRING] += 16 * len(parts)
            landed.append(tot[n % NRING])

        def weights(eng, n):
            eng.wait_ge(ring_loaded[n % NRING], landed[n])

        xb_psum, xr_ready, conv_done, xc_ready = (sem(n) for n in ("xb_psum", "xr_ready", "conv_done", "xc_ready"))
        zt_psum, zt_ready = sem("zt_psum"), sem("zt_ready")
        dt_psum = sem("dt_psum")
        dve_dt, act_dt = sem("dve_dt"), sem("act_dt")
        pads = sem("pads")
        tail_psum, tail_rows = sem("tail_psum"), sem("tail_rows")
        pre_psum, h0_psum, pre_dve, pre_act = sem("pre_psum"), sem("h0_psum"), sem("pre_dve"), sem("pre_act")
        (ssd_tr, sx_done, cumb_psum, seg_done, e_ready, m_ready, ec_psum, ec_done, inter_psum, t1_done,
         intra_psum, t2_done, st_psum, h_dec, h_ready, dx_ready, t3_done, yz_done) = (
            sem(n) for n in ("ssd_tr", "sx_done", "cumb_psum", "seg_done", "e_ready", "m_ready", "ec_psum",
                             "ec_done", "inter_psum", "t1_done", "intra_psum", "t2_done", "st_psum", "h_dec",
                             "h_ready", "dx_ready", "t3_done", "yz_done"))
        so_psum, so_rows = sem("so_psum"), sem("so_rows")
        sq_ready, ssq_psum, rb_ln, rb_ready, yn_ready = (
            sem(n) for n in ("sq_ready", "ssq_psum", "rb_ln", "rb_ready", "yn_ready"))
        (gs_psum, gb_psum, br_psum, sb_psum, gs_ready, gb_ready, m1_done, m2_done, mg_ready) = (
            sem(n) for n in ("gs_psum", "gb_psum", "br_psum", "sb_psum", "gs_ready", "gb_ready", "m1_done",
                             "m2_done", "mg_ready"))
        wo_psum, x1_ready = sem("wo_psum"), sem("x1_ready")
        mkv_psum, mkv_rows, km_psum, km_ready = (sem(n) for n in ("mkv_psum", "mkv_rows", "km_psum", "km_ready"))
        mq_psum, mq_ready = sem("mq_psum"), sem("mq_ready")
        (ms_psum, nm_ready, px_ready, rr_ready, pn_ready, pt_psum, pt_ready, ot_psum, ot_ready) = (
            sem(n) for n in ("ms_psum", "nm_ready", "px_ready", "rr_ready", "pn_ready", "pt_psum", "pt_ready",
                             "ot_psum", "ot_ready"))
        mo_psum, x2_ready = sem("mo_psum"), sem("x2_ready")

        retire = {W_K: (kv_psum, 5), W_V: (kv_psum, 10), W_Q: (q_psum, 4)}
        for j in range(3):
            retire[W_X + j] = (xb_psum, 4 * (j + 1))
        for j in range(2):
            retire[W_Z + j] = (zt_psum, 4 * (j + 1))
            retire[W_O + j] = (wo_psum, 2 * NC_ - 1 + j)
            retire[W_MQ + j] = (mq_psum, 4 * (j + 1))
            retire[W_MO + j] = (mo_psum, 2 * NC_ - 1 + j)
        for j in range(KD):
            retire[W_M + j] = (sb_psum, j + 1)
        for j in range(4):
            retire[W_KV + j] = (mkv_psum, 2 * (j + 1))

        conv_step = sem("conv_step")
        wr_loaded, hn_stored = sem("wr_loaded"), sem("hn_stored")
        lg_psum, route, route_exp, pos_psum, g_ready, g_psum = (
            sem(n) for n in ("lg_psum", "route", "route_exp", "pos_psum", "g_ready", "g_psum"))
        route_const, idx_ready, nf_loaded = sem("route_const"), sem("idx_ready"), sem("nf_loaded")
        mring_loaded = [sem(f"mring_loaded{i}") for i in range(NMRING)]
        xg_loaded = [sem(f"xg_loaded{i}") for i in range(NXG)]
        y_stored = [sem(f"y_stored{i}") for i in range(2)]
        (gt_psum, gt_ready, ge_psum, up_psum, sg_ready, he_ready, het_psum, het_ready, yd_psum, yo_ready) = (
            sem(n) for n in ("gt_psum", "gt_ready", "ge_psum", "up_psum", "sg_ready", "he_ready", "het_psum",
                             "het_ready", "yd_psum", "yo_ready"))
        fin_loaded = [sem(f"fin_loaded{i}") for i in range(2)]
        y1_sum, x3_ready, fin_ready = (sem(n) for n in ("y1_sum", "x3_ready", "fin_ready"))
        KV_STORES = 4
        MIX_STORES = 8
        stored = [0]

        U_ = 10
        OFF = [0, 512, 1024, 896]

        def keycols(u, kc):
            if u < SBH:
                return OFF[kc], LP - kc * P
            return kc * 256, 256

        def out_dma(eng, dst, src, done=out_stored):
            eng.dma_start(dst, src).then_inc(done, 16)
            if done is out_stored:
                stored[0] += 1

        def norm_stat(i, src, n, scratch):
            sl = slice(i, i + 1)
            nc.scalar.activation(scratch[:n, :], src, ACT.Square, accum_out=SS[:n, sl]).then_inc(ss_ready, 1)
            nc.scalar.wait_ge(ss_ready, i + 1)
            nc.scalar.activation(RL[:n, sl], SS[:n, sl], ACT.Ln, scale=1.0 / D, bias=CST[:n, 0:1]).then_inc(rl_ready, 1)
            nc.scalar.wait_ge(rl_ready, i + 1)
            nc.scalar.activation(RI[:n, sl], RL[:n, sl], ACT.Exp, scale=-0.5).then_inc(ri_ready, 1)

        def norm_scale(dve, i, src, n, dst, reused):
            dve.wait_ge(ri_ready, i + 1)
            if reused:
                dve.wait_ge(tp_psum, i - 1)
            nc.vector.tensor_scalar(dst, src, RI[:n, i:i + 1], None, ALU.mult).then_inc(xn_ready, 1)

        def norm_banks(i, b0):
            return bank(b0 + 2 * (i % 2), 2).rearrange("p (c n) -> p c n", c=KD)

        def norm_turn(pe, i, src, n, b0):
            pe.wait_ge(xn_ready, i + 1)
            if i >= 2:
                pe.wait_ge(ht_ready, i - 1)
            for c in range(KD):
                last = nc.tensor.transpose(norm_banks(i, b0)[:, c, 0:n], src[:, c * P:(c + 1) * P], IDENT[:n, :n])
            last.then_inc(tp_psum, 1)

        def norm_gain(dve, i, gain, n, b0, dst):
            dve.wait_ge(tp_psum, i + 1)
            nc.vector.tensor_tensor(dst, norm_banks(i, b0)[:, :, 0:n], bc(gain.unsqueeze(2), [P, KD, n]),
                                    ALU.mult).then_inc(ht_ready, 1)

        srcA = [(X[:n, m, :], n) for m, (_, n) in enumerate(CH)] + [(MR[:, m, :], P) for m in range(2)]
        dstA = [HT[:, :, t0:t0 + n] for t0, n in CH] + [MT[:, :, m * P:(m + 1) * P] for m in range(2)]

        def rstep(dve, n, ins):
            ins.then_inc(route, 1)
            dve.wait_ge(route, n)

        def route_dve(dve):
            k = [0]

            def go(ins):
                k[0] += 1
                rstep(dve, k[0], ins)

            v = nc.vector
            b3 = lambda a: bc(a.unsqueeze(2), [P, NC_, 4])
            g4 = lambda a: a.rearrange("p c (g k) -> p c g k", g=4)
            dve.wait_ge(hn_stored, 16 * NC_)
            dve.wait_ge(tp_psum, N_I + NC_)
            go(v.memset(LG, 0.0))
            dve.wait_ge(lg_psum, 1)
            go(v.tensor_copy(LG[:, 0:4, :], bank(0)[:, 0:128].rearrange("p (c n) -> p c n", c=4)[:, :, 0:20]))
            go(v.tensor_copy(LG[:LS, 4, :], bank(0)[:LS, 128:148]))
            lgg = LG[:, :, 0:4]
            dve.wait_ge(route_const, 4)
            go(v.tensor_reduce(MX, lgg, AX.X, ALU.max))
            go(v.tensor_tensor(E4, lgg, b3(MX), ALU.subtract))
            assert k[0] == 5
            go(v.tensor_tensor(EQ, lgg, b3(MX), ALU.is_equal))

            def first_largest(eq, oh):
                go(v.tensor_tensor(eq, eq, bc(W4.unsqueeze(1), [P, NC_, 4]), ALU.mult))
                go(v.tensor_reduce(RF, eq, AX.X, ALU.max))
                go(v.tensor_tensor(oh, eq, b3(RF), ALU.is_equal))

            first_largest(EQ, OHG)
            le = LG[:, :, 4:20]
            for g in range(4):
                if g == 0:
                    go(v.tensor_tensor(LSEL, le[:, :, 0:4], bc(OHG[:, :, 0:1], [P, NC_, 4]), ALU.mult))
                else:
                    go(v.tensor_tensor(OH2, le[:, :, 4 * g:4 * g + 4], bc(OHG[:, :, g:g + 1], [P, NC_, 4]), ALU.mult))
                    go(v.tensor_tensor(LSEL, LSEL, OH2, ALU.add))
            go(v.tensor_reduce(MA, LSEL, AX.X, ALU.max))
            go(v.tensor_tensor(EQ, LSEL, b3(MA), ALU.is_equal))
            first_largest(EQ, OH1)
            go(v.scalar_tensor_tensor(out=L2, in0=OH1, scalar=-BIG, in1=LSEL, op0=ALU.mult, op1=ALU.add))
            go(v.tensor_reduce(MB, L2, AX.X, ALU.max))
            go(v.tensor_tensor(EQ, L2, b3(MB), ALU.is_equal))
            first_largest(EQ, OH2)
            go(v.tensor_tensor(EX, MB, MA, ALU.subtract))
            route_steps["diff"] = k[0]
            for s_, oh in ((S1, OH1), (S2, OH2)):
                for g in range(4):
                    go(v.tensor_tensor(s_[:, :, 4 * g:4 * g + 4], oh, bc(OHG[:, :, g:g + 1], [P, NC_, 4]), ALU.mult))
                go(v.memset(s_[LS:, 4, :], 0.0))
            go(v.tensor_tensor(MK, S1, S2, ALU.add))
            route_steps["mask"] = k[0]
            dve.wait_ge(route_exp, 2)
            go(v.tensor_reduce(SM, E4, AX.X, ALU.add))
            go(v.reciprocal(PSEL, SM))
            go(v.tensor_scalar(DEN, EX, 1.0, None, ALU.add))
            go(v.reciprocal(GA, DEN))
            go(v.tensor_tensor(GA, GA, PSEL, ALU.mult))
            go(v.tensor_tensor(GB_, GA, EX, ALU.mult))
            b16 = lambda a: bc(a.unsqueeze(2), [P, NC_, NE])
            go(v.tensor_tensor(DW, S1, b16(GA), ALU.mult))
            go(v.tensor_tensor(TMP, S2, b16(GB_), ALU.mult))
            go(v.tensor_tensor(TW[:, :, :, 1], DW, TMP, ALU.add))
            dve.wait_ge(pos_psum, 1)
            go(v.tensor_copy(POSP, bank(1)[:, 0:80].rearrange("p (c e) -> p c e", c=NC_)))
            go(v.tensor_copy(CNT, bank(1)[:, 80:96]))
            go(v.scalar_tensor_tensor(out=POSM, in0=POSP, scalar=1.0, in1=MK, op0=ALU.add, op1=ALU.mult))
            go(v.tensor_scalar(POSM, POSM, -1.0, None, ALU.add))
            route_steps["pos"] = k[0]
            for e in range(NE):
                if e >= 2:
                    dve.wait_ge(g_psum, e - 1)
                nc.vector.tensor_tensor(GM[e % 2], bc(IOTA.unsqueeze(1), [P, NC_, P]),
                                        bc(POSM[:, :, e:e + 1], [P, NC_, P]), ALU.is_equal).then_inc(g_ready, 1)
            go(v.tensor_scalar(TMP2, POSP, float(P), None, ALU.is_ge))
            for j in range(2, NC_):
                go(v.scalar_tensor_tensor(out=TMP2, in0=POSP, scalar=float(P * j), in1=TMP2, op0=ALU.is_ge, op1=ALU.add))
            go(v.scalar_tensor_tensor(out=POSP, in0=TMP2, scalar=float((NE - 1) * P), in1=POSP, op0=ALU.mult, op1=ALU.add))
            go(v.tensor_tensor(POSP, POSP, bc(ECAP.unsqueeze(1), [P, NC_, NE]), ALU.add))
            for s_, r, i in ((S1, R1F, 0), (S2, R2F, 1)):
                go(v.tensor_tensor(TMP, POSP, s_, ALU.mult))
                go(v.tensor_reduce(r, TMP, AX.X, ALU.add))
                go(v.tensor_copy(R12[:, i, :].bitcast(U32), r))
            go(v.tensor_reduce(FLAG[:, 0:1], CNT, AX.X, ALU.max))
            dve.wait_ge(g_psum, NE)
            go(v.tensor_copy(SLOT, bank(2)[:, 0:2 * NE].rearrange("p (e n) -> p e n", e=NE)))
            v.tensor_copy(FLAG[:, 1:2].bitcast(U32), FLAG[:, 0:1]).then_inc(idx_ready, 1)
            v.tensor_copy(IDX.bitcast(U32), SLOT[:, :, 0]).then_inc(idx_ready, 1)

        route_steps = {}

        def route_pe(pe):
            pe.wait_ge(wr_loaded, 32)
            pe.wait_ge(ht_ready, N_I + NC_)
            pe.wait_ge(x2_ready, 2 * NC_)
            for m, (t0, n) in enumerate(CH):
                for k in range(KD):
                    last = nc.tensor.matmul(bank(0)[:n, 32 * m:32 * m + 20], HT[:, k, t0:t0 + n], WR[:, k, :],
                                            start=(k == 0), stop=(k == KD - 1))
            last.then_inc(lg_psum, 1)
            pe.wait_ge(route, route_steps["mask"])
            for c in range(NC_ + 1):
                for c2 in range(min(c + 1, NC_)):
                    last = nc.tensor.matmul(bank(1)[:, 16 * c:16 * c + 16], TSTR if c2 == c else ONES, MK[:, c2, :],
                                            start=(c2 == 0), stop=(c2 == min(c, NC_ - 1)))
            last.then_inc(pos_psum, 1)
            for e in range(NE):
                pe.wait_ge(g_ready, e + 1)
                for c in range(NC_):
                    last = nc.tensor.matmul(bank(2)[:, 2 * e:2 * e + 2], GM[e % 2][:, c, :], TW[:, c, e, :],
                                            start=(c == 0), stop=(c == NC_ - 1))
                last.then_inc(g_psum, 1)
            pe.wait_ge(idx_ready, 2)

        MT_SRC = []
        for e in range(NE):
            MT_SRC += [I["w_gate_e"][0, e].rearrange("(k p) f -> p k f", p=P),
                       I["w_up_e"][0, e].rearrange("(k p) f -> p k f", p=P),
                       I["w_down_e"][0, e].rearrange("(k p) f -> p k f", p=P)]

        def mview(q):
            return MSLOT[q % NMRING].rearrange("p (k f) -> p k f", f=FF if q % 3 < 2 else D)

        def experts_sp(sp):
            for q in range(3 * NE):
                if q < NRING:
                    sp.wait_ge(*((mo_psum, 9), (mo_psum, 10), (mq_psum, 8))[q])
                elif q < NMRING:
                    sp.wait_ge(hn_stored, 16 * NC_)
                    sp.wait_ge(ht_ready, N_I + NC_)
                else:
                    e, j = divmod(q - NMRING, 3)
                    sp.wait_ge((ge_psum, up_psum, yd_psum)[j], e + 1)
                sp.dma_start(mview(q), MT_SRC[q]).then_inc(mring_loaded[q % NMRING], 16)
                if q == 8:
                    sp.wait_ge(idx_ready, 1)
                    sp.dma_start(NF, I["norm_final"].rearrange("(a d) -> a d", a=1).to_broadcast([P, D])).then_inc(nf_loaded, 16)

        def expert_weights(pe, q):
            pe.wait_ge(mring_loaded[q % NMRING], 16 * (q // NMRING + 1))

        def turn_tokens(src):
            for c in range(KD):
                last = nc.tensor.transpose(bank(0, 2)[:, c * P:(c + 1) * P], src[:, c * P:(c + 1) * P], IDENT)
            return last

        def expert_rows(b, gt, w):
            for k in range(KD):
                last = nc.tensor.matmul(bank(b), gt[:, k, :], w[:, k, :], start=(k == 0), stop=(k == KD - 1))
            return last

        def turn_hidden(he):
            for c in range(4):
                last = nc.tensor.transpose(bank(4)[:, c * P:(c + 1) * P], he[:, c * P:(c + 1) * P], IDENT)
            return last

        def expert_down(het, w):
            for h in range(2):
                for c in range(4):
                    last = nc.tensor.matmul(bank(5 + h), het[:, c, :], w[:, c, 512 * h:512 * (h + 1)],
                                            start=(c == 0), stop=(c == 3))
            return last

        def experts_pe(pe):
            def turn(e):
                pe.wait_ge(xg_loaded[e % NXG], 16 * (e // NXG + 1))
                if e:
                    pe.wait_ge(gt_ready, e)
                turn_tokens(XG[e % NXG]).then_inc(gt_psum, 1)

            turn(0)
            for e in range(NE):
                pe.wait_ge(gt_ready, e + 1)
                expert_weights(pe, 3 * e)
                if e:
                    pe.wait_ge(sg_ready, e)
                expert_rows(2, GT[e % 2], mview(3 * e)).then_inc(ge_psum, 1)
                expert_weights(pe, 3 * e + 1)
                if e:
                    pe.wait_ge(he_ready, e)
                expert_rows(3, GT[e % 2], mview(3 * e + 1)).then_inc(up_psum, 1)
                if e + 1 < NE:
                    turn(e + 1)
                pe.wait_ge(he_ready, e + 1)
                if e:
                    pe.wait_ge(het_ready, e)
                turn_hidden(HE[e % 2]).then_inc(het_psum, 1)
                pe.wait_ge(het_ready, e + 1)
                expert_weights(pe, 3 * e + 2)
                if e:
                    pe.wait_ge(yo_ready, e)
                expert_down(HET[e % 2], mview(3 * e + 2)).then_inc(yd_psum, 1)

        def experts_act(act):
            for e in range(NE):
                act.wait_ge(ge_psum, e + 1)
                if e >= 2:
                    act.wait_ge(he_ready, e - 1)
                nc.scalar.activation(SG[e % 2], bank(2), ACT.Silu).then_inc(sg_ready, 1)
                act.wait_ge(yd_psum, e + 1)
                if e >= 2:
                    act.wait_ge(y_stored[e % 2], 16 * (e // 2))
                nc.scalar.activation(YO[e % 2], bank(5, 2), ACT.Copy, scale=SLOT[:, e, 1:2]).then_inc(yo_ready, 1)
                act.wait_ge(yo_ready, e + 1)
                act.dma_start(y_rows[e * P:(e + 1) * P, :], YO[e % 2]).then_inc(y_stored[e % 2], 16)

        def experts_dve(dve):
            for e in range(NE):
                if e == 0:
                    dve.wait_ge(gt_psum, 1)
                    gain_tokens(GT[0]).then_inc(gt_ready, 1)
                dve.wait_ge(sg_ready, e + 1)
                dve.wait_ge(up_psum, e + 1)
                if e >= 2:
                    dve.wait_ge(het_psum, e - 1)
                nc.vector.tensor_tensor(HE[e % 2], bank(3), SG[e % 2], ALU.mult).then_inc(he_ready, 1)
                if e + 1 < NE:
                    dve.wait_ge(gt_psum, e + 2)
                    if e >= 1:
                        dve.wait_ge(up_psum, e)
                    gain_tokens(GT[(e + 1) % 2]).then_inc(gt_ready, 1)
                dve.wait_ge(het_psum, e + 1)
                if e >= 2:
                    dve.wait_ge(yd_psum, e - 1)
                nc.vector.tensor_copy(HET[e % 2], bank(4).rearrange("p (c n) -> p c n", c=4)).then_inc(het_ready, 1)

        def gain_tokens(dst):
            return nc.vector.tensor_tensor(dst, bank(0, 2).rearrange("p (c n) -> p c n", c=KD),
                                           bc(G_FFN.unsqueeze(2), [P, KD, P]), ALU.mult)

        def experts_pool(pool):
            for e in range(NE):
                if e >= NXG:
                    pool.wait_ge(gt_psum, e - NXG + 1)
                pool.indirect_dma_start(XG[e % NXG], None, hn_rows,
                                        bass.IndirectOffsetOnAxis(ap=IDX.bitcast(U32)[:, e:e + 1], axis=0)
                                        ).then_inc(xg_loaded[e % NXG], 16)

        def overflow(eng, body):
            count = eng.value_load(FLAG[0:1, 1:2].bitcast(U32), min_val=0, max_val=T)
            with eng.If(count > P):
                with eng.Fori(0, NE) as e:
                    for j in range(1, NC_):
                        body(e, j)
                        eng.wait_ge(y_stored[0], 16 * (NE // 2) + nth(e, j, 16))

        def nth(e, j, k=1):
            return e * (k * (NC_ - 1)) + k * j

        def overflow_sp(e):
            nc.sync.wait_ge(y_stored[0], 16 * (NE // 2) + nth(e, 0, 16))
            for i, name in enumerate(("w_gate_e", "w_up_e", "w_down_e")):
                nc.sync.dma_start(mview(i), I[name][0, bass.ds(e, 1)].rearrange("a (k p) f -> p (a k) f", p=P)
                                  ).then_inc(mring_loaded[0], 16)

        def overflow_pool(e, j):
            nc.gpsimd.wait_ge(idx_ready, 2 + nth(e, j, 2))
            nc.gpsimd.indirect_dma_start(XG[0], None, hn_rows, bass.IndirectOffsetOnAxis(ap=IDXO.bitcast(U32), axis=0)
                                         ).then_inc(xg_loaded[0], 16)

        def overflow_pe(e, j):
            pe = nc.tensor
            pe.wait_ge(g_ready, NE + nth(e, j, 3))
            for c in range(NC_):
                last = pe.matmul(bank(7)[:, 0:2], GM[0][:, c, :], TWO[:, c, :], start=(c == 0), stop=(c == NC_ - 1))
            last.then_inc(g_psum, 1)
            pe.wait_ge(xg_loaded[0], 16 * (NE // NXG) + nth(e, j, 16))
            turn_tokens(XG[0]).then_inc(gt_psum, 1)
            pe.wait_ge(gt_ready, NE + nth(e, j))
            pe.wait_ge(mring_loaded[0], 16 * (3 * NE // NMRING) + e * 48 + 48)
            expert_rows(2, GT[0], mview(0)).then_inc(ge_psum, 1)
            expert_rows(3, GT[0], mview(1)).then_inc(up_psum, 1)
            pe.wait_ge(he_ready, NE + nth(e, j))
            turn_hidden(HE[0]).then_inc(het_psum, 1)
            pe.wait_ge(het_ready, NE + nth(e, j))
            expert_down(HET[0], mview(2)).then_inc(yd_psum, 1)

        def overflow_dve(e, j):
            dve = nc.vector
            dve.tensor_scalar(PC.unsqueeze(2), POSM[:, :, bass.ds(e, 1)], -float(P * j), None, ALU.add).then_inc(g_ready, 1)
            dve.tensor_copy(TWO.unsqueeze(2), TW[:, :, bass.ds(e, 1), :]).then_inc(g_ready, 1)
            dve.wait_ge(g_ready, NE + nth(e, j, 3) - 1)
            dve.tensor_tensor(GM[0], bc(IOTA.unsqueeze(1), [P, NC_, P]), bc(PC.unsqueeze(2), [P, NC_, P]),
                              ALU.is_equal).then_inc(g_ready, 1)
            dve.wait_ge(g_psum, NE + nth(e, j))
            dve.tensor_copy(SLOTO, bank(7)[:, 0:2]).then_inc(idx_ready, 1)
            dve.wait_ge(idx_ready, 1 + nth(e, j, 2))
            dve.tensor_copy(IDXO.bitcast(U32), SLOTO[:, 0:1]).then_inc(idx_ready, 1)
            dve.wait_ge(gt_psum, NE + nth(e, j))
            gain_tokens(GT[0]).then_inc(gt_ready, 1)
            dve.wait_ge(sg_ready, NE + nth(e, j))
            dve.wait_ge(up_psum, NE + nth(e, j))
            dve.tensor_tensor(HE[0], bank(3), SG[0], ALU.mult).then_inc(he_ready, 1)
            dve.wait_ge(het_psum, NE + nth(e, j))
            dve.tensor_copy(HET[0], bank(4).rearrange("p (c n) -> p c n", c=4)).then_inc(het_ready, 1)

        def overflow_act(e, j):
            act = nc.scalar
            act.wait_ge(ge_psum, NE + nth(e, j))
            act.activation(SG[0], bank(2), ACT.Silu).then_inc(sg_ready, 1)
            act.wait_ge(yd_psum, NE + nth(e, j))
            act.wait_ge(idx_ready, 1 + nth(e, j, 2))
            act.activation(YO[0], bank(5, 2), ACT.Copy, scale=SLOTO[:, 1:2]).then_inc(yo_ready, 1)
            act.wait_ge(yo_ready, NE + nth(e, j))
            act.dma_start(y_rows[bass.ds(e * P + NE * P * j, P), :], YO[0]).then_inc(y_stored[0], 16)

        def moe_sp(sp):
            experts_sp(sp)
            sp.wait_ge(yd_psum, NE)
            count = sp.value_load(FLAG[0:1, 1:2].bitcast(U32), min_val=0, max_val=T)
            with sp.If(count > P):
                with sp.Fori(0, NE) as e:
                    overflow_sp(e)

        def moe_pool(pool):
            for m, (t0, n) in enumerate(CH):
                pool.wait_ge(xn_ready, N_I + m + 1)
                pool.dma_start(hn_rows[t0:t0 + n, :], XNR[:n, m, :]).then_inc(hn_stored, 16)
            pool.wait_ge(hn_stored, 16 * NC_)
            pool.wait_ge(tp_psum, N_I + NC_)
            pool.iota(IOTA, [[1, P]], base=0, channel_multiplier=0, allow_small_or_imprecise_dtypes=True).then_inc(route_const, 1)
            pool.iota(ECAP, [[P, NE]], base=0, channel_multiplier=0, allow_small_or_imprecise_dtypes=True).then_inc(route_const, 1)
            for i in range(4):
                last = pool.memset(W4[:, i:i + 1], float(8 >> i))
            last.then_inc(route_const, 1)
            for c in range(NC_):
                last = pool.iota(TW[:, c, :, 0], [[0, NE]], base=c * P, channel_multiplier=1, allow_small_or_imprecise_dtypes=True)
            last.then_inc(route_const, 1)
            pool.wait_ge(idx_ready, 2)
            experts_pool(pool)
            pool.wait_ge(gt_psum, NE)
            count = pool.value_load(FLAG[0:1, 1:2].bitcast(U32), min_val=0, max_val=T)
            with pool.If(count > P):
                for e in range(NE):
                    for j in range(1, NC_):
                        overflow_pool(e, j)
                        pool.wait_ge(y_stored[0], 16 * (NE // 2) + nth(e, j, 16))
            for i in range(2):
                pool.wait_ge(y_stored[i], 16 * (NE // 2))
            with pool.If(count > P):
                gather_results(pool, y_rows)
            with pool.If(count <= P):
                gather_results(pool, y_rows[0:NE * P, :])
            for m, (t0, n) in enumerate(CH):
                pool.wait_ge(fin_ready, m + 1)
                dst = O["y_prompt"][0, t0:t0 + n, :] if m < 4 else O["y_sample"][0]
                out_dma(pool, dst, X[:n, m, :], late_stored)

        def gather_results(pool, rows):
            for m, (t0, n) in enumerate(CH):
                if m >= 2:
                    pool.wait_ge(x3_ready, m - 1)
                for i in range(2):
                    pool.indirect_dma_start(XG[2 * (m % 2) + i][:n, :], None, rows,
                                            bass.IndirectOffsetOnAxis(ap=R12.bitcast(U32)[:n, i, m:m + 1], axis=0)
                                            ).then_inc(fin_loaded[m % 2], 16)

        def moe_act(act):
            act.wait_ge(route, 5)
            nc.scalar.activation(E4, E4, ACT.Exp).then_inc(route_exp, 1)
            act.wait_ge(route, route_diff)
            nc.scalar.activation(EX, EX, ACT.Exp).then_inc(route_exp, 1)
            act.wait_ge(idx_ready, 2)
            experts_act(act)
            act.wait_ge(y_stored[0], 16 * (NE // 2))
            overflow(act, overflow_act)
            for m, (_, n) in enumerate(CH):
                act.wait_ge(x3_ready, m + 1)
                norm_stat(N_F + m, X[:n, m, :], n, SQ2)

        def moe_dve(dve):
            route_dve(dve)
            dve.wait_ge(idx_ready, 2)
            experts_dve(dve)
            overflow(dve, overflow_dve)
            dve.wait_ge(nf_loaded, 16)

            def finish(m):
                n = CH[m][1]
                dve.wait_ge(ri_ready, N_F + m + 1)
                nc.vector.scalar_tensor_tensor(out=X[:n, m, :], in0=X[:n, m, :], scalar=RI[:n, 17 + m:18 + m], in1=NF[:n, :],
                                               op0=ALU.mult, op1=ALU.mult).then_inc(fin_ready, 1)

            for m, (_, n) in enumerate(CH):
                dve.wait_ge(fin_loaded[m % 2], 32 * (m // 2 + 1))
                nc.vector.tensor_tensor(X[:n, m, :], X[:n, m, :], XG[2 * (m % 2)][:n, :], ALU.add).then_inc(y1_sum, 1)
                dve.wait_ge(y1_sum, m + 1)
                nc.vector.tensor_tensor(X[:n, m, :], X[:n, m, :], XG[2 * (m % 2) + 1][:n, :], ALU.add).then_inc(x3_ready, 1)
                if m:
                    finish(m - 1)
            finish(NC_ - 1)

        def moe_pe(pe):
            route_pe(pe)
            experts_pe(pe)
            overflow(pe, overflow_pe)

        route_diff = 28
        SQ2 = GT[0].rearrange("p c n -> p (c n)")
        block = ctx.enter_context(nc.Block())

        @block.sync
        def _(sp):
            xr = I["x_prompt"][0].rearrange("(m p) d -> p m d", p=P)
            for m in range(4):
                sp.dma_start(X[:, m, :], xr[:, m, :]).then_inc(x_loaded[m], 16)
            sp.dma_start(X[:LS, 4, :], I["x_sample"][0]).then_inc(x_loaded[4], 16)

            def load(n):
                if n >= NRING:
                    sp.wait_ge(*retire[n - NRING])
                for view, src in loads[n]:
                    sp.dma_start(view(n % NRING), src).then_inc(ring_loaded[n % NRING], 16)

            load(0)
            for m in range(2):
                sp.dma_start(MR[:, m, :], I["mem_prompt"][0, m * P:(m + 1) * P, :]).then_inc(mem_loaded[m], 16)
            load(1)
            load(2)
            sp.dma_start(PVR, I["cache_sb_v"][0, 0].rearrange("(c p) h d -> p c (h d)", p=P)).then_inc(past_loaded, 16)
            sp.wait_ge(xn_ready, 7)
            sp.dma_start(PKR, I["cache_sb_k"][0, 0].rearrange("(c p) h d -> p c (h d)", p=P)).then_inc(past_loaded, 16)
            for n in (3, 4, 5):
                load(n)
            sp.wait_ge(ysb_ready, 5)
            sp.wait_ge(out_stored, 16 * KV_STORES)
            sp.dma_start(WDT, w_in[:, :, C_DT:C_DT + NH]).then_inc(cols_loaded, 16)
            sp.dma_start(H0R, I["state_ssm"][0, 0].rearrange("h q n -> (h q) n").rearrange("(b p) n -> p b n", p=P)
                         ).then_inc(state_loaded, 16)
            for n in range(6, W_O):
                load(n)
            for n in range(W_O, len(loads)):
                if n == W_KV:
                    sp.wait_ge(mg_ready, KD)
                    sp.wait_ge(wo_psum, 2 * NC_)
                    sp.dma_start(MC[:, 0], I["cache_mem_k"][0, 0].rearrange("(m p) h d -> p m (h d)", p=P)).then_inc(memc_loaded, 16)
                    sp.dma_start(MC[:, 1], I["cache_mem_v"][0, 0].rearrange("(m p) h d -> p m (h d)", p=P)).then_inc(memc_loaded, 16)
                load(n)
            moe_sp(sp)
            sp.wait_ge(out_stored, 16 * MIX_STORES)
            sp.wait_ge(late_stored, 16 * (4 + NC_))

        @block.gpsimd
        def _(pool):
            rows = [("norm_mix", 0), ("norm_mem_kv", 8), ("ssm_norm", 16), ("norm_mem_q", 24), ("norm_ffn", 32),
                    ("conv_b", 40)]
            for name, r in rows:
                v = I[name][0].rearrange("(r p) -> r p", p=P)
                pool.dma_start(VEC[r:r + v.shape[0], :], v).then_inc(vec_loaded, 16)
            pool.dma_start(VEC[52:100, :], I["conv_w"][0].rearrange("j (c p) -> (j c) p", p=P)).then_inc(vec_loaded, 16)
            pool.dma_start(CTXR[0:36, :], I["state_conv"][0, 0].rearrange("j (c p) -> (j c) p", p=P)).then_inc(vec_loaded, 16)
            for i, name in enumerate(("dt_bias", "a_log", "d_skip")):
                pool.dma_start(HCOL[0:NH, i:i + 1], I[name].rearrange("a h -> h a")).then_inc(vec_loaded, 16)
            pool.dma_start(WR[:, :, 0:4], I["w_group_router"][0].rearrange("(k p) n -> p k n", p=P)).then_inc(wr_loaded, 16)
            pool.dma_start(WR[:, :, 4:20], I["w_expert_router"][0].rearrange("(k p) n -> p k n", p=P)).then_inc(wr_loaded, 16)
            for m in (IDENT, ):
                nc.gpsimd.memset(m, 0.0).then_inc(const0, 1)
            for m in (TSUF, TINC, TSTR):
                nc.gpsimd.memset(m, 1.0).then_inc(const0, 1)
            nc.gpsimd.memset(ONES, 1.0).then_inc(consts, 1)
            nc.gpsimd.memset(CST, EPS).then_inc(consts, 1)
            pool.wait_ge(const0, 4)
            for m, op, step, cm in ((IDENT, ALU.not_equal, -1, 1), (TSUF, ALU.is_ge, -1, 1),
                                    (TINC, ALU.is_ge, 1, -1), (TSTR, ALU.is_gt, 1, -1)):
                pool.affine_select(out=m, in_=m, compare_op=op, fill=1.0 if m is IDENT else 0.0, base=0,
                                   pattern=[[step, P]], channel_multiplier=cm).then_inc(consts, 1)
            for g, (name, rows_) in enumerate((("sb_k", KR), ("sb_v", VR))):
                pool.wait_ge(kv_rows, 5 * (g + 1))
                out_dma(pool, O[name + "_prompt"][0, 0].rearrange("(m p) h d -> p m (h d)", p=P), rows_[:, 0:4, :])
                out_dma(pool, O[name + "_sample"][0, 0].rearrange("p h d -> p (h d)"), rows_[:LS, 4, :])

            def mask(u, buf, done):
                if u < SBH:
                    for kc in range(4):
                        v = buf[:, OFF[kc]:OFF[kc] + P]
                        last = pool.affine_select(out=v, in_=v, compare_op=ALU.is_gt, fill=0.0, base=0,
                                                  pattern=[[1, P]], channel_multiplier=-1)
                else:
                    v = buf[:, 1024:1280].rearrange("p (h t) -> p h t", h=4)
                    last = pool.affine_select(out=v, in_=v, compare_op=ALU.is_gt, fill=0.0, base=0,
                                              pattern=[[0, 4], [1, LS]], channel_multiplier=-1)
                last.then_inc(done, 1)

            for u in range(U_ + 1):
                if u < U_:
                    pool.wait_ge(sp_raw, u + 1)
                    mask(u, LB[u % 2], sp_ready)
                if u >= 1:
                    pool.wait_ge(w_raw, u)
                    mask(u - 1, ZSB[(u - 1) % 3], w_ready)
            pool.wait_ge(ysb_ready, 5)
            pool.wait_ge(out_stored, 16 * KV_STORES)
            nc.gpsimd.memset(XC[:, :, T:TS], 0.0).then_inc(pads, 1)
            for s, name in ((0, "conv_prompt"), (1, "conv_sample")):
                pool.wait_ge(tail_rows, s + 1)
                out_dma(pool, O[name][0, 0].rearrange("j (c p) -> (j c) p", p=P), TAILR[0:36, s, :])
            pool.wait_ge(out_stored, 16 * stored[0])
            pool.wait_ge(dve_dt, 7)
            nc.gpsimd.memset(HS[:, 0], 0.0).then_inc(pads, 1)
            for v in range(10):
                c, g = divmod(v, 2)
                if v == 0:
                    pool.wait_ge(xc_ready, CONV_C)
                    pool.wait_ge(vec_ready, 3)
                if v >= 1:
                    pool.wait_ge(t3_done, v)
                nc.gpsimd.tensor_tensor(DX, XC[:, 4 * g:4 * g + 4, c * P:(c + 1) * P],
                                        bc(DP[:, 4 * g:4 * g + 4].unsqueeze(2), [P, 4, P]),
                                        ALU.mult).then_inc(dx_ready, 1)
            for s, name in ((0, "ssm_prompt"), (1, "ssm_sample")):
                pool.wait_ge(so_rows, s + 1)
                out_dma(pool, O[name][0, 0].rearrange("h q n -> (h q) n").rearrange("(b p) n -> p b n", p=P), HO)
            for t in range(4):
                pool.wait_ge(mkv_rows, 2 * (t + 1))
                name = ("mem_k_prompt", "mem_v_prompt")[t // 2]
                dst = O[name][0, 0].rearrange("(m p) h d -> p m (h d)", p=P)[:, :, 512 * (t % 2):512 * (t % 2) + 512]
                out_dma(pool, dst, MKV[:, :, 512 * t:512 * (t + 1)], late_stored)
            moe_pool(pool)

        def mem_out(act, h):
            for dc in range(2):
                act.wait_ge(ot_psum, 2 * h + dc + 1)
                nc.scalar.copy(OT[:, 2 * h + dc, :], bank(4 + 2 * dc, 2)[:, 0:T]).then_inc(ot_ready, 1)

        @block.scalar
        def _(act):
            act.wait_ge(consts, 6)
            for i, (src, n) in enumerate(srcA):
                act.wait_ge(x_loaded[i] if i < NC_ else mem_loaded[i - NC_], 16)
                norm_stat(i, src, n, SQ)
            for i in range(10):
                t, m = divmod(i, 5)
                n = CH[m][1]
                act.wait_ge(kv_psum, i + 1)
                nc.scalar.copy((KR, VR)[t][:n, m, :], bank(4 + i % 4)[:n, :]).then_inc(kv_rows, 1)
            for b in range(9):
                act.wait_ge(kt_psum, b + 1)
                nc.scalar.copy(KTA[:, :, b * P:(b + 1) * P],
                               bank(4 + b % 4).rearrange("p (h n) -> p h n", h=4)).then_inc(kt_ready, 1)
            for u in range(U_ + 1):
                if u < U_:
                    act.wait_ge(z_copied, u + 1)
                    if u >= 2:
                        act.wait_ge(s_psum, u - 1)
                    lb = LB[u % 2]
                    nc.scalar.activation(lb, ZSB[u % 3], ACT.Abs).then_inc(z_abs, 1)
                    act.wait_ge(z_abs, u + 1)
                    nc.scalar.activation(lb, lb, ACT.Exp, scale=-1.0).then_inc(z_exp, 1)
                    act.wait_ge(z_exp, u + 1)
                    nc.scalar.activation(lb, lb, ACT.Ln, bias=1.0).then_inc(l_ready, 1)
                if u >= 1:
                    act.wait_ge(u_ready, u)
                    nc.scalar.activation(ZSB[(u - 1) % 3], ZSB[(u - 1) % 3], ACT.Exp).then_inc(w_raw, 1)
            act.wait_ge(ysb_ready, 5)
            act.wait_ge(out_stored, 16 * KV_STORES)
            for i in range(CONV_C + 1):
                if i < CONV_C:
                    act.wait_ge(xb_psum, i + 1)
                    if i >= 3:
                        act.wait_ge(conv_done, i - 2)
                    b = bank(2 * (i % 2), 2)
                    nc.scalar.copy(XR[i % 3][:, 3:515], b[:, 0:512])
                    nc.scalar.copy(XR[i % 3][:, 518:582], b[:, 512:576]).then_inc(xr_ready, 1)
                if i >= 1:
                    j = i - 1
                    act.wait_ge(conv_done, j + 1)
                    nc.scalar.activation(XC[:, j, 0:LP], CV[j % 2][:, 0:512], ACT.Silu)
                    nc.scalar.activation(XC[:, j, LP:T], CV[j % 2][:, 515:579], ACT.Silu).then_inc(xc_ready, 1)
            for i in range(KD):
                act.wait_ge(zt_psum, i + 1)
                nc.scalar.activation(ZS[:, i, :], bank(2 * (i % 2), 2)[:, 0:T], ACT.Silu).then_inc(zt_ready, 1)
            act.wait_ge(dve_dt, 1)
            nc.scalar.activation(AD[0:NH, :], UD[0:NH, :], ACT.Abs).then_inc(act_dt, 1)
            act.wait_ge(act_dt, 1)
            nc.scalar.activation(AD[0:NH, :], AD[0:NH, :], ACT.Exp, scale=-1.0).then_inc(act_dt, 1)
            act.wait_ge(act_dt, 2)
            nc.scalar.activation(AD[0:NH, :], AD[0:NH, :], ACT.Ln, bias=1.0).then_inc(act_dt, 1)
            nc.scalar.activation(HCOL[0:NH, 3:4], HCOL[0:NH, 1:2], ACT.Exp).then_inc(act_dt, 1)
            act.wait_ge(dve_dt, 6)
            nc.scalar.activation(ECM[0:NH, :], CUM[0:NH, :], ACT.Exp).then_inc(act_dt, 1)
            act.wait_ge(pre_dve, 4)
            nc.scalar.activation(TE, TE, ACT.Exp).then_inc(pre_act, 1)
            act.wait_ge(pre_psum, 1)
            nc.scalar.activation(CD, bank(7)[:, 160:240].rearrange("p (c h) -> p c h", c=NC_), ACT.Exp).then_inc(pre_act, 1)
            for v in range(10):
                act.wait_ge(ec_psum, v + 1)
                if v >= 1:
                    act.wait_ge(t1_done, v)
                nc.scalar.copy(ECS, bank(5)).then_inc(ec_done, 1)
                act.wait_ge(seg_done, v + 1)
                nc.scalar.activation(SEG[v % 2], SEG[v % 2], ACT.Exp).then_inc(e_ready, 1)
            for i in range(KD):
                act.wait_ge(yz_done, 10)
                if i >= 2:
                    act.wait_ge(ssq_psum, i - 1)
                nc.scalar.activation(SQT[i % 2], ZS[:, i, :], ACT.Square).then_inc(sq_ready, 1)
            act.wait_ge(ssq_psum, KD)
            nc.scalar.activation(RB, bank(0, 2)[:, 0:T], ACT.Ln, scale=1.0 / D, bias=CST[:, 0:1]).then_inc(rb_ln, 1)
            act.wait_ge(rb_ln, 1)
            nc.scalar.activation(RB, RB, ACT.Exp, scale=-0.5).then_inc(rb_ready, 1)
            for c in range(KD):
                act.wait_ge(gs_psum, c + 1)
                if c >= 2:
                    act.wait_ge(m1_done, c - 1)
                nc.scalar.activation(GS[c % 2], bank(0, 2)[:, 0:T], ACT.Sigmoid).then_inc(gs_ready, 1)
                act.wait_ge(gb_psum, c + 1)
                if c >= 2:
                    act.wait_ge(m2_done, c - 1)
                nc.scalar.activation(GB[c % 2], bank(2, 2)[:, 0:T], ACT.Sigmoid).then_inc(gb_ready, 1)
            for m, (_, n) in enumerate(CH):
                act.wait_ge(x1_ready, 2 * (m + 1))
                norm_stat(N_G + m, X[:n, m, :], n, SQ)
            for i in range(8):
                t, m = divmod(i, 2)
                act.wait_ge(mkv_psum, i + 1)
                nc.scalar.copy(MKV[:, m, 512 * t:512 * (t + 1)], bank(i % 4)).then_inc(mkv_rows, 1)
            for i in range(KD):
                act.wait_ge(mq_psum, i + 1)
                nc.scalar.mul(QM[:, i, :], bank(2 * (i % 2), 2)[:, 0:T], MHD ** -0.5).then_inc(mq_ready, 1)
            for a in range(20):
                h, m = divmod(a, 5)
                n = CH[m][1]
                act.wait_ge(nm_ready, a + 1)
                if a >= 2:
                    act.wait_ge(pt_psum, a - 1)
                nc.scalar.activation(PX[a % 2][:n, :], bank(a % 2)[:n, 0:ML], ACT.Exp, bias=NM[:n, a:a + 1],
                                     accum_out=RS[:n, a:a + 1]).then_inc(px_ready, 1)
                if m == 1 and h >= 1:
                    mem_out(act, h - 1)
            mem_out(act, MH - 1)
            for m, (_, n) in enumerate(CH):
                act.wait_ge(x2_ready, 2 * (m + 1))
                norm_stat(N_I + m, X[:n, m, :], n, SQ)
            moe_act(act)

        @block.vector
        def _(dve):
            nc.vector.memset(KR[LS:, 4, :], 0.0)
            nc.vector.memset(VR[LS:, 4, :], 0.0)
            dve.wait_ge(vec_psum, 1)
            nc.vector.tensor_copy(VT, bank(7)[:, 0:100]).then_inc(vec_ready, 1)
            nc.vector.tensor_copy(CTXT, bank(7)[:, 128:164]).then_inc(vec_ready, 1)
            dve.wait_ge(vec_ready, 2)
            for i in range(len(srcA) + 1):
                if i < len(srcA):
                    src, n = srcA[i]
                    norm_scale(dve, i, src, n, XN[i % 2][:n, :], i >= 2)
                if i >= 1:
                    norm_gain(dve, i - 1, G_MIX if i - 1 < NC_ else G_MKV, srcA[i - 1][1], 0, dstA[i - 1])
            for i in range(4):
                dve.wait_ge(q_psum, i + 1)
                nc.vector.tensor_scalar(QT[:, i, :], bank(2 * (i % 2), 2)[:, 0:T], HD ** -0.5, None,
                                        ALU.mult).then_inc(q_ready, 1)

            def u_op(u):
                dve.wait_ge(s_psum, u + 1)
                nc.vector.tensor_tensor(ZSB[u % 3], ZSB[u % 3], ps[:, 1536:1536 + 1280], ALU.subtract).then_inc(u_ready, 1)

            def ysb_out(g):
                if g < 4:
                    dve.wait_ge(pv_psum, 2 * (g + 1))
                    nc.vector.tensor_copy(YSBT[:, g, 0:LP], bank(6 + g % 2)).then_inc(ysb_ready, 1)
                else:
                    dve.wait_ge(pv_psum, U_)
                    nc.vector.tensor_copy(YSBT[:, :, LP:T],
                                          bank(6 + g % 2)[:, 0:256].rearrange("p (h t) -> p h t", h=4)).then_inc(ysb_ready, 1)

            for u in range(U_ + 2):
                if u < U_:
                    dve.wait_ge(z_psum, u + 1)
                    if u >= 3:
                        dve.wait_ge(pv_psum, u - 2)
                    nc.vector.tensor_copy(ZSB[u % 3], ps[:, 0:1280]).then_inc(z_copied, 1)
                    dve.wait_ge(l_ready, u + 1)
                    dve.wait_ge(z_copied, u + 1)
                    nc.vector.scalar_tensor_tensor(out=LB[u % 2], in0=ZSB[u % 3], scalar=0.0, in1=LB[u % 2],
                                                   op0=ALU.max, op1=ALU.add).then_inc(sp_raw, 1)
                if 1 <= u <= U_:
                    u_op(u - 1)
                done = u - 2 + 1
                if u >= 2 and done % 2 == 0:
                    ysb_out(done // 2 - 1)

            dve.wait_ge(consts, 6)
            dve.wait_ge(out_stored, 16 * KV_STORES)
            for s in range(3):
                nc.vector.memset(XR[s][:, 0:3], 0.0)
            nc.vector.tensor_copy(SELP[0:NH], bc(IDENT[0:NH, 0:NH].unsqueeze(2), [NH, NH, HD])).then_inc(sel_ready, 1)
            for i in range(CONV_C):
                xr, cv = XR[i % 3], CV[i % 2]
                if i >= 2:
                    dve.wait_ge(xc_ready, i - 1)
                ctxv = CTXT.rearrange("p (j c) -> p j c", j=3)[:, :, i:i + 1]
                nc.vector.tensor_copy(xr[:, 515:518].unsqueeze(2), ctxv).then_inc(conv_step, 1)
                dve.wait_ge(xr_ready, i + 1)
                dve.wait_ge(conv_step, 4 * i + 1)
                nc.vector.tensor_copy(TAIL[:, 0, :, i:i + 1], xr[:, 512:515].unsqueeze(2))
                nc.vector.tensor_copy(TAIL[:, 1, :, i:i + 1], xr[:, 579:582].unsqueeze(2))
                nc.vector.tensor_scalar(cv[:, 0:579], xr[:, 0:579], CW[:, 0, i:i + 1], CB[:, i:i + 1],
                                        ALU.mult, ALU.add).then_inc(conv_step, 1)
                for j in range(1, 4):
                    dve.wait_ge(conv_step, 4 * i + 1 + j)
                    o = nc.vector.scalar_tensor_tensor(out=cv[:, 0:579], in0=xr[:, j:j + 579],
                                                       scalar=CW[:, j, i:i + 1], in1=cv[:, 0:579],
                                                       op0=ALU.mult, op1=ALU.add)
                    o.then_inc(conv_step if j < 3 else conv_done, 1)
            dve.wait_ge(dp_psum, 1)
            nc.vector.tensor_copy(DP, bank(7)[:, 240:248]).then_inc(vec_ready, 1)
            for s in range(2):
                dve.wait_ge(tail_psum, 2)
                nc.vector.tensor_copy(TAILR[0:36, s, :], bank(6)[0:36, P * s:P * (s + 1)]).then_inc(tail_rows, 1)
            dve.wait_ge(dt_psum, 1)
            nc.vector.tensor_scalar(UD[0:NH, :], bank(0, 2)[0:NH, 0:T], HCOL[0:NH, 0:1], None, ALU.add).then_inc(dve_dt, 1)
            nc.vector.memset(DTT[0:NH, T:TS], 0.0)
            nc.vector.memset(RST[0:NH, :], 1.0).then_inc(dve_dt, 1)
            dve.wait_ge(dve_dt, 2)
            nc.vector.memset(RST[0:NH, :].rearrange("p (c t) -> p c t", t=P)[:, :, 0:1], 0.0).then_inc(dve_dt, 1)
            dve.wait_ge(act_dt, 3)
            nc.vector.scalar_tensor_tensor(out=DTT[0:NH, 0:T], in0=UD[0:NH, :], scalar=0.0, in1=AD[0:NH, :],
                                           op0=ALU.max, op1=ALU.add).then_inc(dve_dt, 1)
            dve.wait_ge(act_dt, 4)
            dve.wait_ge(dve_dt, 4)
            nc.vector.tensor_scalar(DTA[0:NH, :], DTT[0:NH, :], HCOL[0:NH, 3:4], -1.0, ALU.mult, ALU.mult).then_inc(dve_dt, 1)
            dve.wait_ge(dve_dt, 5)
            nc.vector.tensor_tensor_scan(CUM[0:NH, :], RST[0:NH, :], DTA[0:NH, :], 0.0, ALU.mult, ALU.add).then_inc(dve_dt, 1)
            dve.wait_ge(dve_dt, 6)
            last_cum = CUM[0:NH, :].rearrange("p (c t) -> p c t", t=P)[:, :, P - 1:P]
            nc.vector.tensor_tensor(DIAG[0:NH], bc(IDENT[0:NH, 0:NH].unsqueeze(1), [NH, NC_, NH]),
                                    bc(last_cum, [NH, NC_, NH]), ALU.mult).then_inc(dve_dt, 1)
            dve.wait_ge(pre_psum, 1)
            p7 = lambda a: bank(7)[:, a:a + 80].rearrange("p (c h) -> p c h", c=NC_)
            nc.vector.tensor_copy(CR, p7(0)).then_inc(pre_dve, 1)
            nc.vector.tensor_copy(DR, p7(80)).then_inc(pre_dve, 1)
            dve.wait_ge(h0_psum, 1)
            dve.wait_ge(pads, 2)
            nc.vector.tensor_copy(HS[:, 1], bank(1, 2).rearrange("p (g n) -> p g n", g=2)).then_inc(pre_dve, 1)
            dve.wait_ge(pre_dve, 3)
            nc.vector.tensor_tensor(TE, p7(160), CR, ALU.subtract).then_inc(pre_dve, 1)
            dve.wait_ge(pre_act, 2)
            nc.vector.tensor_tensor(WRW, DR, TE, ALU.mult).then_inc(pre_dve, 1)
            dve.wait_ge(pre_dve, 5)

            def xdt(v):
                c, g = divmod(v, 2)
                dve.wait_ge(ssd_tr, v + 1)
                if v >= 2:
                    dve.wait_ge(st_psum, v - 1)
                    dve.wait_ge(intra_psum, v - 1)
                nc.vector.tensor_copy(BROW[v % 2], bank(0)[:, 0:P])
                nc.vector.tensor_tensor(CBM[v % 2], bank(0)[:, P:2 * P], TINC, ALU.mult)
                xr = bank(7).rearrange("p (h q) -> p h q", h=8)
                for dst, w in ((XD, DR), (XW, WRW)):
                    last = nc.vector.tensor_tensor(dst[v % 2].rearrange("p (h q) -> p h q", h=8), xr,
                                                   bc(w[:, c, 8 * g:8 * g + 8].unsqueeze(2), [P, 8, HD]), ALU.mult)
                last.then_inc(sx_done, 1)

            def seg(v):
                c, g = divmod(v, 2)
                dve.wait_ge(cumb_psum, v + 1)
                if v >= 2:
                    dve.wait_ge(intra_psum, v - 1)
                b = bank(1, 2).rearrange("p (h t) -> p h t", h=8)
                for h in range(8):
                    last = nc.vector.tensor_scalar(SEG[v % 2][:, h, :], b[:, h, :], CR[:, c, 8 * g + h:8 * g + h + 1],
                                                   0.0, ALU.subtract, ALU.min)
                last.then_inc(seg_done, 1)

            for v in range(10):
                c, g = divmod(v, 2)
                sq = 0 if c < 4 else 1
                if v == 0:
                    xdt(0)
                    seg(0)
                dve.wait_ge(e_ready, v + 1)
                dve.wait_ge(sx_done, v + 1)
                nc.vector.tensor_tensor(SEG[v % 2], SEG[v % 2], bc(CBM[v % 2].unsqueeze(1), [P, 8, P]),
                                        ALU.mult).then_inc(m_ready, 1)
                dve.wait_ge(inter_psum, v + 1)
                dve.wait_ge(ec_done, v + 1)
                if v >= 2:
                    dve.wait_ge(yz_done, v - 1)
                nc.vector.tensor_tensor(T1[v % 2].rearrange("p j t -> p (j t)"), bank(4), ECS,
                                        ALU.mult).then_inc(t1_done, 1)
                hs = HS[:, sq, g, :].rearrange("p (h q) -> p h q", h=8)
                nc.vector.tensor_tensor(hs, hs, bc(CD[:, c, 8 * g:8 * g + 8].unsqueeze(2), [P, 8, HD]),
                                        ALU.mult).then_inc(h_dec, 1)
                dve.wait_ge(st_psum, v + 1)
                dve.wait_ge(h_dec, v + 1)
                nc.vector.tensor_tensor(HS[:, sq, g, :], HS[:, sq, g, :], bank(6), ALU.add).then_inc(h_ready, 1)
                if v < 9:
                    xdt(v + 1)
                    seg(v + 1)
                dve.wait_ge(intra_psum, v + 1)
                dve.wait_ge(t1_done, v + 1)
                t1 = T1[v % 2]
                nc.vector.tensor_tensor(t1.rearrange("p j t -> p (j t)"), t1.rearrange("p j t -> p (j t)"), bank(3),
                                        ALU.add).then_inc(t2_done, 1)
                dve.wait_ge(t2_done, v + 1)
                dve.wait_ge(dx_ready, v + 1)
                nc.vector.tensor_tensor(t1, t1, DX, ALU.add).then_inc(t3_done, 1)
                dve.wait_ge(t3_done, v + 1)
                n = CH[c][1]
                zv = ZS[:, 4 * g:4 * g + 4, c * P:c * P + n]
                nc.vector.tensor_tensor(zv, zv, t1[:, :, 0:n], ALU.mult).then_inc(yz_done, 1)
            for s in range(2):
                dve.wait_ge(so_psum, s + 1)
                if s:
                    dve.wait_ge(out_stored, 16 * (KV_STORES + 3))
                nc.vector.tensor_copy(HO, bank(1, 2).rearrange("p (b n) -> p b n", b=8)).then_inc(so_rows, 1)
            dve.wait_ge(rb_ready, 1)
            dve.wait_ge(yz_done, 10)
            for i in range(KD):
                nc.vector.scalar_tensor_tensor(out=ZS[:, i, :], in0=ZS[:, i, :], scalar=G_SSM[:, i:i + 1], in1=RB,
                                               op0=ALU.mult, op1=ALU.mult).then_inc(yn_ready, 1)
            for c in range(KD):
                dve.wait_ge(br_psum, c + 1)
                dve.wait_ge(gs_ready, c + 1)
                nc.vector.tensor_tensor(M1[c % 2], bank(4, 2)[:, 0:T], GS[c % 2], ALU.mult).then_inc(m1_done, 1)
                dve.wait_ge(sb_psum, c + 1)
                dve.wait_ge(gb_ready, c + 1)
                nc.vector.tensor_tensor(MG[:, c, :], bank(6, 2)[:, 0:T], GB[c % 2], ALU.mult).then_inc(m2_done, 1)
                dve.wait_ge(m1_done, c + 1)
                dve.wait_ge(m2_done, c + 1)
                nc.vector.tensor_tensor(MG[:, c, :], MG[:, c, :], M1[c % 2], ALU.add).then_inc(mg_ready, 1)
            def add_rows(psum, done):
                for i in range(2 * NC_):
                    m, h = divmod(i, 2)
                    n = CH[m][1]
                    dve.wait_ge(psum, i + 1)
                    xv = X[:n, m, 512 * h:512 * (h + 1)]
                    nc.vector.tensor_tensor(xv, xv, bank(i % 4)[:n, :], ALU.add).then_inc(done, 1)

            add_rows(wo_psum, x1_ready)
            for m in range(NC_ + 1):
                if m < NC_:
                    n = CH[m][1]
                    norm_scale(dve, N_G + m, X[:n, m, :], n, XN[m % 2][:n, :], m >= 2)
                if m >= 1:
                    t0, n = CH[m - 1]
                    norm_gain(dve, N_G + m - 1, G_MQ, n, 4, HT[:, :, t0:t0 + n])
            dve.wait_ge(out_stored, 16 * MIX_STORES)
            for b in range(4):
                s, m = divmod(b, 2)
                dve.wait_ge(km_psum, b + 1)
                nc.vector.tensor_copy(KM[:, s, :, m * P:(m + 1) * P],
                                      bank(2 * (b % 2), 2).rearrange("p (c n) -> p c n", c=KD)).then_inc(km_ready, 1)

            def pt_out(a):
                h, m = divmod(a, 5)
                t0, n = CH[m]
                dve.wait_ge(pt_psum, a + 1)
                if m == 0 and h >= 2:
                    dve.wait_ge(ot_psum, 2 * (h - 1))
                nc.vector.tensor_copy(PT[h % 2][:, :, t0:t0 + n],
                                      bank(2 + a % 2)[:, 0:256].rearrange("p (k n) -> p k n", k=2)[:, :, 0:n]
                                      ).then_inc(pt_ready, 1)

            for a in range(20):
                n = CH[a % 5][1]
                dve.wait_ge(ms_psum, a + 1)
                nc.vector.tensor_reduce(NM[:n, a:a + 1], bank(a % 2)[:n, 0:ML], AX.X, ALU.max, negate=True).then_inc(nm_ready, 1)
                if a >= 1:
                    pt_out(a - 1)
                dve.wait_ge(px_ready, a + 1)
                nc.vector.reciprocal(RR[:n, a:a + 1], RS[:n, a:a + 1]).then_inc(rr_ready, 1)
                dve.wait_ge(rr_ready, a + 1)
                nc.vector.tensor_scalar(PX[a % 2][:n, :], PX[a % 2][:n, :], RR[:n, a:a + 1], None, ALU.mult).then_inc(pn_ready, 1)
            pt_out(19)
            add_rows(mo_psum, x2_ready)
            for m in range(NC_ + 1):
                if m < NC_:
                    n = CH[m][1]
                    norm_scale(dve, N_I + m, X[:n, m, :], n, XNR[:n, m, :], False)
                if m >= 1:
                    t0, n = CH[m - 1]
                    norm_gain(dve, N_I + m - 1, G_FFN, n, 4, HT[:, :, t0:t0 + n])
            moe_dve(dve)

        def tproj(n, c, b, wt, src=HT, nk=KD, k0=0, m=P):
            for k in range(nk):
                nc.tensor.matmul(bank(b)[0:m, 0:512], wt[:, k0 + k, c:c + m], src[:, k, 0:LP], start=(k == 0), stop=(k == nk - 1))
            for k in range(nk):
                last = nc.tensor.matmul(bank(b + 1)[0:m, 0:LS], wt[:, k0 + k, c:c + m], src[:, k, LP:T], start=(k == 0), stop=(k == nk - 1))
            return last

        def rproj(m, b, wt, src):
            t0, n = CH[m]
            for k in range(KD):
                last = nc.tensor.matmul(bank(b)[:n, :], src[:, k, t0:t0 + n], wt[:, k, :], start=(k == 0), stop=(k == KD - 1))
            return last

        @block.tensor
        def _(pe):
            pe.wait_ge(consts, 6)
            pe.wait_ge(vec_loaded, 16 * 11)
            nc.tensor.transpose(bank(7)[:, 0:100], VEC[0:100, :], IDENT[0:100, 0:100])
            nc.tensor.transpose(bank(7)[:, 128:164], CTXR[0:36, :], IDENT[0:36, 0:36]).then_inc(vec_psum, 1)
            for i, (_, n) in enumerate(srcA):
                norm_turn(pe, i, XN[i % 2][:n, :], n, 0)
            pe.wait_ge(vec_ready, 2)
            for i in range(10):
                t, m = divmod(i, 5)
                if m == 0:
                    weights(pe, (W_K, W_V)[t])
                if t == 0:
                    pe.wait_ge(ht_ready, m + 1)
                if i >= 4:
                    pe.wait_ge(kv_rows, i - 3)
                rproj(m, 4 + i % 4, tile8((W_K, W_V)[t]), HT).then_inc(kv_psum, 1)
            weights(pe, W_Q)
            for i in range(4):
                if i < 2:
                    pe.wait_ge(ht_ready, 7)
                else:
                    pe.wait_ge(q_ready, i - 1)
                tproj(W_Q, i * P, 2 * (i % 2), tile8(W_Q)).then_inc(q_psum, 1)
            pe.wait_ge(kv_rows, 10)
            pe.wait_ge(past_loaded, 32)
            for b in range(9):
                if b >= 4:
                    pe.wait_ge(kt_ready, b - 3)
                rows = KR[:, b, :] if b < 4 else PKR[:, b - 4, :] if b < 8 else KR[:, 4, :]
                for h in range(4):
                    last = nc.tensor.transpose(bank(4 + b % 4)[:, h * P:(h + 1) * P], rows[:, h * P:(h + 1) * P], IDENT)
                last.then_inc(kt_psum, 1)

            def scores(u):
                if u == 0:
                    pe.wait_ge(q_ready, 4)
                    pe.wait_ge(kt_ready, 9)
                else:
                    pe.wait_ge(z_copied, u)
                if u < SBH:
                    hp, lo = divmod(u, 2)
                    r = slice(64 * lo, 64 * lo + 64)
                    for kc in range(4):
                        o, n = keycols(u, kc)
                        last = nc.tensor.matmul(ps[:, o:o + n], KTA[r, hp, kc * P:(kc + 1) * P], QT[r, hp, kc * P:LP],
                                                start=True, stop=True)
                else:
                    for kc in range(5):
                        for j in range(4):
                            hp, lo = j, u - SBH
                            r = slice(64 * lo, 64 * lo + 64)
                            o = kc * 256 + j * 64
                            last = nc.tensor.matmul(ps[:, o:o + 64], KTA[r, hp, LP + kc * P:LP + (kc + 1) * P],
                                                    QT[r, hp, LP:T], start=True, stop=True)
                last.then_inc(z_psum, 1)

            def sums(u):
                pe.wait_ge(sp_ready, u + 1)
                if u >= 1:
                    pe.wait_ge(u_ready, u)
                nk = 4 if u < SBH else 5
                for kc in range(nk):
                    o, n = keycols(u, kc)
                    for j in range(kc, nk):
                        oj, nj = keycols(u, j)
                        last = nc.tensor.matmul(ps[:, 1536 + o + n - nj:1536 + o + n], TSUF if j == kc else ONES,
                                                LB[u % 2][:, oj:oj + nj], start=(j == kc), stop=(j == nk - 1))
                last.then_inc(s_psum, 1)

            def values(u):
                pe.wait_ge(w_ready, u + 1)
                g = u // 2
                if g >= 2 and u % 2 == 0:
                    pe.wait_ge(ysb_ready, g - 1)
                w = ZSB[u % 3]
                if u < SBH:
                    r = slice(64 * (u % 2), 64 * (u % 2) + 64)
                    for kc in range(4):
                        o, n = keycols(u, kc)
                        last = nc.tensor.matmul(bank(6 + g % 2)[r, kc * P:LP], VR[:, kc, u * HD:(u + 1) * HD], w[:, o:o + n],
                                                start=(kc == 0), stop=(kc == 3))
                else:
                    for j in range(4):
                        h = 2 * j + u - SBH
                        r = slice(64 * (h % 2), 64 * (h % 2) + 64)
                        for kc in range(5):
                            vv = PVR[:, kc, h * HD:(h + 1) * HD] if kc < 4 else VR[:, 4, h * HD:(h + 1) * HD]
                            last = nc.tensor.matmul(bank(6 + g % 2)[r, j * 64:j * 64 + 64], vv,
                                                    w[:, kc * 256 + j * 64:kc * 256 + j * 64 + 64],
                                                    start=(kc == 0), stop=(kc == 4))
                last.then_inc(pv_psum, 1)

            scores(0)
            for u in range(U_):
                if u + 1 < U_:
                    scores(u + 1)
                sums(u)
                if u >= 1:
                    values(u - 1)
            values(U_ - 1)

            for i in range(CONV_C):
                if i % 4 == 0:
                    weights(pe, W_X + i // 4)
                if i == 0:
                    pe.wait_ge(z_copied, U_)
                    pe.wait_ge(u_ready, U_)
                if i >= 2:
                    pe.wait_ge(xr_ready, i - 1)
                tproj(0, (i % 4) * P, 2 * (i % 2), tile8((W_X + i // 4) % NRING)).then_inc(xb_psum, 1)
            for i in range(KD):
                if i % 4 == 0:
                    weights(pe, W_Z + i // 4)
                if i < 2:
                    pe.wait_ge(xr_ready, CONV_C - 1 + i)
                else:
                    pe.wait_ge(zt_ready, i - 1)
                tproj(0, (i % 4) * P, 2 * (i % 2), tile8((W_Z + i // 4) % NRING)).then_inc(zt_psum, 1)
            pe.wait_ge(sel_ready, 1)
            pe.wait_ge(ysb_ready, 5)
            for j in range(8):
                last = nc.tensor.matmul(bank(7)[:, 240 + j:241 + j], SELP[0:NH, 2 * j:2 * j + 2, :].rearrange("p a b -> p (a b)"),
                                        HCOL[0:NH, 2:3], start=True, stop=True)
            last.then_inc(dp_psum, 1)
            pe.wait_ge(conv_done, CONV_C)
            for s in range(2):
                nc.tensor.transpose(bank(6)[0:36, P * s:P * (s + 1)], TAIL[:, s].rearrange("p j c -> p (j c)"),
                                    IDENT).then_inc(tail_psum, 1)
            pe.wait_ge(cols_loaded, 16)
            pe.wait_ge(zt_ready, 7)
            tproj(0, 0, 0, WDT, m=NH).then_inc(dt_psum, 1)
            pe.wait_ge(state_loaded, 16)
            pe.wait_ge(dve_dt, 1)
            pe.wait_ge(zt_ready, 8)
            for b in range(8):
                last = nc.tensor.transpose(bank(1, 2)[:, b * P:(b + 1) * P], H0R[:, b, :], IDENT)
            last.then_inc(h0_psum, 1)
            pe.wait_ge(dve_dt, 7)
            pe.wait_ge(vec_ready, 3)
            for c in range(NC_):
                nc.tensor.transpose(bank(7)[:, 16 * c:16 * c + 16], CUM[0:NH, c * P:(c + 1) * P], IDENT[0:NH, 0:NH])
                nc.tensor.transpose(bank(7)[:, 80 + 16 * c:96 + 16 * c], DTT[0:NH, c * P:(c + 1) * P], IDENT[0:NH, 0:NH])
            nc.tensor.matmul(bank(7)[:, 160:240], ONES[0:NH, :], DIAG[0:NH].rearrange("p c h -> p (c h)"),
                             start=True, stop=True).then_inc(pre_psum, 1)
            pe.wait_ge(pre_dve, 4)
            pe.wait_ge(pre_act, 2)
            pe.wait_ge(xc_ready, CONV_C)
            pe.wait_ge(act_dt, 5)
            pe.wait_ge(pads, 2)
            pe.wait_ge(tail_rows, 2)
            for v in range(10):
                c, g = divmod(v, 2)
                tk = slice(c * P, (c + 1) * P)
                sq = 0 if c < 4 else 1
                if v >= 1:
                    pe.wait_ge(sx_done, v)
                for j in range(4):
                    nc.tensor.transpose(bank(7)[:, j * P:(j + 1) * P], XC[:, 4 * g + j, tk], IDENT)
                nc.tensor.transpose(bank(0)[:, 0:P], XC[:, 8 + g, tk], IDENT)
                nc.tensor.matmul(bank(0)[:, P:2 * P], XC[:, 8 + g, tk], XC[:, 10 + g, tk], start=True, stop=True).then_inc(ssd_tr, 1)
                if v >= 1:
                    pe.wait_ge(seg_done, v)
                for h in range(8):
                    last = nc.tensor.matmul(bank(1, 2)[:, h * P:(h + 1) * P], bc(IDENT[0:NH, 8 * g + h:8 * g + h + 1], [NH, P]), CUM[0:NH, tk],
                                            start=True, stop=True)
                last.then_inc(cumb_psum, 1)
                if v >= 1:
                    pe.wait_ge(ec_done, v)
                for j in range(4):
                    a = 8 * g + 2 * j
                    last = nc.tensor.matmul(bank(5)[:, j * P:(j + 1) * P], SELP[0:NH, a:a + 2, :].rearrange("p a b -> p (a b)"),
                                            ECM[0:NH, tk], start=True, stop=True)
                last.then_inc(ec_psum, 1)
                if v >= 1:
                    pe.wait_ge(t1_done, v)
                if v >= 2:
                    pe.wait_ge(h_ready, v - 1)
                for j in range(4):
                    last = nc.tensor.matmul(bank(4)[:, j * P:(j + 1) * P], HS[:, sq, g, j * P:(j + 1) * P], XC[:, 10 + g, tk],
                                            start=True, stop=True)
                last.then_inc(inter_psum, 1)
                pe.wait_ge(sx_done, v + 1)
                if v >= 1:
                    pe.wait_ge(h_ready, v)
                nc.tensor.matmul(bank(6), BROW[v % 2], XW[v % 2], start=True, stop=True).then_inc(st_psum, 1)
                pe.wait_ge(m_ready, v + 1)
                if v >= 1:
                    pe.wait_ge(t2_done, v)
                for h in range(8):
                    r = slice(64 * (h % 2), 64 * (h % 2) + 64)
                    last = nc.tensor.matmul(bank(3)[r, (h // 2) * P:(h // 2 + 1) * P], XD[v % 2][:, h * HD:(h + 1) * HD],
                                            SEG[v % 2][:, h, :], start=True, stop=True)
                last.then_inc(intra_psum, 1)
            pe.wait_ge(h_ready, 10)
            for s in range(2):
                if s:
                    pe.wait_ge(so_rows, 1)
                for b in range(8):
                    last = nc.tensor.transpose(bank(1, 2)[:, b * P:(b + 1) * P],
                                               HS[:, s].rearrange("p g n -> p (g n)")[:, b * P:(b + 1) * P], IDENT)
                last.then_inc(so_psum, 1)
            pe.wait_ge(so_rows, 2)
            pe.wait_ge(sx_done, 10)
            for i in range(KD):
                pe.wait_ge(sq_ready, i + 1)
                nc.tensor.matmul(bank(0), ONES, SQT[i % 2][:, 0:LP], start=(i == 0), stop=(i == KD - 1))
                nc.tensor.matmul(bank(1)[:, 0:LS], ONES, SQT[i % 2][:, LP:T], start=(i == 0), stop=(i == KD - 1)).then_inc(ssq_psum, 1)
            for c in range(KD):
                weights(pe, W_M + c)
                w = mtile((W_M + c) % NRING)
                if c == 0:
                    pe.wait_ge(rb_ln, 1)
                    pe.wait_ge(t2_done, 10)
                    pe.wait_ge(h_ready, 10)
                else:
                    pe.wait_ge(gs_ready, c)
                tproj(0, 0, 0, w, HT, KD, 0).then_inc(gs_psum, 1)
                if c:
                    pe.wait_ge(gb_ready, c)
                tproj(0, 0, 2, w, HT, KD, 8).then_inc(gb_psum, 1)
                if c:
                    pe.wait_ge(m1_done, c)
                else:
                    pe.wait_ge(yn_ready, KD)
                tproj(0, 0, 4, w, ZS, KD, 16).then_inc(br_psum, 1)
                if c:
                    pe.wait_ge(m2_done, c)
                tproj(0, 0, 6, w, YSBT, 4, 24).then_inc(sb_psum, 1)
            pe.wait_ge(mg_ready, KD)
            weights(pe, W_O)
            weights(pe, W_O + 1)
            for i in range(2 * NC_):
                m, h = divmod(i, 2)
                if i >= 4:
                    pe.wait_ge(x1_ready, i - 3)
                rproj(m, i % 4, tile8((W_O + h) % NRING), MG).then_inc(wo_psum, 1)
            pe.wait_ge(x1_ready, 2 * NC_)
            for i in range(8):
                t, m = divmod(i, 2)
                if m == 0:
                    weights(pe, W_KV + t)
                if i >= 4:
                    pe.wait_ge(mkv_rows, i - 3)
                for k in range(KD):
                    last = nc.tensor.matmul(bank(i % 4), MT[:, k, m * P:(m + 1) * P], tile8((W_KV + t) % NRING)[:, k, :],
                                            start=(k == 0), stop=(k == KD - 1))
                last.then_inc(mkv_psum, 1)
            for i, (_, n) in enumerate(CH):
                norm_turn(pe, N_G + i, XN[i % 2][:n, :], n, 4)
            pe.wait_ge(mkv_rows, 8)
            pe.wait_ge(memc_loaded, 32)
            for b in range(4):
                s, m = divmod(b, 2)
                if b >= 2:
                    pe.wait_ge(km_ready, b - 1)
                src = MKV[:, m, 0:D] if s == 0 else MC[:, 0, m, :]
                for c in range(KD):
                    last = nc.tensor.transpose(bank(2 * (b % 2), 2)[:, c * P:(c + 1) * P], src[:, c * P:(c + 1) * P], IDENT)
                last.then_inc(km_psum, 1)
            pe.wait_ge(ht_ready, N_G + NC_)
            for i in range(KD):
                if i % 4 == 0:
                    weights(pe, W_MQ + i // 4)
                if i < 2:
                    pe.wait_ge(km_ready, 3 + i)
                else:
                    pe.wait_ge(mq_ready, i - 1)
                tproj(0, (i % 4) * P, 2 * (i % 2), tile8((W_MQ + i // 4) % NRING)).then_inc(mq_psum, 1)
            pe.wait_ge(mq_ready, KD)

            def mscores(a):
                h, m = divmod(a, 5)
                t0, n = CH[m]
                if a >= 2:
                    pe.wait_ge(px_ready, a - 1)
                for j in range(2):
                    last = nc.tensor.matmul(bank(a % 2)[:n, 0:ML], QM[:, 2 * h + j, t0:t0 + n],
                                            KM[:, 0 if m < 4 else 1, 2 * h + j, :], start=(j == 0), stop=(j == 1))
                last.then_inc(ms_psum, 1)

            def mvalues(h):
                pe.wait_ge(pt_ready, 5 * (h + 1))
                for dc in range(2):
                    if h >= 1:
                        pe.wait_ge(ot_ready, 2 * (h - 1) + dc + 1)
                    f = h * MHD + dc * P
                    for kc in range(2):
                        nc.tensor.matmul(bank(4 + 2 * dc), MKV[:, kc, D + f:D + f + P], PT[h % 2][:, kc, 0:LP],
                                         start=(kc == 0), stop=(kc == 1))
                    for kc in range(2):
                        last = nc.tensor.matmul(bank(5 + 2 * dc)[:, 0:LS], MC[:, 1, kc, f:f + P], PT[h % 2][:, kc, LP:T],
                                                start=(kc == 0), stop=(kc == 1))
                    last.then_inc(ot_psum, 1)

            mscores(0)
            for a in range(20):
                if a + 1 < 20:
                    mscores(a + 1)
                n = CH[a % 5][1]
                pe.wait_ge(pn_ready, a + 1)
                if a >= 2:
                    pe.wait_ge(pt_ready, a - 1)
                for kc in range(2):
                    last = nc.tensor.transpose(bank(2 + a % 2)[:, kc * P:kc * P + n], PX[a % 2][:n, kc * P:(kc + 1) * P],
                                               IDENT[:n, :n])
                last.then_inc(pt_psum, 1)
                if a % 5 == 0 and a >= 5:
                    mvalues(a // 5 - 1)
            mvalues(MH - 1)
            pe.wait_ge(ot_ready, 2 * MH)
            pe.wait_ge(px_ready, 20)
            pe.wait_ge(pt_ready, 20)
            weights(pe, W_MO)
            weights(pe, W_MO + 1)
            for i in range(2 * NC_):
                m, h = divmod(i, 2)
                if i >= 4:
                    pe.wait_ge(x2_ready, i - 3)
                rproj(m, i % 4, tile8((W_MO + h) % NRING), OT).then_inc(mo_psum, 1)
            for i, (_, n) in enumerate(CH):
                norm_turn(pe, N_I + i, XNR[:n, i, :], n, 4)
            moe_pe(pe)


_INS = ["x_prompt", "x_sample", "cache_sb_k", "cache_sb_v", "state_ssm", "state_conv", "cache_mem_k", "cache_mem_v",
        "mem_prompt", "norm_mix", "w_in", "conv_w", "conv_b", "dt_bias", "a_log", "d_skip", "ssm_norm", "w_ssm_br",
        "w_sb_br", "w_out", "norm_mem_q", "norm_mem_kv", "w_mem_q", "w_mem_kv", "w_mem_o", "norm_ffn",
        "w_group_router", "w_expert_router", "w_gate_e", "w_up_e", "w_down_e", "norm_final"]
_OUTS = [("y_prompt", (1, LP, D)), ("y_sample", (1, LS, D)),
         ("sb_k_prompt", (1, 1, LP, SBH, 64)), ("sb_v_prompt", (1, 1, LP, SBH, 64)),
         ("ssm_prompt", (1, 1, NH, HD, NS)), ("conv_prompt", (1, 1, 3, CONV_C * P)),
         ("mem_k_prompt", (1, 1, ML, MH, MHD)), ("mem_v_prompt", (1, 1, ML, MH, MHD)),
         ("sb_k_sample", (1, 1, LS, SBH, 64)), ("sb_v_sample", (1, 1, LS, SBH, 64)),
         ("ssm_sample", (1, 1, NH, HD, NS)), ("conv_sample", (1, 1, 3, CONV_C * P))]


def kernel(**inputs):
    import concourse.bacc as bacc
    from concourse.bass_utils import run_bass_kernel_spmd

    nc = bacc.Bacc("TRN2", target_bir_lowering=False, num_devices=1)
    arrays, ins = {}, {}
    for name in _INS:
        a = np.ascontiguousarray(inputs[name])
        arrays["in_" + name] = a
        ins[name] = nc.dram_tensor("in_" + name, a.shape, mybir.dt.from_np(a.dtype), kind="ExternalInput").ap()
    outs = {name: nc.dram_tensor("out_" + name, shape, F32, kind="ExternalOutput").ap() for name, shape in _OUTS}
    encoder_step(nc, ins, outs)
    r = run_bass_kernel_spmd(nc, [arrays], core_ids=[0])
    return tuple(r.results[0]["out_" + name] for name, _ in _OUTS)
```

```python
from contextlib import ExitStack

import numpy as np
import concourse.bass as bass
from concourse import mybir

F32 = mybir.dt.float32
F32R = mybir.dt.float32r
U32 = mybir.dt.uint32
ACT = mybir.ActivationFunctionType
ALU = mybir.AluOpType
AX = mybir.AxisListType

P = 128
D = 1024
KD = D // P
LP, LS = 512, 64
T = LP + LS
CH = [(0, 128), (128, 128), (256, 128), (384, 128), (512, 64)]
NC_ = len(CH)
PAST = 512
NH, HD, NS = 16, 64, 128
SBH = 8
MH, MHD, ML = 4, 256, 256
NE, FF, TOPG, EPG = 16, 512, 4, 4
CONV_C = 12
EPS = 1e-6
TS = NC_ * P
CAP = NC_ * P
BIG = 1.0e30
C_Z, C_X, C_DT, C_Q, C_K, C_V, C_GS, C_GB = 0, 1024, 2560, 2576, 3088, 3600, 4112, 5136
NRAW, NHI = 4, 2
WT = 2048
NMRING = 6
NXG = 4


class Arena:

    def __init__(self, nc, words):
        self.nc, self.words, self.at, self.count = nc, words, 0, 0
        self.base = -(-nc.sbuf_base // 32) * 32
        self.offset, self.twin = {}, {}

    def mark(self):
        return self.at

    def back(self, at):
        self.at = at

    def flat(self, n):
        n += -n % 8
        self.count += 1
        t = self.nc.alloc_sbuf_tensor_at(f"buf{self.count}", [P, n], F32, offset=self.base + 4 * self.at)
        self.offset[t.name] = (self.base + 4 * self.at, n)
        self.at += n
        assert self.at <= self.words, (self.at, self.words)
        return t

    def view(self, *shape):
        return shaped(self.flat(int(np.prod(shape))), shape)

    def guarded(self, *shape):
        n = int(np.prod(shape))
        t = self.flat(n + 64)
        return shaped(t, shape), t[:, 0:n + 64], t[:, n:n + 64]

    def rounded(self, ap):
        name = ap.tensor.name
        if name not in self.twin:
            offset, n = self.offset[name]
            self.twin[name] = self.nc.alloc_sbuf_tensor_at(name + "_r", [P, n], F32R, offset=offset)
        return bass.AP(tensor=self.twin[name], offset=ap.offset, ap=ap.ap)


def shaped(t, shape):
    a = t[:, 0:int(np.prod(shape))]
    if len(shape) == 1:
        return a
    names = "abcd"[:len(shape)]
    return a.rearrange("p (%s) -> p %s" % (" ".join(names), " ".join(names)),
                       **{c: s for c, s in zip(names[:-1], shape[:-1])})


def bc(ap, shape):
    return ap.to_broadcast(list(shape))


def encoder_step(nc, I, O):
    ctx = ExitStack()
    with ctx:
        sem_names = []

        def sem(name):
            assert name not in sem_names
            sem_names.append(name)
            return ctx.enter_context(nc.semaphore(name))

        WORDS = 53200
        A = Arena(nc, WORDS)
        r32 = A.rounded
        ps = ctx.enter_context(nc.psum_tensor("ps", [P, 8 * 512], F32))
        bank = lambda b, n=1: ps[:, b * 512:(b + n) * 512]

        def pair(b, np_=P):
            return bank(b, 2)[:np_].rearrange("p (h n) -> p h n", h=2)[:, :, 0:T // 2]

        def halves(ap):
            return ap.rearrange("p (h n) -> p h n", h=2)

        hn_rows = nc.dram_tensor("hn_rows", [T, D], F32, kind="Internal").ap()
        y_rows = nc.dram_tensor("y_rows", [NE * CAP, D], F32, kind="Internal").ap()

        X = A.view(NC_, D)
        A.back(0)
        HTH, HTH_F, HTH_END = A.guarded(KD, T)
        A.back(NC_ * D)
        HT, HT_F, HT_END = A.guarded(KD, T)
        IDENT = A.view(P)
        TSUF = A.view(P)
        TINC = A.view(P)
        TSTR = A.view(P)
        ONES = A.view(P)
        VT = A.view(100)
        CTXT = A.view(36)
        SS = A.view(24)
        RL = A.view(24)
        RI = A.view(24)
        DP = A.view(8)
        CST = A.view(4)
        HCOL = A.view(4)
        G_MIX, G_MKV, G_SSM, G_MQ, G_FFN = (VT[:, 8 * i:8 * i + 8] for i in range(5))
        CB = VT[:, 40:52]
        CW = VT[:, 52:100].rearrange("p (j c) -> p j c", j=4)
        WR = A.view(KD, 20)
        ring = A.mark()
        RAW = [A.view(WT) for _ in range(NRAW)]
        HI = [A.view(WT) for _ in range(NHI)]
        A.back(ring)
        MSLOT = [A.view(4096) for _ in range(3)]
        base = A.mark()

        XN = [A.view(D) for _ in range(2)]
        SQ = A.view(D)
        MT = A.view(KD, ML)
        YSBT = A.view(4, T)
        mix = A.mark()

        VEC = A.view(P)
        CTXR = A.view(P)
        KR = A.view(NC_, 512)
        VR = A.view(NC_, 512)
        PVR = A.view(4, 512)
        QT = A.view(4, T)
        KTA = A.view(4, 9 * P)
        att = A.mark()
        XS = A.view(NC_, D)
        MR = A.view(2, D)
        A.back(att + NC_ * D)
        PKR = A.view(4, 512)
        A.back(att)
        ZSB = [A.view(1280) for _ in range(3)]
        LB = [A.view(1280) for _ in range(2)]
        A.back(mix)

        XC = A.view(CONV_C, TS)
        ZS = A.view(KD, T)
        ssd = A.mark()
        XR = [A.view(584) for _ in range(3)]
        CV = [A.view(580) for _ in range(2)]
        UD, AD = A.view(T), A.view(T)
        TAIL = A.view(2, 3, CONV_C)
        TAILR = A.view(2, P)
        DTA, RST = A.view(TS), A.view(TS)
        ssd2 = A.mark()
        A.back(ssd)
        SEG = [A.view(8, P) for _ in range(2)]
        T1 = [A.view(4, P) for _ in range(2)]
        DX = A.view(4, P)
        assert A.at <= ssd + 3 * 584 + 2 * 580 + 2 * T
        HS = A.view(2, 2, 512)
        assert A.at <= ssd2
        A.back(ssd2)
        DTT, CUM, ECM = (A.view(TS) for _ in range(3))
        SELP = A.view(NH, HD)
        DIAG = A.view(NC_, NH)
        CR, DR, TE, CD, WRW = (A.view(NC_, NH) for _ in range(5))
        H0R = HO = A.view(8, P)
        A.back(base)
        XD = [A.view(512) for _ in range(2)]
        XW = [A.view(512) for _ in range(2)]
        BROW = [A.view(P) for _ in range(2)]
        CBM = [A.view(P) for _ in range(2)]
        ECS = A.view(512)
        assert A.at <= base + 3 * D
        A.back(mix)

        MG, MG_F, MG_END = A.guarded(KD, T)
        GS = [A.view(T) for _ in range(2)]
        GB = [A.view(T) for _ in range(2)]
        assert A.at <= mix + CONV_C * TS
        A.back(mix)
        RB = A.view(T)
        SQT = [A.view(T) for _ in range(2)]
        A.back(ssd)
        MGH, MGH_F, MGH_END = A.guarded(KD, T)
        ZSH = A.view(KD, T)
        M1 = [A.view(T)]
        A.back(base)
        YSBTH = A.view(4, T)
        M1.append(A.view(T))
        A.back(mix)

        A.back(mix - 4 * T)
        OT, OT_F, OT_END = A.guarded(KD, T)
        HTH2 = OT
        QM, OTH_F, OTH_END = A.guarded(KD, T)
        OTH = QM
        MKV = A.view(2, 2 * D)
        MC = A.view(2, 2, D)
        late = A.mark()
        KM = A.view(2, KD, ML)
        MTH = A.view(KD, ML)
        A.back(late + 2 * KD * ML)
        PX = [A.view(ML) for _ in range(2)]
        PT = [A.view(2, T) for _ in range(2)]
        NM = A.view(20)
        RS = A.view(20)
        RR = A.view(20)
        A.back(late)
        XNR = A.view(NC_, D)

        A.back(base)
        MSLOT += [A.view(4096) for _ in range(NMRING - 3)]
        XG = [A.view(D) for _ in range(NXG)]
        GT = [A.view(KD, P) for _ in range(2)]
        SG = [A.view(FF) for _ in range(2)]
        HE = [A.view(FF) for _ in range(2)]
        HET = [A.view(4, P) for _ in range(2)]
        A.back(late)
        assert A.at >= base + 3 * 4096 + NXG * D + 2048 + 3 * 1024
        A.view(NC_, D)
        YO = [A.view(D) for _ in range(2)]
        A.back(late)
        NF = A.view(D)
        GM = [A.view(NC_, P) for _ in range(2)]
        IOTA = A.view(P)
        ECAP = A.view(NE)
        W4 = A.view(4)
        TW = A.view(NC_, NE, 2)
        LG = A.view(NC_, 20)
        MX, SM, PSEL, MA, MB, EX, DEN, GA, GB_, RF = (A.view(NC_) for _ in range(10))
        E4, EQ, OHG, LSEL, OH1, L2, OH2 = (A.view(NC_, 4) for _ in range(7))
        TMP, S1, S2, MK, DW, POSP, POSM, TMP2 = (A.view(NC_, NE) for _ in range(8))
        R1F, R2F = A.view(NC_), A.view(NC_)
        R12 = A.view(2, NC_)
        SLOT = A.view(NE, 2)
        IDX = A.view(NE)
        CNT = A.view(NE)
        FLAG = A.view(2)
        PC = A.view(NC_)
        TWO = A.view(NC_, 2)
        SLOTO = A.view(2)
        IDXO = A.view(1)
        assert A.at <= late + NC_ * D
        x_loaded = [sem(f"x_loaded{i}") for i in range(NC_)]
        mem_loaded = [sem(f"mem_loaded{i}") for i in range(2)]
        vec_loaded = sem("vec_loaded")
        past_loaded = sem("past_loaded")
        ring_loaded = [sem(f"ring_loaded{i}") for i in range(NRAW)]
        wh_ready, wl_ready = sem("wh_ready"), sem("wl_ready")
        ah_ready, al_ready = sem("ah_ready"), sem("al_ready")
        state_loaded = sem("state_loaded")
        memc_loaded = sem("memc_loaded")
        out_stored = sem("out_stored")
        late_stored = sem("late_stored")
        const0 = sem("const0")
        consts = sem("consts")
        vec_psum = sem("vec_psum")
        vec_ready = sem("vec_ready")
        dp_psum = sem("dp_psum")
        ss_ready, rl_ready, ri_ready, xn_ready, tp_psum, ht_ready = (
            sem(n) for n in ("ss_ready", "rl_ready", "ri_ready", "xn_ready", "tp_psum", "ht_ready"))
        N_A, N_G, N_I, N_F = 0, 7, 12, 17
        kv_psum, kv_rows = sem("kv_psum"), sem("kv_rows")
        q_psum, q_ready = sem("q_psum"), sem("q_ready")
        kt_psum, kt_ready = sem("kt_psum"), sem("kt_ready")
        z_psum, z_abs, z_copied, z_exp, l_ready = (sem(n) for n in ("z_psum", "z_abs", "z_copied", "z_exp", "l_ready"))
        sp_raw, sp_ready, s_psum, u_ready, w_raw, w_ready, pv_psum, ysb_ready = (
            sem(n) for n in ("sp_raw", "sp_ready", "s_psum", "u_ready", "w_raw", "w_ready", "pv_psum", "ysb_ready"))

        def cols(w, c0, n):
            return w.rearrange("(k p) n -> p k n", p=P)[:, :, c0:c0 + n]

        w_in = I["w_in"][0]
        tiles = []

        def add_tiles(w, c0, n, width=256):
            first = len(tiles)
            for c in range(0, n, width):
                tiles.append(([(0, cols(w, c0 + c, width))], width))
            return first

        W_K = add_tiles(w_in, C_K, 512)
        W_V = add_tiles(w_in, C_V, 512)
        W_Q = add_tiles(w_in, C_Q, 512)
        W_X = add_tiles(w_in, C_X, CONV_C * P)
        W_Z = add_tiles(w_in, C_Z, D)
        W_DT = add_tiles(w_in, C_DT, P, P)
        W_M = len(tiles)
        for c in range(0, D, P):
            tiles.append(([(0, cols(w_in, C_GS + c, P)), (8, cols(w_in, C_GB + c, P))], P))
            tiles.append(([(0, cols(I["w_ssm_br"][0], c, P)), (8, cols(I["w_sb_br"][0], c, P))], P))
        W_O = add_tiles(I["w_out"][0], 0, D)
        W_KV = add_tiles(I["w_mem_kv"][0], 0, 2 * D)
        W_MQ = add_tiles(I["w_mem_q"][0], 0, D)
        W_MO = add_tiles(I["w_mem_o"][0], 0, D)
        landed, tot = [], [0] * NRAW
        for n, (parts, _) in enumerate(tiles):
            tot[n % NRAW] += 16 * len(parts)
            landed.append(tot[n % NRAW])

        def tile_words(n):
            parts, width = tiles[n]
            return width * sum(src.shape[1] for _, src in parts)

        def tile_view(buf, n):
            return buf[:, 0:tile_words(n)].rearrange("p (k n) -> p k n", n=tiles[n][1])

        def w_hi(n):
            return r32(tile_view(HI[n % NHI], n))

        def w_lo(n):
            return r32(tile_view(RAW[n % NRAW], n))

        def split_high(act, n):
            if n >= NHI:
                act.wait_ge(*retire[n - NHI])
            act.wait_ge(ring_loaded[n % NRAW], landed[n])
            nc.scalar.copy(w_hi(n), tile_view(RAW[n % NRAW], n)).then_inc(wh_ready, 1)

        def split_low(dve, n):
            dve.wait_ge(wh_ready, n + 1)
            raw = tile_view(RAW[n % NRAW], n)
            nc.vector.tensor_tensor(r32(raw), raw, w_hi(n), ALU.subtract).then_inc(wl_ready, 1)

        A_HT, A_YSB, A_ZS, A_MG, A_MT, A_HT2, A_OT = 0, 5, 6, 14, 22, 23, 28

        def act_high(hi, src):
            nc.scalar.copy(r32(hi), src).then_inc(ah_ready, 1)

        def act_low(dve, count, src, hi):
            dve.wait_ge(ah_ready, count)
            nc.vector.tensor_tensor(r32(src), src, r32(hi), ALU.subtract).then_inc(al_ready, 1)

        xb_psum, xr_ready, conv_done, xc_ready = (sem(n) for n in ("xb_psum", "xr_ready", "conv_done", "xc_ready"))
        zt_psum, zt_ready = sem("zt_psum"), sem("zt_ready")
        dt_psum = sem("dt_psum")
        dve_dt, act_dt = sem("dve_dt"), sem("act_dt")
        pads = sem("pads")
        tail_rows = sem("tail_rows")
        pre_psum, pre_dve, pre_act = sem("pre_psum"), sem("pre_dve"), sem("pre_act")
        (ssd_tr, sx_done, cumb_psum, seg_done, e_ready, m_ready, ec_psum, ec_done, inter_psum, t1_done,
         intra_psum, t2_done, st_psum, h_dec, h_ready, dx_ready, t3_done, yz_done) = (
            sem(n) for n in ("ssd_tr", "sx_done", "cumb_psum", "seg_done", "e_ready", "m_ready", "ec_psum",
                             "ec_done", "inter_psum", "t1_done", "intra_psum", "t2_done", "st_psum", "h_dec",
                             "h_ready", "dx_ready", "t3_done", "yz_done"))
        so_psum, so_rows = sem("so_psum"), sem("so_rows")
        sq_ready, ssq_psum, rb_ln, rb_ready, yn_ready = (
            sem(n) for n in ("sq_ready", "ssq_psum", "rb_ln", "rb_ready", "yn_ready"))
        (gs_psum, gb_psum, br_psum, sb_psum, gs_ready, gb_ready, m1_done, m2_done, mg_ready) = (
            sem(n) for n in ("gs_psum", "gb_psum", "br_psum", "sb_psum", "gs_ready", "gb_ready", "m1_done",
                             "m2_done", "mg_ready"))
        wo_psum, x1_ready = sem("wo_psum"), sem("x1_ready")
        mkv_psum, mkv_rows, km_psum, km_ready = (sem(n) for n in ("mkv_psum", "mkv_rows", "km_psum", "km_ready"))
        mq_psum, mq_ready = sem("mq_psum"), sem("mq_ready")
        (ms_psum, nm_ready, px_ready, rr_ready, pn_ready, pt_psum, pt_ready, ot_psum, ot_ready) = (
            sem(n) for n in ("ms_psum", "nm_ready", "px_ready", "rr_ready", "pn_ready", "pt_psum", "pt_ready",
                             "ot_psum", "ot_ready"))
        mo_psum, x2_ready = sem("mo_psum"), sem("x2_ready")

        retire = {}
        for first, count, psum, groups in ((W_K, 4, kv_psum, NC_), (W_Q, 2, q_psum, 2), (W_X, 6, xb_psum, 2),
                                           (W_Z, 4, zt_psum, 2), (W_DT, 1, dt_psum, 1), (W_O, 4, wo_psum, NC_),
                                           (W_KV, 8, mkv_psum, 2), (W_MQ, 4, mq_psum, 2), (W_MO, 4, mo_psum, NC_)):
            for j in range(count):
                retire[first + j] = (psum, groups * (j + 1))
        for c in range(KD):
            retire[W_M + 2 * c] = (gb_psum, c + 1)
            retire[W_M + 2 * c + 1] = (sb_psum, c + 1)

        conv_step = sem("conv_step")
        wr_loaded, hn_stored = sem("wr_loaded"), sem("hn_stored")
        lg_psum, route, route_exp, pos_psum, g_ready, g_psum = (
            sem(n) for n in ("lg_psum", "route", "route_exp", "pos_psum", "g_ready", "g_psum"))
        route_const, idx_ready, nf_loaded = sem("route_const"), sem("idx_ready"), sem("nf_loaded")
        mring_loaded = [sem(f"mring_loaded{i}") for i in range(NMRING)]
        xg_loaded = [sem(f"xg_loaded{i}") for i in range(NXG)]
        y_stored = [sem(f"y_stored{i}") for i in range(2)]
        (gt_psum, gt_ready, ge_psum, up_psum, sg_ready, he_ready, het_psum, het_ready, yd_psum, yo_ready) = (
            sem(n) for n in ("gt_psum", "gt_ready", "ge_psum", "up_psum", "sg_ready", "he_ready", "het_psum",
                             "het_ready", "yd_psum", "yo_ready"))
        fin_loaded = [sem(f"fin_loaded{i}") for i in range(2)]
        y1_sum, x3_ready, fin_ready = (sem(n) for n in ("y1_sum", "x3_ready", "fin_ready"))
        KV_STORES = 4
        MIX_STORES = 8
        stored = [0]

        U_ = 10
        OFF = [0, 512, 1024, 896]

        def keycols(u, kc):
            if u < SBH:
                return OFF[kc], LP - kc * P
            return kc * 256, 256

        def out_dma(eng, dst, src, done=out_stored):
            eng.dma_start(dst, src).then_inc(done, 16)
            if done is out_stored:
                stored[0] += 1

        def norm_stat(i, src, n, scratch):
            sl = slice(i, i + 1)
            nc.scalar.activation(scratch[:n, :], src, ACT.Square, accum_out=SS[:n, sl]).then_inc(ss_ready, 1)
            nc.scalar.wait_ge(ss_ready, i + 1)
            nc.scalar.activation(RL[:n, sl], SS[:n, sl], ACT.Ln, scale=1.0 / D, bias=CST[:n, 0:1]).then_inc(rl_ready, 1)
            nc.scalar.wait_ge(rl_ready, i + 1)
            nc.scalar.activation(RI[:n, sl], RL[:n, sl], ACT.Exp, scale=-0.5).then_inc(ri_ready, 1)

        def norm_scale(dve, i, src, n, dst, reused):
            dve.wait_ge(ri_ready, i + 1)
            if reused:
                dve.wait_ge(tp_psum, i - 1)
            nc.vector.tensor_scalar(dst, src, RI[:n, i:i + 1], None, ALU.mult).then_inc(xn_ready, 1)

        def norm_banks(i, b0):
            return bank(b0 + 2 * (i % 2), 2).rearrange("p (c n) -> p c n", c=KD)

        def norm_turn(pe, i, src, n, b0):
            pe.wait_ge(xn_ready, i + 1)
            if i >= 2:
                pe.wait_ge(ht_ready, i - 1)
            for c in range(KD):
                last = nc.tensor.transpose(norm_banks(i, b0)[:, c, 0:n], src[:, c * P:(c + 1) * P], IDENT[:n, :n])
            last.then_inc(tp_psum, 1)

        def norm_gain(dve, i, gain, n, b0, dst):
            dve.wait_ge(tp_psum, i + 1)
            nc.vector.tensor_tensor(dst, norm_banks(i, b0)[:, :, 0:n], bc(gain.unsqueeze(2), [P, KD, n]),
                                    ALU.mult).then_inc(ht_ready, 1)

        srcA = [(XS[:n, m, :], n) for m, (_, n) in enumerate(CH)] + [(MR[:, m, :], P) for m in range(2)]
        dstA = [HT[:, :, t0:t0 + n] for t0, n in CH] + [MT[:, :, m * P:(m + 1) * P] for m in range(2)]

        def rstep(dve, n, ins):
            ins.then_inc(route, 1)
            dve.wait_ge(route, n)

        def route_dve(dve):
            k = [0]

            def go(ins):
                k[0] += 1
                rstep(dve, k[0], ins)

            v = nc.vector
            b3 = lambda a: bc(a.unsqueeze(2), [P, NC_, 4])
            g4 = lambda a: a.rearrange("p c (g k) -> p c g k", g=4)
            dve.wait_ge(hn_stored, 16 * NC_)
            dve.wait_ge(tp_psum, N_I + NC_)
            go(v.memset(LG, 0.0))
            dve.wait_ge(lg_psum, 1)
            go(v.tensor_copy(LG[:, 0:4, :], bank(0)[:, 0:128].rearrange("p (c n) -> p c n", c=4)[:, :, 0:20]))
            go(v.tensor_copy(LG[:LS, 4, :], bank(0)[:LS, 128:148]))
            lgg = LG[:, :, 0:4]
            dve.wait_ge(route_const, 4)
            go(v.tensor_reduce(MX, lgg, AX.X, ALU.max))
            go(v.tensor_tensor(E4, lgg, b3(MX), ALU.subtract))
            assert k[0] == 5
            go(v.tensor_tensor(EQ, lgg, b3(MX), ALU.is_equal))

            def first_largest(eq, oh):
                go(v.tensor_tensor(eq, eq, bc(W4.unsqueeze(1), [P, NC_, 4]), ALU.mult))
                go(v.tensor_reduce(RF, eq, AX.X, ALU.max))
                go(v.tensor_tensor(oh, eq, b3(RF), ALU.is_equal))

            first_largest(EQ, OHG)
            le = LG[:, :, 4:20]
            for g in range(4):
                if g == 0:
                    go(v.tensor_tensor(LSEL, le[:, :, 0:4], bc(OHG[:, :, 0:1], [P, NC_, 4]), ALU.mult))
                else:
                    go(v.tensor_tensor(OH2, le[:, :, 4 * g:4 * g + 4], bc(OHG[:, :, g:g + 1], [P, NC_, 4]), ALU.mult))
                    go(v.tensor_tensor(LSEL, LSEL, OH2, ALU.add))
            go(v.tensor_reduce(MA, LSEL, AX.X, ALU.max))
            go(v.tensor_tensor(EQ, LSEL, b3(MA), ALU.is_equal))
            first_largest(EQ, OH1)
            go(v.scalar_tensor_tensor(out=L2, in0=OH1, scalar=-BIG, in1=LSEL, op0=ALU.mult, op1=ALU.add))
            go(v.tensor_reduce(MB, L2, AX.X, ALU.max))
            go(v.tensor_tensor(EQ, L2, b3(MB), ALU.is_equal))
            first_largest(EQ, OH2)
            go(v.tensor_tensor(EX, MB, MA, ALU.subtract))
            route_steps["diff"] = k[0]
            for s_, oh in ((S1, OH1), (S2, OH2)):
                for g in range(4):
                    go(v.tensor_tensor(s_[:, :, 4 * g:4 * g + 4], oh, bc(OHG[:, :, g:g + 1], [P, NC_, 4]), ALU.mult))
                go(v.memset(s_[LS:, 4, :], 0.0))
            go(v.tensor_tensor(MK, S1, S2, ALU.add))
            route_steps["mask"] = k[0]
            dve.wait_ge(route_exp, 2)
            go(v.tensor_reduce(SM, E4, AX.X, ALU.add))
            go(v.reciprocal(PSEL, SM))
            go(v.tensor_scalar(DEN, EX, 1.0, None, ALU.add))
            go(v.reciprocal(GA, DEN))
            go(v.tensor_tensor(GA, GA, PSEL, ALU.mult))
            go(v.tensor_tensor(GB_, GA, EX, ALU.mult))
            b16 = lambda a: bc(a.unsqueeze(2), [P, NC_, NE])
            go(v.tensor_tensor(DW, S1, b16(GA), ALU.mult))
            go(v.tensor_tensor(TMP, S2, b16(GB_), ALU.mult))
            go(v.tensor_tensor(TW[:, :, :, 1], DW, TMP, ALU.add))
            dve.wait_ge(pos_psum, 1)
            go(v.tensor_copy(POSP, bank(1)[:, 0:80].rearrange("p (c e) -> p c e", c=NC_)))
            go(v.tensor_copy(CNT, bank(1)[:, 80:96]))
            go(v.scalar_tensor_tensor(out=POSM, in0=POSP, scalar=1.0, in1=MK, op0=ALU.add, op1=ALU.mult))
            go(v.tensor_scalar(POSM, POSM, -1.0, None, ALU.add))
            route_steps["pos"] = k[0]
            for e in range(NE):
                if e >= 2:
                    dve.wait_ge(g_psum, e - 1)
                nc.vector.tensor_tensor(GM[e % 2], bc(IOTA.unsqueeze(1), [P, NC_, P]),
                                        bc(POSM[:, :, e:e + 1], [P, NC_, P]), ALU.is_equal).then_inc(g_ready, 1)
            go(v.tensor_scalar(TMP2, POSP, float(P), None, ALU.is_ge))
            for j in range(2, NC_):
                go(v.scalar_tensor_tensor(out=TMP2, in0=POSP, scalar=float(P * j), in1=TMP2, op0=ALU.is_ge, op1=ALU.add))
            go(v.scalar_tensor_tensor(out=POSP, in0=TMP2, scalar=float((NE - 1) * P), in1=POSP, op0=ALU.mult, op1=ALU.add))
            go(v.tensor_tensor(POSP, POSP, bc(ECAP.unsqueeze(1), [P, NC_, NE]), ALU.add))
            for s_, r, i in ((S1, R1F, 0), (S2, R2F, 1)):
                go(v.tensor_tensor(TMP, POSP, s_, ALU.mult))
                go(v.tensor_reduce(r, TMP, AX.X, ALU.add))
                go(v.tensor_copy(R12[:, i, :].bitcast(U32), r))
            go(v.tensor_reduce(FLAG[:, 0:1], CNT, AX.X, ALU.max))
            dve.wait_ge(g_psum, NE)
            go(v.tensor_copy(SLOT, bank(2)[:, 0:2 * NE].rearrange("p (e n) -> p e n", e=NE)))
            v.tensor_copy(FLAG[:, 1:2].bitcast(U32), FLAG[:, 0:1]).then_inc(idx_ready, 1)
            v.tensor_copy(IDX.bitcast(U32), SLOT[:, :, 0]).then_inc(idx_ready, 1)

        route_steps = {}

        def route_pe(pe):
            pe.wait_ge(wr_loaded, 32)
            pe.wait_ge(ht_ready, N_I + NC_)
            pe.wait_ge(x2_ready, 4 * NC_)
            for m, (t0, n) in enumerate(CH):
                for k in range(KD):
                    last = nc.tensor.matmul(bank(0)[:n, 32 * m:32 * m + 20], HT[:, k, t0:t0 + n], WR[:, k, :],
                                            start=(k == 0), stop=(k == KD - 1))
            last.then_inc(lg_psum, 1)
            pe.wait_ge(route, route_steps["mask"])
            for c in range(NC_ + 1):
                for c2 in range(min(c + 1, NC_)):
                    last = nc.tensor.matmul(bank(1)[:, 16 * c:16 * c + 16], TSTR if c2 == c else ONES, MK[:, c2, :],
                                            start=(c2 == 0), stop=(c2 == min(c, NC_ - 1)))
            last.then_inc(pos_psum, 1)
            for e in range(NE):
                pe.wait_ge(g_ready, e + 1)
                for c in range(NC_):
                    last = nc.tensor.matmul(bank(2)[:, 2 * e:2 * e + 2], GM[e % 2][:, c, :], TW[:, c, e, :],
                                            start=(c == 0), stop=(c == NC_ - 1))
                last.then_inc(g_psum, 1)
            pe.wait_ge(idx_ready, 2)

        MT_SRC = []
        for e in range(NE):
            MT_SRC += [I["w_gate_e"][0, e].rearrange("(k p) f -> p k f", p=P),
                       I["w_up_e"][0, e].rearrange("(k p) f -> p k f", p=P),
                       I["w_down_e"][0, e].rearrange("(k p) f -> p k f", p=P)]

        def mview(q):
            return MSLOT[q % NMRING].rearrange("p (k f) -> p k f", f=FF if q % 3 < 2 else D)

        def experts_sp(sp):
            for q in range(3 * NE):
                if q < 3:
                    sp.wait_ge(mo_psum, 4 * NC_)
                elif q < NMRING:
                    sp.wait_ge(hn_stored, 16 * NC_)
                    sp.wait_ge(ht_ready, N_I + NC_)
                else:
                    e, j = divmod(q - NMRING, 3)
                    sp.wait_ge((ge_psum, up_psum, yd_psum)[j], e + 1)
                sp.dma_start(mview(q), MT_SRC[q]).then_inc(mring_loaded[q % NMRING], 16)
                if q == 8:
                    sp.wait_ge(idx_ready, 1)
                    sp.dma_start(NF, I["norm_final"].rearrange("(a d) -> a d", a=1).to_broadcast([P, D])).then_inc(nf_loaded, 16)

        def expert_weights(pe, q):
            pe.wait_ge(mring_loaded[q % NMRING], 16 * (q // NMRING + 1))

        def turn_tokens(src):
            for c in range(KD):
                last = nc.tensor.transpose(bank(0, 2)[:, c * P:(c + 1) * P], src[:, c * P:(c + 1) * P], IDENT)
            return last

        def expert_rows(b, gt, w):
            for k in range(KD):
                last = nc.tensor.matmul(bank(b), gt[:, k, :], w[:, k, :], start=(k == 0), stop=(k == KD - 1))
            return last

        def turn_hidden(he):
            for c in range(4):
                last = nc.tensor.transpose(bank(4)[:, c * P:(c + 1) * P], he[:, c * P:(c + 1) * P], IDENT)
            return last

        def expert_down(het, w):
            for h in range(2):
                for c in range(4):
                    last = nc.tensor.matmul(bank(5 + h), het[:, c, :], w[:, c, 512 * h:512 * (h + 1)],
                                            start=(c == 0), stop=(c == 3))
            return last

        def experts_pe(pe):
            def turn(e):
                pe.wait_ge(xg_loaded[e % NXG], 16 * (e // NXG + 1))
                if e:
                    pe.wait_ge(gt_ready, e)
                turn_tokens(XG[e % NXG]).then_inc(gt_psum, 1)

            turn(0)
            for e in range(NE):
                pe.wait_ge(gt_ready, e + 1)
                expert_weights(pe, 3 * e)
                if e:
                    pe.wait_ge(sg_ready, e)
                expert_rows(2, GT[e % 2], mview(3 * e)).then_inc(ge_psum, 1)
                expert_weights(pe, 3 * e + 1)
                if e:
                    pe.wait_ge(he_ready, e)
                expert_rows(3, GT[e % 2], mview(3 * e + 1)).then_inc(up_psum, 1)
                if e + 1 < NE:
                    turn(e + 1)
                pe.wait_ge(he_ready, e + 1)
                if e:
                    pe.wait_ge(het_ready, e)
                turn_hidden(HE[e % 2]).then_inc(het_psum, 1)
                pe.wait_ge(het_ready, e + 1)
                expert_weights(pe, 3 * e + 2)
                if e:
                    pe.wait_ge(yo_ready, e)
                expert_down(HET[e % 2], mview(3 * e + 2)).then_inc(yd_psum, 1)

        def experts_act(act):
            for e in range(NE):
                act.wait_ge(ge_psum, e + 1)
                if e >= 2:
                    act.wait_ge(he_ready, e - 1)
                nc.scalar.activation(SG[e % 2], bank(2), ACT.Silu).then_inc(sg_ready, 1)
                act.wait_ge(yd_psum, e + 1)
                if e >= 2:
                    act.wait_ge(y_stored[e % 2], 16 * (e // 2))
                nc.scalar.activation(YO[e % 2], bank(5, 2), ACT.Copy, scale=SLOT[:, e, 1:2]).then_inc(yo_ready, 1)
                act.wait_ge(yo_ready, e + 1)
                act.dma_start(y_rows[e * P:(e + 1) * P, :], YO[e % 2]).then_inc(y_stored[e % 2], 16)

        def experts_dve(dve):
            for e in range(NE):
                if e == 0:
                    dve.wait_ge(gt_psum, 1)
                    gain_tokens(GT[0]).then_inc(gt_ready, 1)
                dve.wait_ge(sg_ready, e + 1)
                dve.wait_ge(up_psum, e + 1)
                if e >= 2:
                    dve.wait_ge(het_psum, e - 1)
                nc.vector.tensor_tensor(HE[e % 2], bank(3), SG[e % 2], ALU.mult).then_inc(he_ready, 1)
                if e + 1 < NE:
                    dve.wait_ge(gt_psum, e + 2)
                    if e >= 1:
                        dve.wait_ge(up_psum, e)
                    gain_tokens(GT[(e + 1) % 2]).then_inc(gt_ready, 1)
                dve.wait_ge(het_psum, e + 1)
                if e >= 2:
                    dve.wait_ge(yd_psum, e - 1)
                nc.vector.tensor_copy(HET[e % 2], bank(4).rearrange("p (c n) -> p c n", c=4)).then_inc(het_ready, 1)

        def gain_tokens(dst):
            return nc.vector.tensor_tensor(dst, bank(0, 2).rearrange("p (c n) -> p c n", c=KD),
                                           bc(G_FFN.unsqueeze(2), [P, KD, P]), ALU.mult)

        def experts_pool(pool):
            for e in range(NE):
                if e >= NXG:
                    pool.wait_ge(gt_psum, e - NXG + 1)
                pool.indirect_dma_start(XG[e % NXG], None, hn_rows,
                                        bass.IndirectOffsetOnAxis(ap=IDX.bitcast(U32)[:, e:e + 1], axis=0)
                                        ).then_inc(xg_loaded[e % NXG], 16)

        def overflow(eng, body):
            count = eng.value_load(FLAG[0:1, 1:2].bitcast(U32), min_val=0, max_val=T)
            with eng.If(count > P):
                with eng.Fori(0, NE) as e:
                    for j in range(1, NC_):
                        body(e, j)
                        eng.wait_ge(y_stored[0], 16 * (NE // 2) + nth(e, j, 16))

        def nth(e, j, k=1):
            return e * (k * (NC_ - 1)) + k * j

        def overflow_sp(e):
            nc.sync.wait_ge(y_stored[0], 16 * (NE // 2) + nth(e, 0, 16))
            for i, name in enumerate(("w_gate_e", "w_up_e", "w_down_e")):
                nc.sync.dma_start(mview(i), I[name][0, bass.ds(e, 1)].rearrange("a (k p) f -> p (a k) f", p=P)
                                  ).then_inc(mring_loaded[0], 16)

        def overflow_pool(e, j):
            nc.gpsimd.wait_ge(idx_ready, 2 + nth(e, j, 2))
            nc.gpsimd.indirect_dma_start(XG[0], None, hn_rows, bass.IndirectOffsetOnAxis(ap=IDXO.bitcast(U32), axis=0)
                                         ).then_inc(xg_loaded[0], 16)

        def overflow_pe(e, j):
            pe = nc.tensor
            pe.wait_ge(g_ready, NE + nth(e, j, 3))
            for c in range(NC_):
                last = pe.matmul(bank(7)[:, 0:2], GM[0][:, c, :], TWO[:, c, :], start=(c == 0), stop=(c == NC_ - 1))
            last.then_inc(g_psum, 1)
            pe.wait_ge(xg_loaded[0], 16 * (NE // NXG) + nth(e, j, 16))
            turn_tokens(XG[0]).then_inc(gt_psum, 1)
            pe.wait_ge(gt_ready, NE + nth(e, j))
            pe.wait_ge(mring_loaded[0], 16 * (3 * NE // NMRING) + e * 48 + 48)
            expert_rows(2, GT[0], mview(0)).then_inc(ge_psum, 1)
            expert_rows(3, GT[0], mview(1)).then_inc(up_psum, 1)
            pe.wait_ge(he_ready, NE + nth(e, j))
            turn_hidden(HE[0]).then_inc(het_psum, 1)
            pe.wait_ge(het_ready, NE + nth(e, j))
            expert_down(HET[0], mview(2)).then_inc(yd_psum, 1)

        def overflow_dve(e, j):
            dve = nc.vector
            dve.tensor_scalar(PC.unsqueeze(2), POSM[:, :, bass.ds(e, 1)], -float(P * j), None, ALU.add).then_inc(g_ready, 1)
            dve.tensor_copy(TWO.unsqueeze(2), TW[:, :, bass.ds(e, 1), :]).then_inc(g_ready, 1)
            dve.wait_ge(g_ready, NE + nth(e, j, 3) - 1)
            dve.tensor_tensor(GM[0], bc(IOTA.unsqueeze(1), [P, NC_, P]), bc(PC.unsqueeze(2), [P, NC_, P]),
                              ALU.is_equal).then_inc(g_ready, 1)
            dve.wait_ge(g_psum, NE + nth(e, j))
            dve.tensor_copy(SLOTO, bank(7)[:, 0:2]).then_inc(idx_ready, 1)
            dve.wait_ge(idx_ready, 1 + nth(e, j, 2))
            dve.tensor_copy(IDXO.bitcast(U32), SLOTO[:, 0:1]).then_inc(idx_ready, 1)
            dve.wait_ge(gt_psum, NE + nth(e, j))
            gain_tokens(GT[0]).then_inc(gt_ready, 1)
            dve.wait_ge(sg_ready, NE + nth(e, j))
            dve.wait_ge(up_psum, NE + nth(e, j))
            dve.tensor_tensor(HE[0], bank(3), SG[0], ALU.mult).then_inc(he_ready, 1)
            dve.wait_ge(het_psum, NE + nth(e, j))
            dve.tensor_copy(HET[0], bank(4).rearrange("p (c n) -> p c n", c=4)).then_inc(het_ready, 1)

        def overflow_act(e, j):
            act = nc.scalar
            act.wait_ge(ge_psum, NE + nth(e, j))
            act.activation(SG[0], bank(2), ACT.Silu).then_inc(sg_ready, 1)
            act.wait_ge(yd_psum, NE + nth(e, j))
            act.wait_ge(idx_ready, 1 + nth(e, j, 2))
            act.activation(YO[0], bank(5, 2), ACT.Copy, scale=SLOTO[:, 1:2]).then_inc(yo_ready, 1)
            act.wait_ge(yo_ready, NE + nth(e, j))
            act.dma_start(y_rows[bass.ds(e * P + NE * P * j, P), :], YO[0]).then_inc(y_stored[0], 16)

        def moe_sp(sp):
            experts_sp(sp)
            sp.wait_ge(yd_psum, NE)
            count = sp.value_load(FLAG[0:1, 1:2].bitcast(U32), min_val=0, max_val=T)
            with sp.If(count > P):
                with sp.Fori(0, NE) as e:
                    overflow_sp(e)

        def moe_pool(pool):
            for m, (t0, n) in enumerate(CH):
                pool.wait_ge(xn_ready, N_I + m + 1)
                pool.dma_start(hn_rows[t0:t0 + n, :], XNR[:n, m, :]).then_inc(hn_stored, 16)
            pool.wait_ge(hn_stored, 16 * NC_)
            pool.wait_ge(tp_psum, N_I + NC_)
            pool.iota(IOTA, [[1, P]], base=0, channel_multiplier=0, allow_small_or_imprecise_dtypes=True).then_inc(route_const, 1)
            pool.iota(ECAP, [[P, NE]], base=0, channel_multiplier=0, allow_small_or_imprecise_dtypes=True).then_inc(route_const, 1)
            for i in range(4):
                last = pool.memset(W4[:, i:i + 1], float(8 >> i))
            last.then_inc(route_const, 1)
            for c in range(NC_):
                last = pool.iota(TW[:, c, :, 0], [[0, NE]], base=c * P, channel_multiplier=1, allow_small_or_imprecise_dtypes=True)
            last.then_inc(route_const, 1)
            pool.wait_ge(idx_ready, 2)
            experts_pool(pool)
            pool.wait_ge(gt_psum, NE)
            count = pool.value_load(FLAG[0:1, 1:2].bitcast(U32), min_val=0, max_val=T)
            with pool.If(count > P):
                for e in range(NE):
                    for j in range(1, NC_):
                        overflow_pool(e, j)
                        pool.wait_ge(y_stored[0], 16 * (NE // 2) + nth(e, j, 16))
            for i in range(2):
                pool.wait_ge(y_stored[i], 16 * (NE // 2))
            with pool.If(count > P):
                gather_results(pool, y_rows)
            with pool.If(count <= P):
                gather_results(pool, y_rows[0:NE * P, :])
            for m, (t0, n) in enumerate(CH):
                pool.wait_ge(fin_ready, m + 1)
                dst = O["y_prompt"][0, t0:t0 + n, :] if m < 4 else O["y_sample"][0]
                out_dma(pool, dst, X[:n, m, :], late_stored)

        def gather_results(pool, rows):
            for m, (t0, n) in enumerate(CH):
                if m >= 2:
                    pool.wait_ge(x3_ready, m - 1)
                for i in range(2):
                    pool.indirect_dma_start(XG[2 * (m % 2) + i][:n, :], None, rows,
                                            bass.IndirectOffsetOnAxis(ap=R12.bitcast(U32)[:n, i, m:m + 1], axis=0)
                                            ).then_inc(fin_loaded[m % 2], 16)

        def moe_act(act):
            act.wait_ge(route, 5)
            nc.scalar.activation(E4, E4, ACT.Exp).then_inc(route_exp, 1)
            act.wait_ge(route, route_diff)
            nc.scalar.activation(EX, EX, ACT.Exp).then_inc(route_exp, 1)
            act.wait_ge(idx_ready, 2)
            experts_act(act)
            act.wait_ge(y_stored[0], 16 * (NE // 2))
            overflow(act, overflow_act)
            for m, (_, n) in enumerate(CH):
                act.wait_ge(x3_ready, m + 1)
                norm_stat(N_F + m, X[:n, m, :], n, SQ2)

        def moe_dve(dve):
            route_dve(dve)
            dve.wait_ge(idx_ready, 2)
            experts_dve(dve)
            overflow(dve, overflow_dve)
            dve.wait_ge(nf_loaded, 16)

            def finish(m):
                n = CH[m][1]
                dve.wait_ge(ri_ready, N_F + m + 1)
                nc.vector.scalar_tensor_tensor(out=X[:n, m, :], in0=X[:n, m, :], scalar=RI[:n, 17 + m:18 + m], in1=NF[:n, :],
                                               op0=ALU.mult, op1=ALU.mult).then_inc(fin_ready, 1)

            for m, (_, n) in enumerate(CH):
                dve.wait_ge(fin_loaded[m % 2], 32 * (m // 2 + 1))
                nc.vector.tensor_tensor(X[:n, m, :], X[:n, m, :], XG[2 * (m % 2)][:n, :], ALU.add).then_inc(y1_sum, 1)
                dve.wait_ge(y1_sum, m + 1)
                nc.vector.tensor_tensor(X[:n, m, :], X[:n, m, :], XG[2 * (m % 2) + 1][:n, :], ALU.add).then_inc(x3_ready, 1)
                if m:
                    finish(m - 1)
            finish(NC_ - 1)

        def moe_pe(pe):
            route_pe(pe)
            experts_pe(pe)
            overflow(pe, overflow_pe)

        route_diff = 28
        SQ2 = GT[0].rearrange("p c n -> p (c n)")
        block = ctx.enter_context(nc.Block())

        @block.sync
        def _(sp):
            xr = I["x_prompt"][0].rearrange("(m p) d -> p m d", p=P)
            def load_rows(dst):
                for m in range(4):
                    sp.dma_start(dst[:, m, :], xr[:, m, :]).then_inc(x_loaded[m], 16)
                sp.dma_start(dst[:LS, 4, :], I["x_sample"][0]).then_inc(x_loaded[4], 16)

            def load(n):
                if n >= NRAW:
                    sp.wait_ge(*retire[n - NRAW])
                for k0, src in tiles[n][0]:
                    sp.dma_start(tile_view(RAW[n % NRAW], n)[:, k0:k0 + src.shape[1], :], src).then_inc(ring_loaded[n % NRAW], 16)

            load_rows(XS)
            load(0)
            load(1)
            for m in range(2):
                sp.dma_start(MR[:, m, :], I["mem_prompt"][0, m * P:(m + 1) * P, :]).then_inc(mem_loaded[m], 16)
            load(2)
            load(3)
            sp.dma_start(PVR, I["cache_sb_v"][0, 0].rearrange("(c p) h d -> p c (h d)", p=P)).then_inc(past_loaded, 16)
            sp.wait_ge(xn_ready, 7)
            sp.dma_start(PKR, I["cache_sb_k"][0, 0].rearrange("(c p) h d -> p c (h d)", p=P)).then_inc(past_loaded, 16)
            for n in range(4, W_X + 4):
                load(n)
            sp.wait_ge(ysb_ready, 5)
            sp.wait_ge(out_stored, 16 * KV_STORES)
            sp.dma_start(H0R, I["state_ssm"][0, 0].rearrange("h q n -> (h q) n").rearrange("(b p) n -> p b n", p=P)
                         ).then_inc(state_loaded, 16)
            for n in range(W_X + 4, W_O + 2):
                load(n)
            sp.wait_ge(gb_psum, KD)
            load_rows(X)
            for n in range(W_O + 2, W_KV + 5):
                load(n)
            sp.wait_ge(mg_ready, KD)
            sp.wait_ge(wo_psum, 4 * NC_)
            sp.dma_start(MC[:, 0], I["cache_mem_k"][0, 0].rearrange("(m p) h d -> p m (h d)", p=P)).then_inc(memc_loaded, 16)
            sp.dma_start(MC[:, 1], I["cache_mem_v"][0, 0].rearrange("(m p) h d -> p m (h d)", p=P)).then_inc(memc_loaded, 16)
            for n in range(W_KV + 5, len(tiles)):
                load(n)
            moe_sp(sp)
            sp.wait_ge(out_stored, 16 * MIX_STORES)
            sp.wait_ge(late_stored, 16 * (4 + NC_))

        @block.gpsimd
        def _(pool):
            rows = [("norm_mix", 0), ("norm_mem_kv", 8), ("ssm_norm", 16), ("norm_mem_q", 24), ("norm_ffn", 32),
                    ("conv_b", 40)]
            for name, r in rows:
                v = I[name][0].rearrange("(r p) -> r p", p=P)
                pool.dma_start(VEC[r:r + v.shape[0], :], v).then_inc(vec_loaded, 16)
            pool.dma_start(VEC[52:100, :], I["conv_w"][0].rearrange("j (c p) -> (j c) p", p=P)).then_inc(vec_loaded, 16)
            pool.dma_start(CTXR[0:36, :], I["state_conv"][0, 0].rearrange("j (c p) -> (j c) p", p=P)).then_inc(vec_loaded, 16)
            for i, name in enumerate(("dt_bias", "a_log", "d_skip")):
                pool.dma_start(HCOL[0:NH, i:i + 1], I[name].rearrange("a h -> h a")).then_inc(vec_loaded, 16)
            pool.dma_start(WR[:, :, 0:4], I["w_group_router"][0].rearrange("(k p) n -> p k n", p=P)).then_inc(wr_loaded, 16)
            pool.dma_start(WR[:, :, 4:20], I["w_expert_router"][0].rearrange("(k p) n -> p k n", p=P)).then_inc(wr_loaded, 16)
            for m in (IDENT, ):
                nc.gpsimd.memset(m, 0.0).then_inc(const0, 1)
            for m in (TSUF, TINC, TSTR):
                nc.gpsimd.memset(m, 1.0).then_inc(const0, 1)
            nc.gpsimd.memset(ONES, 1.0).then_inc(consts, 1)
            nc.gpsimd.memset(CST, EPS).then_inc(consts, 1)
            pool.wait_ge(const0, 4)
            for m, op, step, cm in ((IDENT, ALU.not_equal, -1, 1), (TSUF, ALU.is_ge, -1, 1),
                                    (TINC, ALU.is_ge, 1, -1), (TSTR, ALU.is_gt, 1, -1)):
                pool.affine_select(out=m, in_=m, compare_op=op, fill=1.0 if m is IDENT else 0.0, base=0,
                                   pattern=[[step, P]], channel_multiplier=cm).then_inc(consts, 1)
            for g, (name, rows_) in enumerate((("sb_k", KR), ("sb_v", VR))):
                pool.wait_ge(kv_rows, 10 * (g + 1))
                out_dma(pool, O[name + "_prompt"][0, 0].rearrange("(m p) h d -> p m (h d)", p=P), rows_[:, 0:4, :])
                out_dma(pool, O[name + "_sample"][0, 0].rearrange("p h d -> p (h d)"), rows_[:LS, 4, :])

            def mask(u, buf, done):
                if u < SBH:
                    for kc in range(4):
                        v = buf[:, OFF[kc]:OFF[kc] + P]
                        last = pool.affine_select(out=v, in_=v, compare_op=ALU.is_gt, fill=0.0, base=0,
                                                  pattern=[[1, P]], channel_multiplier=-1)
                else:
                    v = buf[:, 1024:1280].rearrange("p (h t) -> p h t", h=4)
                    last = pool.affine_select(out=v, in_=v, compare_op=ALU.is_gt, fill=0.0, base=0,
                                              pattern=[[0, 4], [1, LS]], channel_multiplier=-1)
                last.then_inc(done, 1)

            for u in range(U_ + 1):
                if u < U_:
                    pool.wait_ge(sp_raw, u + 1)
                    mask(u, LB[u % 2], sp_ready)
                if u >= 1:
                    pool.wait_ge(w_raw, u)
                    mask(u - 1, ZSB[(u - 1) % 3], w_ready)
            pool.wait_ge(ysb_ready, 5)
            pool.wait_ge(out_stored, 16 * KV_STORES)
            nc.gpsimd.memset(XC[:, :, T:TS], 0.0).then_inc(pads, 1)
            for s, name in ((0, "conv_prompt"), (1, "conv_sample")):
                pool.wait_ge(tail_rows, s + 1)
                out_dma(pool, O[name][0, 0].rearrange("j (c p) -> (j c) p", p=P), TAILR[0:36, s, :])
            pool.wait_ge(out_stored, 16 * stored[0])
            pool.wait_ge(dve_dt, 7)
            nc.gpsimd.memset(HS[:, 0], 0.0).then_inc(pads, 1)
            for v in range(10):
                c, g = divmod(v, 2)
                if v == 0:
                    pool.wait_ge(xc_ready, CONV_C)
                    pool.wait_ge(vec_ready, 4)
                if v >= 1:
                    pool.wait_ge(t3_done, v)
                nc.gpsimd.tensor_tensor(DX, XC[:, 4 * g:4 * g + 4, c * P:(c + 1) * P],
                                        bc(DP[:, 4 * g:4 * g + 4].unsqueeze(2), [P, 4, P]),
                                        ALU.mult).then_inc(dx_ready, 1)
            for s, name in ((0, "ssm_prompt"), (1, "ssm_sample")):
                pool.wait_ge(so_rows, s + 1)
                out_dma(pool, O[name][0, 0].rearrange("h q n -> (h q) n").rearrange("(b p) n -> p b n", p=P), HO)
            for t in range(4):
                pool.wait_ge(mkv_rows, 4 * (t + 1))
                name = ("mem_k_prompt", "mem_v_prompt")[t // 2]
                dst = O[name][0, 0].rearrange("(m p) h d -> p m (h d)", p=P)[:, :, 512 * (t % 2):512 * (t % 2) + 512]
                out_dma(pool, dst, MKV[:, :, 512 * t:512 * (t + 1)], late_stored)
            moe_pool(pool)

        def mem_out(act, h):
            for dc in range(2):
                act.wait_ge(ot_psum, 2 * h + dc + 1)
                nc.scalar.copy(OT[:, 2 * h + dc, :], bank(4 + 2 * dc, 2)[:, 0:T]).then_inc(ot_ready, 1)
                act.wait_ge(ot_ready, 2 * h + dc + 1)
                act_high(OTH[:, 2 * h + dc, :], OT[:, 2 * h + dc, :])

        def act_ht(i):
            t0, n = CH[i]
            nc.scalar.wait_ge(ht_ready, i + 1)
            act_high(HTH[:, :, t0:t0 + n], HT[:, :, t0:t0 + n])

        @block.scalar
        def _(act):
            act.wait_ge(consts, 6)
            for i, (src, n) in enumerate(srcA):
                act.wait_ge(x_loaded[i] if i < NC_ else mem_loaded[i - NC_], 16)
                norm_stat(i, src, n, SQ)
                if i == 2:
                    split_high(act, 0)
                if i >= 3:
                    act_ht(i - 3)
            act_ht(4)
            split_high(act, 1)
            for i in range(20):
                t, m = divmod(i, 5)
                n = CH[m][1]
                act.wait_ge(kv_psum, i + 1)
                nc.scalar.copy((KR, VR)[t // 2][:n, m, 256 * (t % 2):256 * (t % 2) + 256], bank(4 + i % 4)[:n, 0:256]).then_inc(kv_rows, 1)
                if m == 4:
                    split_high(act, t + 2)
            split_high(act, W_X)
            split_high(act, W_X + 1)
            for b in range(9):
                act.wait_ge(kt_psum, b + 1)
                nc.scalar.copy(KTA[:, :, b * P:(b + 1) * P],
                               bank(4 + b % 4).rearrange("p (h n) -> p h n", h=4)).then_inc(kt_ready, 1)
            for u in range(U_ + 1):
                if u < U_:
                    act.wait_ge(z_copied, u + 1)
                    if u >= 2:
                        act.wait_ge(s_psum, u - 1)
                    lb = LB[u % 2]
                    nc.scalar.activation(lb, ZSB[u % 3], ACT.Abs).then_inc(z_abs, 1)
                    act.wait_ge(z_abs, u + 1)
                    nc.scalar.activation(lb, lb, ACT.Exp, scale=-1.0).then_inc(z_exp, 1)
                    act.wait_ge(z_exp, u + 1)
                    nc.scalar.activation(lb, lb, ACT.Ln, bias=1.0).then_inc(l_ready, 1)
                if u >= 1:
                    act.wait_ge(u_ready, u)
                    nc.scalar.activation(ZSB[(u - 1) % 3], ZSB[(u - 1) % 3], ACT.Exp).then_inc(w_raw, 1)
            act.wait_ge(ysb_ready, 5)
            act.wait_ge(out_stored, 16 * KV_STORES)
            for i in range(CONV_C + 1):
                if i < CONV_C:
                    act.wait_ge(xb_psum, i + 1)
                    if i >= 3:
                        act.wait_ge(conv_done, i - 2)
                    b = bank(2 * (i % 2), 2)
                    h = T // 2
                    nc.scalar.copy(XR[i % 3][:, 3:3 + h], b[:, 0:h])
                    nc.scalar.copy(XR[i % 3][:, 3 + h:515], b[:, 512:512 + LP - h])
                    nc.scalar.copy(XR[i % 3][:, 518:582], b[:, 512 + LP - h:512 + h]).then_inc(xr_ready, 1)
                    if i % 2:
                        split_high(act, W_X + 2 + i // 2)
                if i >= 1:
                    j = i - 1
                    act.wait_ge(conv_done, j + 1)
                    nc.scalar.activation(XC[:, j, 0:LP], CV[j % 2][:, 0:512], ACT.Silu)
                    nc.scalar.activation(XC[:, j, LP:T], CV[j % 2][:, 515:579], ACT.Silu).then_inc(xc_ready, 1)
            for i in range(KD):
                act.wait_ge(zt_psum, i + 1)
                nc.scalar.activation(halves(ZS[:, i, :]), pair(2 * (i % 2)), ACT.Silu).then_inc(zt_ready, 1)
                if i % 2:
                    split_high(act, W_Z + 2 + i // 2)
            act.wait_ge(dve_dt, 1)
            nc.scalar.activation(AD[0:NH, :], UD[0:NH, :], ACT.Abs).then_inc(act_dt, 1)
            act.wait_ge(act_dt, 1)
            nc.scalar.activation(AD[0:NH, :], AD[0:NH, :], ACT.Exp, scale=-1.0).then_inc(act_dt, 1)
            act.wait_ge(act_dt, 2)
            nc.scalar.activation(AD[0:NH, :], AD[0:NH, :], ACT.Ln, bias=1.0).then_inc(act_dt, 1)
            nc.scalar.activation(HCOL[0:NH, 3:4], HCOL[0:NH, 1:2], ACT.Exp).then_inc(act_dt, 1)
            split_high(act, W_M + 1)
            act.wait_ge(dve_dt, 6)
            nc.scalar.activation(ECM[0:NH, :], CUM[0:NH, :], ACT.Exp).then_inc(act_dt, 1)
            act.wait_ge(pre_dve, 4)
            nc.scalar.activation(TE, TE, ACT.Exp).then_inc(pre_act, 1)
            act.wait_ge(pre_psum, 2)
            nc.scalar.activation(CD, bank(7)[:, 160:240].rearrange("p (c h) -> p c h", c=NC_), ACT.Exp).then_inc(pre_act, 1)
            for v in range(10):
                act.wait_ge(ec_psum, v + 1)
                if v >= 1:
                    act.wait_ge(t1_done, v)
                nc.scalar.copy(ECS, bank(5)).then_inc(ec_done, 1)
                act.wait_ge(seg_done, v + 1)
                nc.scalar.activation(SEG[v % 2], SEG[v % 2], ACT.Exp).then_inc(e_ready, 1)
            for i in range(KD):
                act.wait_ge(yz_done, 10)
                if i >= 2:
                    act.wait_ge(ssq_psum, i - 1)
                nc.scalar.activation(SQT[i % 2], ZS[:, i, :], ACT.Square).then_inc(sq_ready, 1)
            act.wait_ge(ssq_psum, KD)
            nc.scalar.activation(RB, bank(0, 2)[:, 0:T], ACT.Ln, scale=1.0 / D, bias=CST[:, 0:1]).then_inc(rb_ln, 1)
            act.wait_ge(rb_ln, 1)
            nc.scalar.activation(RB, RB, ACT.Exp, scale=-0.5).then_inc(rb_ready, 1)
            act.wait_ge(intra_psum, 10)
            act_high(YSBTH, YSBT)
            act.wait_ge(out_stored, 16 * MIX_STORES)
            for i in range(KD):
                act.wait_ge(yn_ready, i + 1)
                act_high(ZSH[:, i, :], ZS[:, i, :])
            for c in range(KD):
                act.wait_ge(gs_psum, c + 1)
                if c >= 2:
                    act.wait_ge(m1_done, c - 1)
                nc.scalar.activation(halves(GS[c % 2]), pair(0), ACT.Sigmoid).then_inc(gs_ready, 1)
                act.wait_ge(gb_psum, c + 1)
                if c >= 2:
                    act.wait_ge(m2_done, c - 1)
                nc.scalar.activation(halves(GB[c % 2]), pair(2), ACT.Sigmoid).then_inc(gb_ready, 1)
                split_high(act, W_M + 2 * c + 2)
                if c < KD - 1:
                    split_high(act, W_M + 2 * c + 3)
                act.wait_ge(mg_ready, c + 1)
                act_high(MGH[:, c, :], MG[:, c, :])
            act_high(MTH, MT)
            for n in range(W_O + 1, W_KV + 2):
                split_high(act, n)
            for t in range(8):
                for m in range(2):
                    act.wait_ge(mkv_psum, 2 * t + m + 1)
                    nc.scalar.copy(MKV[:, m, 256 * t:256 * (t + 1)], bank((2 * t + m) % 4)[:, 0:256]).then_inc(mkv_rows, 1)
                split_high(act, W_KV + 2 + t)
                if t < NC_:
                    n = CH[t][1]
                    act.wait_ge(x1_ready, 3 * NC_ + t + 1)
                    norm_stat(N_G + t, X[:n, t, :], n, SQ)
                if 2 <= t < NC_ + 2:
                    t0, n = CH[t - 2]
                    act.wait_ge(ht_ready, N_G + t - 1)
                    act_high(HTH2[:, :, t0:t0 + n], HT[:, :, t0:t0 + n])
            for i in range(KD):
                act.wait_ge(mq_psum, i + 1)
                nc.scalar.mul(halves(QM[:, i, :]), pair(2 * (i % 2)), MHD ** -0.5).then_inc(mq_ready, 1)
                if i % 2:
                    split_high(act, W_MQ + 2 + i // 2)
            for a in range(20):
                h, m = divmod(a, 5)
                n = CH[m][1]
                act.wait_ge(nm_ready, a + 1)
                if a >= 2:
                    act.wait_ge(pt_psum, a - 1)
                nc.scalar.activation(PX[a % 2][:n, :], bank(a % 2)[:n, 0:ML], ACT.Exp, bias=NM[:n, a:a + 1],
                                     accum_out=RS[:n, a:a + 1]).then_inc(px_ready, 1)
                if m == 1 and h >= 1:
                    mem_out(act, h - 1)
            mem_out(act, MH - 1)
            split_high(act, W_MO + 2)
            split_high(act, W_MO + 3)
            for m, (_, n) in enumerate(CH):
                act.wait_ge(x2_ready, 3 * NC_ + m + 1)
                norm_stat(N_I + m, X[:n, m, :], n, SQ)
            moe_act(act)

        @block.vector
        def _(dve):
            nc.vector.memset(KR[LS:, 4, :], 0.0)
            nc.vector.memset(VR[LS:, 4, :], 0.0)
            nc.vector.memset(r32(HTH_END).bitcast(F32), 0.0)
            nc.vector.memset(r32(HT_END).bitcast(F32), 0.0)
            dve.wait_ge(vec_psum, 1)
            nc.vector.tensor_copy(VT, bank(7)[:, 0:100]).then_inc(vec_ready, 1)
            nc.vector.tensor_copy(CTXT, bank(7)[:, 128:164]).then_inc(vec_ready, 1)
            dve.wait_ge(vec_ready, 2)
            for i in range(len(srcA) + 1):
                if i == 3:
                    split_low(dve, 0)
                if i < len(srcA):
                    src, n = srcA[i]
                    norm_scale(dve, i, src, n, XN[i % 2][:n, :], i >= 2)
                if i >= 1:
                    norm_gain(dve, i - 1, G_MIX if i - 1 < NC_ else G_MKV, srcA[i - 1][1], 0, dstA[i - 1])
                if i >= 3:
                    t0, n = CH[i - 3]
                    act_low(dve, A_HT + i - 2, HT[:, :, t0:t0 + n], HTH[:, :, t0:t0 + n])
            for n in range(1, W_Q + 2):
                split_low(dve, n)
            for i in range(4):
                dve.wait_ge(q_psum, i + 1)
                nc.vector.tensor_scalar(halves(QT[:, i, :]), pair(2 * (i % 2)), HD ** -0.5, None,
                                        ALU.mult).then_inc(q_ready, 1)
                if i % 2:
                    split_low(dve, W_X + i // 2)

            def u_op(u):
                dve.wait_ge(s_psum, u + 1)
                nc.vector.tensor_tensor(ZSB[u % 3], ZSB[u % 3], ps[:, 1536:1536 + 1280], ALU.subtract).then_inc(u_ready, 1)

            def ysb_out(g):
                if g < 4:
                    dve.wait_ge(pv_psum, 2 * (g + 1))
                    nc.vector.tensor_copy(YSBT[:, g, 0:LP], bank(6 + g % 2)).then_inc(ysb_ready, 1)
                else:
                    dve.wait_ge(pv_psum, U_)
                    nc.vector.tensor_copy(YSBT[:, :, LP:T],
                                          bank(6 + g % 2)[:, 0:256].rearrange("p (h t) -> p h t", h=4)).then_inc(ysb_ready, 1)

            for u in range(U_ + 2):
                if u < U_:
                    dve.wait_ge(z_psum, u + 1)
                    if u >= 3:
                        dve.wait_ge(pv_psum, u - 2)
                    nc.vector.tensor_copy(ZSB[u % 3], ps[:, 0:1280]).then_inc(z_copied, 1)
                    dve.wait_ge(l_ready, u + 1)
                    dve.wait_ge(z_copied, u + 1)
                    nc.vector.scalar_tensor_tensor(out=LB[u % 2], in0=ZSB[u % 3], scalar=0.0, in1=LB[u % 2],
                                                   op0=ALU.max, op1=ALU.add).then_inc(sp_raw, 1)
                if 1 <= u <= U_:
                    u_op(u - 1)
                done = u - 2 + 1
                if u >= 2 and done % 2 == 0:
                    ysb_out(done // 2 - 1)

            dve.wait_ge(consts, 6)
            dve.wait_ge(out_stored, 16 * KV_STORES)
            for s in range(3):
                nc.vector.memset(XR[s][:, 0:3], 0.0)
            nc.vector.tensor_copy(SELP[0:NH], bc(IDENT[0:NH, 0:NH].unsqueeze(2), [NH, NH, HD])).then_inc(vec_ready, 1)
            for i in range(CONV_C):
                xr, cv = XR[i % 3], CV[i % 2]
                if i >= 2:
                    dve.wait_ge(xc_ready, i - 1)
                ctxv = CTXT.rearrange("p (j c) -> p j c", j=3)[:, :, i:i + 1]
                nc.vector.tensor_copy(xr[:, 515:518].unsqueeze(2), ctxv).then_inc(conv_step, 1)
                dve.wait_ge(xr_ready, i + 1)
                dve.wait_ge(conv_step, 4 * i + 1)
                nc.vector.tensor_copy(TAIL[:, 0, :, i:i + 1], xr[:, 512:515].unsqueeze(2))
                nc.vector.tensor_copy(TAIL[:, 1, :, i:i + 1], xr[:, 579:582].unsqueeze(2))
                nc.vector.tensor_scalar(cv[:, 0:579], xr[:, 0:579], CW[:, 0, i:i + 1], CB[:, i:i + 1],
                                        ALU.mult, ALU.add).then_inc(conv_step, 1)
                for j in range(1, 4):
                    dve.wait_ge(conv_step, 4 * i + 1 + j)
                    o = nc.vector.scalar_tensor_tensor(out=cv[:, 0:579], in0=xr[:, j:j + 579],
                                                       scalar=CW[:, j, i:i + 1], in1=cv[:, 0:579],
                                                       op0=ALU.mult, op1=ALU.add)
                    o.then_inc(conv_step if j < 3 else conv_done, 1)
                if i % 2:
                    split_low(dve, W_X + 2 + i // 2)
            for n in range(W_Z + 2, W_M + 1):
                split_low(dve, n)
            dve.wait_ge(dp_psum, 1)
            nc.vector.tensor_copy(DP, bank(7)[:, 240:248]).then_inc(vec_ready, 1)
            for s in range(2):
                dve.wait_ge(dp_psum, 3)
                nc.vector.tensor_copy(TAILR[0:36, s, :], bank(6)[0:36, P * s:P * (s + 1)]).then_inc(tail_rows, 1)
            dve.wait_ge(dt_psum, 1)
            nc.vector.tensor_scalar(halves(UD[0:NH, :]), pair(0, NH), HCOL[0:NH, 0:1], None, ALU.add).then_inc(dve_dt, 1)
            nc.vector.memset(DTT[0:NH, T:TS], 0.0)
            nc.vector.memset(RST[0:NH, :], 1.0).then_inc(dve_dt, 1)
            dve.wait_ge(dve_dt, 2)
            nc.vector.memset(RST[0:NH, :].rearrange("p (c t) -> p c t", t=P)[:, :, 0:1], 0.0).then_inc(dve_dt, 1)
            dve.wait_ge(act_dt, 3)
            nc.vector.scalar_tensor_tensor(out=DTT[0:NH, 0:T], in0=UD[0:NH, :], scalar=0.0, in1=AD[0:NH, :],
                                           op0=ALU.max, op1=ALU.add).then_inc(dve_dt, 1)
            dve.wait_ge(act_dt, 4)
            dve.wait_ge(dve_dt, 4)
            nc.vector.tensor_scalar(DTA[0:NH, :], DTT[0:NH, :], HCOL[0:NH, 3:4], -1.0, ALU.mult, ALU.mult).then_inc(dve_dt, 1)
            dve.wait_ge(dve_dt, 5)
            nc.vector.tensor_tensor_scan(CUM[0:NH, :], RST[0:NH, :], DTA[0:NH, :], 0.0, ALU.mult, ALU.add).then_inc(dve_dt, 1)
            dve.wait_ge(dve_dt, 6)
            last_cum = CUM[0:NH, :].rearrange("p (c t) -> p c t", t=P)[:, :, P - 1:P]
            nc.vector.tensor_tensor(DIAG[0:NH], bc(IDENT[0:NH, 0:NH].unsqueeze(1), [NH, NC_, NH]),
                                    bc(last_cum, [NH, NC_, NH]), ALU.mult).then_inc(dve_dt, 1)
            dve.wait_ge(pre_psum, 2)
            p7 = lambda a: bank(7)[:, a:a + 80].rearrange("p (c h) -> p c h", c=NC_)
            nc.vector.tensor_copy(CR, p7(0)).then_inc(pre_dve, 1)
            nc.vector.tensor_copy(DR, p7(80)).then_inc(pre_dve, 1)
            dve.wait_ge(pre_psum, 1)
            dve.wait_ge(pads, 2)
            nc.vector.tensor_copy(HS[:, 1], bank(1, 2).rearrange("p (g n) -> p g n", g=2)).then_inc(pre_dve, 1)
            dve.wait_ge(pre_dve, 3)
            nc.vector.tensor_tensor(TE, p7(160), CR, ALU.subtract).then_inc(pre_dve, 1)
            dve.wait_ge(pre_act, 2)
            nc.vector.tensor_tensor(WRW, DR, TE, ALU.mult).then_inc(pre_dve, 1)
            dve.wait_ge(pre_dve, 5)

            def xdt(v):
                c, g = divmod(v, 2)
                dve.wait_ge(ssd_tr, v + 1)
                if v >= 2:
                    dve.wait_ge(st_psum, v - 1)
                    dve.wait_ge(intra_psum, v - 1)
                nc.vector.tensor_copy(BROW[v % 2], bank(0)[:, 0:P])
                nc.vector.tensor_tensor(CBM[v % 2], bank(0)[:, P:2 * P], TINC, ALU.mult)
                xr = bank(7).rearrange("p (h q) -> p h q", h=8)
                for dst, w in ((XD, DR), (XW, WRW)):
                    last = nc.vector.tensor_tensor(dst[v % 2].rearrange("p (h q) -> p h q", h=8), xr,
                                                   bc(w[:, c, 8 * g:8 * g + 8].unsqueeze(2), [P, 8, HD]), ALU.mult)
                last.then_inc(sx_done, 1)

            def seg(v):
                c, g = divmod(v, 2)
                dve.wait_ge(cumb_psum, v + 1)
                if v >= 2:
                    dve.wait_ge(intra_psum, v - 1)
                b = bank(1, 2).rearrange("p (h t) -> p h t", h=8)
                for h in range(8):
                    last = nc.vector.tensor_scalar(SEG[v % 2][:, h, :], b[:, h, :], CR[:, c, 8 * g + h:8 * g + h + 1],
                                                   0.0, ALU.subtract, ALU.min)
                last.then_inc(seg_done, 1)

            for v in range(10):
                c, g = divmod(v, 2)
                sq = 0 if c < 4 else 1
                if v == 0:
                    xdt(0)
                    seg(0)
                dve.wait_ge(e_ready, v + 1)
                dve.wait_ge(sx_done, v + 1)
                nc.vector.tensor_tensor(SEG[v % 2], SEG[v % 2], bc(CBM[v % 2].unsqueeze(1), [P, 8, P]),
                                        ALU.mult).then_inc(m_ready, 1)
                dve.wait_ge(inter_psum, v + 1)
                dve.wait_ge(ec_done, v + 1)
                if v >= 2:
                    dve.wait_ge(yz_done, v - 1)
                nc.vector.tensor_tensor(T1[v % 2].rearrange("p j t -> p (j t)"), bank(4), ECS,
                                        ALU.mult).then_inc(t1_done, 1)
                hs = HS[:, sq, g, :].rearrange("p (h q) -> p h q", h=8)
                nc.vector.tensor_tensor(hs, hs, bc(CD[:, c, 8 * g:8 * g + 8].unsqueeze(2), [P, 8, HD]),
                                        ALU.mult).then_inc(h_dec, 1)
                dve.wait_ge(st_psum, v + 1)
                dve.wait_ge(h_dec, v + 1)
                nc.vector.tensor_tensor(HS[:, sq, g, :], HS[:, sq, g, :], bank(6), ALU.add).then_inc(h_ready, 1)
                if v < 9:
                    xdt(v + 1)
                    seg(v + 1)
                if v == 0:
                    split_low(dve, W_M + 1)
                dve.wait_ge(intra_psum, v + 1)
                dve.wait_ge(t1_done, v + 1)
                t1 = T1[v % 2]
                nc.vector.tensor_tensor(t1.rearrange("p j t -> p (j t)"), t1.rearrange("p j t -> p (j t)"), bank(3),
                                        ALU.add).then_inc(t2_done, 1)
                dve.wait_ge(t2_done, v + 1)
                dve.wait_ge(dx_ready, v + 1)
                nc.vector.tensor_tensor(t1, t1, DX, ALU.add).then_inc(t3_done, 1)
                dve.wait_ge(t3_done, v + 1)
                n = CH[c][1]
                zv = ZS[:, 4 * g:4 * g + 4, c * P:c * P + n]
                nc.vector.tensor_tensor(zv, zv, t1[:, :, 0:n], ALU.mult).then_inc(yz_done, 1)
            for s in range(2):
                dve.wait_ge(so_psum, s + 1)
                if s:
                    dve.wait_ge(out_stored, 16 * (KV_STORES + 3))
                nc.vector.tensor_copy(HO, bank(1, 2).rearrange("p (b n) -> p b n", b=8)).then_inc(so_rows, 1)
            dve.wait_ge(rb_ready, 1)
            dve.wait_ge(yz_done, 10)
            nc.vector.memset(r32(MG_END).bitcast(F32), 0.0)
            nc.vector.memset(r32(MGH_END).bitcast(F32), 0.0)
            for i in range(KD):
                nc.vector.scalar_tensor_tensor(out=ZS[:, i, :], in0=ZS[:, i, :], scalar=G_SSM[:, i:i + 1], in1=RB,
                                               op0=ALU.mult, op1=ALU.mult).then_inc(yn_ready, 1)
            act_low(dve, A_YSB + 1, YSBT, YSBTH)
            for i in range(KD):
                act_low(dve, A_ZS + i + 1, ZS[:, i, :], ZSH[:, i, :])
            for c in range(KD):
                split_low(dve, W_M + 2 * c + 2)
                dve.wait_ge(br_psum, c + 1)
                dve.wait_ge(gs_ready, c + 1)
                nc.vector.tensor_tensor(halves(M1[c % 2]), pair(4), halves(GS[c % 2]), ALU.mult).then_inc(m1_done, 1)
                dve.wait_ge(sb_psum, c + 1)
                dve.wait_ge(gb_ready, c + 1)
                nc.vector.tensor_tensor(halves(MG[:, c, :]), pair(6), halves(GB[c % 2]), ALU.mult).then_inc(m2_done, 1)
                dve.wait_ge(m1_done, c + 1)
                dve.wait_ge(m2_done, c + 1)
                nc.vector.tensor_tensor(MG[:, c, :], MG[:, c, :], M1[c % 2], ALU.add).then_inc(mg_ready, 1)
                if c < KD - 1:
                    split_low(dve, W_M + 2 * c + 3)
                act_low(dve, A_MG + c + 1, MG[:, c, :], MGH[:, c, :])
            def add_rows(psum, done, split):
                for i in range(4 * NC_):
                    t, m = divmod(i, NC_)
                    n = CH[m][1]
                    if psum is wo_psum and t == 0:
                        dve.wait_ge(x_loaded[m], 32)
                    dve.wait_ge(psum, i + 1)
                    xv = X[:n, m, 256 * t:256 * (t + 1)]
                    nc.vector.tensor_tensor(xv, xv, bank(i % 4)[:n, 0:256], ALU.add).then_inc(done, 1)
                    if m == NC_ - 1 and t < len(split):
                        split_low(dve, split[t])

            act_low(dve, A_MT + 1, MT, MTH)
            split_low(dve, W_O + 1)
            add_rows(wo_psum, x1_ready, [W_O + 2, W_O + 3, W_KV, W_KV + 1])
            for t in range(8):
                split_low(dve, W_KV + 2 + t)
                if t < NC_:
                    n = CH[t][1]
                    norm_scale(dve, N_G + t, X[:n, t, :], n, XN[t % 2][:n, :], t >= 2)
                if 1 <= t < NC_ + 1:
                    t0, n = CH[t - 1]
                    norm_gain(dve, N_G + t - 1, G_MQ, n, 4, HT[:, :, t0:t0 + n])
                if 2 <= t < NC_ + 2:
                    t0, n = CH[t - 2]
                    act_low(dve, A_HT2 + t - 1, HT[:, :, t0:t0 + n], HTH2[:, :, t0:t0 + n])
            dve.wait_ge(out_stored, 16 * MIX_STORES)
            for b in range(4):
                s, m = divmod(b, 2)
                dve.wait_ge(km_psum, b + 1)
                nc.vector.tensor_copy(KM[:, s, :, m * P:(m + 1) * P],
                                      bank(2 * (b % 2), 2).rearrange("p (c n) -> p c n", c=KD)).then_inc(km_ready, 1)
            for n in range(W_MQ + 2, W_MO + 2):
                split_low(dve, n)

            def pt_out(a):
                h, m = divmod(a, 5)
                t0, n = CH[m]
                dve.wait_ge(pt_psum, a + 1)
                if m == 0 and h >= 2:
                    dve.wait_ge(ot_psum, 2 * (h - 1))
                nc.vector.tensor_copy(PT[h % 2][:, :, t0:t0 + n],
                                      bank(2 + a % 2)[:, 0:256].rearrange("p (k n) -> p k n", k=2)[:, :, 0:n]
                                      ).then_inc(pt_ready, 1)

            nc.vector.memset(r32(OT_END).bitcast(F32), 0.0)
            nc.vector.memset(r32(OTH_END).bitcast(F32), 0.0)

            def out_low(h):
                for c in (2 * h, 2 * h + 1):
                    act_low(dve, A_OT + c + 1, OT[:, c, :], OTH[:, c, :])

            for a in range(20):
                n = CH[a % 5][1]
                if a % 5 == 3 and a >= 5:
                    out_low(a // 5 - 1)
                dve.wait_ge(ms_psum, a + 1)
                nc.vector.tensor_reduce(NM[:n, a:a + 1], bank(a % 2)[:n, 0:ML], AX.X, ALU.max, negate=True).then_inc(nm_ready, 1)
                if a >= 1:
                    pt_out(a - 1)
                dve.wait_ge(px_ready, a + 1)
                nc.vector.reciprocal(RR[:n, a:a + 1], RS[:n, a:a + 1]).then_inc(rr_ready, 1)
                dve.wait_ge(rr_ready, a + 1)
                nc.vector.tensor_scalar(PX[a % 2][:n, :], PX[a % 2][:n, :], RR[:n, a:a + 1], None, ALU.mult).then_inc(pn_ready, 1)
            pt_out(19)
            out_low(MH - 1)
            add_rows(mo_psum, x2_ready, [W_MO + 2, W_MO + 3])
            for m in range(NC_ + 1):
                if m < NC_:
                    n = CH[m][1]
                    norm_scale(dve, N_I + m, X[:n, m, :], n, XNR[:n, m, :], False)
                if m >= 1:
                    t0, n = CH[m - 1]
                    norm_gain(dve, N_I + m - 1, G_FFN, n, 4, HT[:, :, t0:t0 + n])
            moe_dve(dve)

        def passes(out, parts):
            for k, ((sh, sl), (mh, ml)) in enumerate(parts):
                for j, (a, b) in enumerate(((sh, mh), (sh, ml), (sl, mh))):
                    last = nc.tensor.matmul(out, a, b, start=(k == 0 and j == 0), stop=(k == len(parts) - 1 and j == 2))
            return last

        def tproj(b, n, c, high, low, nk=KD, k0=0):
            for h in range(2):
                t = slice(h * (T // 2), (h + 1) * (T // 2))
                last = passes(bank(b + h)[:, 0:T // 2], [((w_hi(n)[:, k0 + k, c:c + P], w_lo(n)[:, k0 + k, c:c + P]),
                                     (r32(high[:, k, t]), r32(low[:, k, t]))) for k in range(nk)])
            return last

        def rproj(b, n, m, high, low):
            st = lambda flat, k: r32(flat[:, k * T + m * P:k * T + m * P + P])
            return passes(bank(b)[:, 0:256], [((st(high, k), st(low, k)), (w_hi(n)[:, k, :], w_lo(n)[:, k, :]))
                                              for k in range(KD)])


        @block.tensor
        def _(pe):
            pe.wait_ge(consts, 6)
            pe.wait_ge(vec_loaded, 16 * 11)
            nc.tensor.transpose(bank(7)[:, 0:100], VEC[0:100, :], IDENT[0:100, 0:100])
            nc.tensor.transpose(bank(7)[:, 128:164], CTXR[0:36, :], IDENT[0:36, 0:36]).then_inc(vec_psum, 1)
            for i, (_, n) in enumerate(srcA):
                norm_turn(pe, i, XN[i % 2][:n, :], n, 0)
            pe.wait_ge(vec_ready, 2)
            for i in range(20):
                t, m = divmod(i, 5)
                if m == 0:
                    pe.wait_ge(wl_ready, t + 1)
                if t == 0:
                    pe.wait_ge(al_ready, A_HT + (m + 1 if m < 4 else 5))
                if i >= 4:
                    pe.wait_ge(kv_rows, i - 3)
                rproj(4 + i % 4, W_K + t, m, HTH_F, HT_F).then_inc(kv_psum, 1)
            for i in range(4):
                if i % 2 == 0:
                    pe.wait_ge(wl_ready, W_Q + i // 2 + 1)
                if i < 2:
                    pe.wait_ge(ht_ready, 7)
                else:
                    pe.wait_ge(q_ready, i - 1)
                tproj(2 * (i % 2), W_Q + i // 2, (i % 2) * P, HTH, HT).then_inc(q_psum, 1)
            pe.wait_ge(kv_rows, 20)
            pe.wait_ge(past_loaded, 32)
            for b in range(9):
                if b >= 4:
                    pe.wait_ge(kt_ready, b - 3)
                rows = KR[:, b, :] if b < 4 else PKR[:, b - 4, :] if b < 8 else KR[:, 4, :]
                for h in range(4):
                    last = nc.tensor.transpose(bank(4 + b % 4)[:, h * P:(h + 1) * P], rows[:, h * P:(h + 1) * P], IDENT)
                last.then_inc(kt_psum, 1)

            def scores(u):
                if u == 0:
                    pe.wait_ge(q_ready, 4)
                    pe.wait_ge(kt_ready, 9)
                else:
                    pe.wait_ge(z_copied, u)
                if u < SBH:
                    hp, lo = divmod(u, 2)
                    r = slice(64 * lo, 64 * lo + 64)
                    for kc in range(4):
                        o, n = keycols(u, kc)
                        last = nc.tensor.matmul(ps[:, o:o + n], KTA[r, hp, kc * P:(kc + 1) * P], QT[r, hp, kc * P:LP],
                                                start=True, stop=True)
                else:
                    for kc in range(5):
                        for j in range(4):
                            hp, lo = j, u - SBH
                            r = slice(64 * lo, 64 * lo + 64)
                            o = kc * 256 + j * 64
                            last = nc.tensor.matmul(ps[:, o:o + 64], KTA[r, hp, LP + kc * P:LP + (kc + 1) * P],
                                                    QT[r, hp, LP:T], start=True, stop=True)
                last.then_inc(z_psum, 1)

            def sums(u):
                pe.wait_ge(sp_ready, u + 1)
                if u >= 1:
                    pe.wait_ge(u_ready, u)
                nk = 4 if u < SBH else 5
                for kc in range(nk):
                    o, n = keycols(u, kc)
                    for j in range(kc, nk):
                        oj, nj = keycols(u, j)
                        last = nc.tensor.matmul(ps[:, 1536 + o + n - nj:1536 + o + n], TSUF if j == kc else ONES,
                                                LB[u % 2][:, oj:oj + nj], start=(j == kc), stop=(j == nk - 1))
                last.then_inc(s_psum, 1)

            def values(u):
                pe.wait_ge(w_ready, u + 1)
                g = u // 2
                if g >= 2 and u % 2 == 0:
                    pe.wait_ge(ysb_ready, g - 1)
                w = ZSB[u % 3]
                if u < SBH:
                    r = slice(64 * (u % 2), 64 * (u % 2) + 64)
                    for kc in range(4):
                        o, n = keycols(u, kc)
                        last = nc.tensor.matmul(bank(6 + g % 2)[r, kc * P:LP], VR[:, kc, u * HD:(u + 1) * HD], w[:, o:o + n],
                                                start=(kc == 0), stop=(kc == 3))
                else:
                    for j in range(4):
                        h = 2 * j + u - SBH
                        r = slice(64 * (h % 2), 64 * (h % 2) + 64)
                        for kc in range(5):
                            vv = PVR[:, kc, h * HD:(h + 1) * HD] if kc < 4 else VR[:, 4, h * HD:(h + 1) * HD]
                            last = nc.tensor.matmul(bank(6 + g % 2)[r, j * 64:j * 64 + 64], vv,
                                                    w[:, kc * 256 + j * 64:kc * 256 + j * 64 + 64],
                                                    start=(kc == 0), stop=(kc == 4))
                last.then_inc(pv_psum, 1)

            scores(0)
            for u in range(U_):
                if u + 1 < U_:
                    scores(u + 1)
                sums(u)
                if u >= 1:
                    values(u - 1)
            values(U_ - 1)

            for i in range(CONV_C):
                if i % 2 == 0:
                    pe.wait_ge(wl_ready, W_X + i // 2 + 1)
                if i == 0:
                    pe.wait_ge(z_copied, U_)
                    pe.wait_ge(u_ready, U_)
                if i >= 2:
                    pe.wait_ge(xr_ready, i - 1)
                tproj(2 * (i % 2), W_X + i // 2, (i % 2) * P, HTH, HT).then_inc(xb_psum, 1)
            for i in range(KD):
                if i % 2 == 0:
                    pe.wait_ge(wl_ready, W_Z + i // 2 + 1)
                if i < 2:
                    pe.wait_ge(xr_ready, CONV_C - 1 + i)
                else:
                    pe.wait_ge(zt_ready, i - 1)
                tproj(2 * (i % 2), W_Z + i // 2, (i % 2) * P, HTH, HT).then_inc(zt_psum, 1)
            pe.wait_ge(vec_ready, 3)
            pe.wait_ge(ysb_ready, 5)
            for j in range(8):
                last = nc.tensor.matmul(bank(7)[:, 240 + j:241 + j], SELP[0:NH, 2 * j:2 * j + 2, :].rearrange("p a b -> p (a b)"),
                                        HCOL[0:NH, 2:3], start=True, stop=True)
            last.then_inc(dp_psum, 1)
            pe.wait_ge(conv_done, CONV_C)
            for s in range(2):
                nc.tensor.transpose(bank(6)[0:36, P * s:P * (s + 1)], TAIL[:, s].rearrange("p j c -> p (j c)"),
                                    IDENT).then_inc(dp_psum, 1)
            pe.wait_ge(wl_ready, W_DT + 1)
            pe.wait_ge(zt_ready, 7)
            tproj(0, W_DT, 0, HTH, HT).then_inc(dt_psum, 1)
            pe.wait_ge(state_loaded, 16)
            pe.wait_ge(dve_dt, 1)
            pe.wait_ge(zt_ready, 8)
            for b in range(8):
                last = nc.tensor.transpose(bank(1, 2)[:, b * P:(b + 1) * P], H0R[:, b, :], IDENT)
            last.then_inc(pre_psum, 1)
            pe.wait_ge(dve_dt, 7)
            pe.wait_ge(vec_ready, 4)
            for c in range(NC_):
                nc.tensor.transpose(bank(7)[:, 16 * c:16 * c + 16], CUM[0:NH, c * P:(c + 1) * P], IDENT[0:NH, 0:NH])
                nc.tensor.transpose(bank(7)[:, 80 + 16 * c:96 + 16 * c], DTT[0:NH, c * P:(c + 1) * P], IDENT[0:NH, 0:NH])
            nc.tensor.matmul(bank(7)[:, 160:240], ONES[0:NH, :], DIAG[0:NH].rearrange("p c h -> p (c h)"),
                             start=True, stop=True).then_inc(pre_psum, 1)
            pe.wait_ge(pre_dve, 4)
            pe.wait_ge(pre_act, 2)
            pe.wait_ge(xc_ready, CONV_C)
            pe.wait_ge(act_dt, 5)
            pe.wait_ge(pads, 2)
            pe.wait_ge(tail_rows, 2)
            for v in range(10):
                c, g = divmod(v, 2)
                tk = slice(c * P, (c + 1) * P)
                sq = 0 if c < 4 else 1
                if v >= 1:
                    pe.wait_ge(sx_done, v)
                for j in range(4):
                    nc.tensor.transpose(bank(7)[:, j * P:(j + 1) * P], XC[:, 4 * g + j, tk], IDENT)
                nc.tensor.transpose(bank(0)[:, 0:P], XC[:, 8 + g, tk], IDENT)
                nc.tensor.matmul(bank(0)[:, P:2 * P], XC[:, 8 + g, tk], XC[:, 10 + g, tk], start=True, stop=True).then_inc(ssd_tr, 1)
                if v >= 1:
                    pe.wait_ge(seg_done, v)
                for h in range(8):
                    last = nc.tensor.matmul(bank(1, 2)[:, h * P:(h + 1) * P], bc(IDENT[0:NH, 8 * g + h:8 * g + h + 1], [NH, P]), CUM[0:NH, tk],
                                            start=True, stop=True)
                last.then_inc(cumb_psum, 1)
                if v >= 1:
                    pe.wait_ge(ec_done, v)
                for j in range(4):
                    a = 8 * g + 2 * j
                    last = nc.tensor.matmul(bank(5)[:, j * P:(j + 1) * P], SELP[0:NH, a:a + 2, :].rearrange("p a b -> p (a b)"),
                                            ECM[0:NH, tk], start=True, stop=True)
                last.then_inc(ec_psum, 1)
                if v >= 1:
                    pe.wait_ge(t1_done, v)
                if v >= 2:
                    pe.wait_ge(h_ready, v - 1)
                for j in range(4):
                    last = nc.tensor.matmul(bank(4)[:, j * P:(j + 1) * P], HS[:, sq, g, j * P:(j + 1) * P], XC[:, 10 + g, tk],
                                            start=True, stop=True)
                last.then_inc(inter_psum, 1)
                pe.wait_ge(sx_done, v + 1)
                if v >= 1:
                    pe.wait_ge(h_ready, v)
                nc.tensor.matmul(bank(6), BROW[v % 2], XW[v % 2], start=True, stop=True).then_inc(st_psum, 1)
                pe.wait_ge(m_ready, v + 1)
                if v >= 1:
                    pe.wait_ge(t2_done, v)
                for h in range(8):
                    r = slice(64 * (h % 2), 64 * (h % 2) + 64)
                    last = nc.tensor.matmul(bank(3)[r, (h // 2) * P:(h // 2 + 1) * P], XD[v % 2][:, h * HD:(h + 1) * HD],
                                            SEG[v % 2][:, h, :], start=True, stop=True)
                last.then_inc(intra_psum, 1)
            pe.wait_ge(h_ready, 10)
            for s in range(2):
                if s:
                    pe.wait_ge(so_rows, 1)
                for b in range(8):
                    last = nc.tensor.transpose(bank(1, 2)[:, b * P:(b + 1) * P],
                                               HS[:, s].rearrange("p g n -> p (g n)")[:, b * P:(b + 1) * P], IDENT)
                last.then_inc(so_psum, 1)
            pe.wait_ge(so_rows, 2)
            pe.wait_ge(sx_done, 10)
            for i in range(KD):
                pe.wait_ge(sq_ready, i + 1)
                nc.tensor.matmul(bank(0), ONES, SQT[i % 2][:, 0:LP], start=(i == 0), stop=(i == KD - 1))
                nc.tensor.matmul(bank(1)[:, 0:LS], ONES, SQT[i % 2][:, LP:T], start=(i == 0), stop=(i == KD - 1)).then_inc(ssq_psum, 1)
            for c in range(KD):
                na, nb = W_M + 2 * c, W_M + 2 * c + 1
                pe.wait_ge(wl_ready, na + 1)
                if c == 0:
                    pe.wait_ge(rb_ln, 1)
                    pe.wait_ge(t2_done, 10)
                    pe.wait_ge(h_ready, 10)
                else:
                    pe.wait_ge(gs_ready, c)
                tproj(0, na, 0, HTH, HT).then_inc(gs_psum, 1)
                if c:
                    pe.wait_ge(gb_ready, c)
                tproj(2, na, 0, HTH, HT, k0=KD).then_inc(gb_psum, 1)
                if c:
                    pe.wait_ge(m1_done, c)
                else:
                    pe.wait_ge(al_ready, A_ZS + KD)
                pe.wait_ge(wl_ready, nb + 1)
                tproj(4, nb, 0, ZSH, ZS).then_inc(br_psum, 1)
                if c:
                    pe.wait_ge(m2_done, c)
                tproj(6, nb, 0, YSBTH, YSBT, nk=4, k0=KD).then_inc(sb_psum, 1)
            pe.wait_ge(al_ready, A_MG + KD)
            for i in range(4 * NC_):
                t, m = divmod(i, NC_)
                if m == 0:
                    pe.wait_ge(wl_ready, W_O + t + 1)
                if i >= 4:
                    pe.wait_ge(x1_ready, i - 3)
                rproj(i % 4, W_O + t, m, MGH_F, MG_F).then_inc(wo_psum, 1)
            pe.wait_ge(x1_ready, 4 * NC_)
            pe.wait_ge(al_ready, A_MT + 1)
            for i in range(16):
                t, m = divmod(i, 2)
                if m == 0:
                    pe.wait_ge(wl_ready, W_KV + t + 1)
                if i >= 4:
                    pe.wait_ge(mkv_rows, i - 3)
                n = W_KV + t
                passes(bank(i % 4)[:, 0:256], [((r32(MTH[:, k, m * P:(m + 1) * P]), r32(MT[:, k, m * P:(m + 1) * P])),
                                                (w_hi(n)[:, k, :], w_lo(n)[:, k, :])) for k in range(KD)]).then_inc(mkv_psum, 1)
                if m == 1 and 1 <= t <= NC_:
                    n = CH[t - 1][1]
                    norm_turn(pe, N_G + t - 1, XN[(t - 1) % 2][:n, :], n, 4)
            pe.wait_ge(mkv_rows, 16)
            pe.wait_ge(memc_loaded, 32)
            for b in range(4):
                s, m = divmod(b, 2)
                if b >= 2:
                    pe.wait_ge(km_ready, b - 1)
                src = MKV[:, m, 0:D] if s == 0 else MC[:, 0, m, :]
                for c in range(KD):
                    last = nc.tensor.transpose(bank(2 * (b % 2), 2)[:, c * P:(c + 1) * P], src[:, c * P:(c + 1) * P], IDENT)
                last.then_inc(km_psum, 1)
            pe.wait_ge(al_ready, A_HT2 + NC_)
            for i in range(KD):
                if i % 2 == 0:
                    pe.wait_ge(wl_ready, W_MQ + i // 2 + 1)
                if i < 2:
                    pe.wait_ge(km_ready, 3 + i)
                else:
                    pe.wait_ge(mq_ready, i - 1)
                tproj(2 * (i % 2), W_MQ + i // 2, (i % 2) * P, HTH2, HT).then_inc(mq_psum, 1)
            pe.wait_ge(mq_ready, KD)

            def mscores(a):
                h, m = divmod(a, 5)
                t0, n = CH[m]
                if a >= 2:
                    pe.wait_ge(px_ready, a - 1)
                for j in range(2):
                    last = nc.tensor.matmul(bank(a % 2)[:n, 0:ML], QM[:, 2 * h + j, t0:t0 + n],
                                            KM[:, 0 if m < 4 else 1, 2 * h + j, :], start=(j == 0), stop=(j == 1))
                last.then_inc(ms_psum, 1)

            def mvalues(h):
                pe.wait_ge(pt_ready, 5 * (h + 1))
                for dc in range(2):
                    if h >= 1:
                        pe.wait_ge(ot_ready, 2 * (h - 1) + dc + 1)
                    f = h * MHD + dc * P
                    for kc in range(2):
                        nc.tensor.matmul(bank(4 + 2 * dc), MKV[:, kc, D + f:D + f + P], PT[h % 2][:, kc, 0:LP],
                                         start=(kc == 0), stop=(kc == 1))
                    for kc in range(2):
                        last = nc.tensor.matmul(bank(5 + 2 * dc)[:, 0:LS], MC[:, 1, kc, f:f + P], PT[h % 2][:, kc, LP:T],
                                                start=(kc == 0), stop=(kc == 1))
                    last.then_inc(ot_psum, 1)

            mscores(0)
            for a in range(20):
                if a + 1 < 20:
                    mscores(a + 1)
                n = CH[a % 5][1]
                pe.wait_ge(pn_ready, a + 1)
                if a >= 2:
                    pe.wait_ge(pt_ready, a - 1)
                for kc in range(2):
                    last = nc.tensor.transpose(bank(2 + a % 2)[:, kc * P:kc * P + n], PX[a % 2][:n, kc * P:(kc + 1) * P],
                                               IDENT[:n, :n])
                last.then_inc(pt_psum, 1)
                if a % 5 == 0 and a >= 5:
                    mvalues(a // 5 - 1)
            mvalues(MH - 1)
            pe.wait_ge(al_ready, A_OT + KD)
            pe.wait_ge(px_ready, 20)
            pe.wait_ge(pt_ready, 20)
            for i in range(4 * NC_):
                t, m = divmod(i, NC_)
                if m == 0:
                    pe.wait_ge(wl_ready, W_MO + t + 1)
                if i >= 4:
                    pe.wait_ge(x2_ready, i - 3)
                rproj(i % 4, W_MO + t, m, OTH_F, OT_F).then_inc(mo_psum, 1)
            for i, (_, n) in enumerate(CH):
                norm_turn(pe, N_I + i, XNR[:n, i, :], n, 4)
            moe_pe(pe)


_INS = ["x_prompt", "x_sample", "cache_sb_k", "cache_sb_v", "state_ssm", "state_conv", "cache_mem_k", "cache_mem_v",
        "mem_prompt", "norm_mix", "w_in", "conv_w", "conv_b", "dt_bias", "a_log", "d_skip", "ssm_norm", "w_ssm_br",
        "w_sb_br", "w_out", "norm_mem_q", "norm_mem_kv", "w_mem_q", "w_mem_kv", "w_mem_o", "norm_ffn",
        "w_group_router", "w_expert_router", "w_gate_e", "w_up_e", "w_down_e", "norm_final"]
_OUTS = [("y_prompt", (1, LP, D)), ("y_sample", (1, LS, D)),
         ("sb_k_prompt", (1, 1, LP, SBH, 64)), ("sb_v_prompt", (1, 1, LP, SBH, 64)),
         ("ssm_prompt", (1, 1, NH, HD, NS)), ("conv_prompt", (1, 1, 3, CONV_C * P)),
         ("mem_k_prompt", (1, 1, ML, MH, MHD)), ("mem_v_prompt", (1, 1, ML, MH, MHD)),
         ("sb_k_sample", (1, 1, LS, SBH, 64)), ("sb_v_sample", (1, 1, LS, SBH, 64)),
         ("ssm_sample", (1, 1, NH, HD, NS)), ("conv_sample", (1, 1, 3, CONV_C * P))]


def kernel(**inputs):
    import concourse.bacc as bacc
    from concourse.bass_utils import run_bass_kernel_spmd

    nc = bacc.Bacc("TRN2", target_bir_lowering=False, num_devices=1)
    arrays, ins = {}, {}
    for name in _INS:
        a = np.ascontiguousarray(inputs[name])
        arrays["in_" + name] = a
        ins[name] = nc.dram_tensor("in_" + name, a.shape, mybir.dt.from_np(a.dtype), kind="ExternalInput").ap()
    outs = {name: nc.dram_tensor("out_" + name, shape, F32, kind="ExternalOutput").ap() for name, shape in _OUTS}
    encoder_step(nc, ins, outs)
    r = run_bass_kernel_spmd(nc, [arrays], core_ids=[0])
    return tuple(r.results[0]["out_" + name] for name, _ in _OUTS)
```

```python
from contextlib import ExitStack

import numpy as np
import concourse.bass as bass
from concourse import mybir

F32 = mybir.dt.float32
F32R = mybir.dt.float32r
U32 = mybir.dt.uint32
BF16 = mybir.dt.bfloat16
ACT = mybir.ActivationFunctionType
ALU = mybir.AluOpType
AX = mybir.AxisListType

P = 128
D = 1024
KD = D // P
LP, LS = 512, 64
T = LP + LS
CH = [(0, 128), (128, 128), (256, 128), (384, 128), (512, 64)]
NC_ = len(CH)
PAST = 512
NH, HD, NS = 16, 64, 128
SBH = 8
MH, MHD, ML = 4, 256, 256
NE, FF, TOPG, EPG = 16, 512, 4, 4
CONV_C = 12
EPS = 1e-6
TS = NC_ * P
CAP = NC_ * P
BIG = 1.0e30
C_Z, C_X, C_DT, C_Q, C_K, C_V, C_GS, C_GB = 0, 1024, 2560, 2576, 3088, 3600, 4112, 5136
NRAW, NHI = 4, 2
WT = 2048
NMRAW, NMHI = 8, 4
NXG = 4


class Arena:

    def __init__(self, nc, words):
        self.nc, self.words, self.at, self.count = nc, words, 0, 0
        self.base = -(-nc.sbuf_base // 32) * 32
        self.offset, self.twin = {}, {}

    def mark(self):
        return self.at

    def back(self, at):
        self.at = at

    def flat(self, n, dtype=F32):
        n += -n % 8
        self.count += 1
        t = self.nc.alloc_sbuf_tensor_at(f"buf{self.count}", [P, n * (1 if dtype is F32 else 2)], dtype,
                                         offset=self.base + 4 * self.at)
        self.offset[t.name] = (self.base + 4 * self.at, n)
        self.at += n
        assert self.at <= self.words, (self.at, self.words)
        return t

    def view(self, *shape):
        return shaped(self.flat(int(np.prod(shape))), shape)

    def half(self, *shape):
        return shaped(self.flat((int(np.prod(shape)) + 1) // 2, BF16), shape)

    def guarded(self, *shape):
        n = int(np.prod(shape))
        t = self.flat(n + 64)
        return shaped(t, shape), t[:, 0:n + 64], t[:, n:n + 64]

    def rounded(self, ap):
        name = ap.tensor.name
        if name not in self.twin:
            offset, n = self.offset[name]
            self.twin[name] = self.nc.alloc_sbuf_tensor_at(name + "_r", [P, n], F32R, offset=offset)
        return bass.AP(tensor=self.twin[name], offset=ap.offset, ap=ap.ap)


def shaped(t, shape):
    a = t[:, 0:int(np.prod(shape))]
    if len(shape) == 1:
        return a
    names = "abcd"[:len(shape)]
    return a.rearrange("p (%s) -> p %s" % (" ".join(names), " ".join(names)),
                       **{c: s for c, s in zip(names[:-1], shape[:-1])})


def bc(ap, shape):
    return ap.to_broadcast(list(shape))


def encoder_step(nc, I, O):
    ctx = ExitStack()
    with ctx:
        sem_names = []

        def sem(name):
            assert name not in sem_names
            sem_names.append(name)
            return ctx.enter_context(nc.semaphore(name))

        WORDS = 53200
        A = Arena(nc, WORDS)
        r32 = A.rounded
        ps = ctx.enter_context(nc.psum_tensor("ps", [P, 8 * 512], F32))
        bank = lambda b, n=1: ps[:, b * 512:(b + n) * 512]

        def pair(b, np_=P):
            return bank(b, 2)[:np_].rearrange("p (h n) -> p h n", h=2)[:, :, 0:T // 2]

        def halves(ap):
            return ap.rearrange("p (h n) -> p h n", h=2)

        hn_rows = nc.dram_tensor("hn_rows", [T, D], F32, kind="Internal").ap()
        y_rows = nc.dram_tensor("y_rows", [NE * CAP, D], F32, kind="Internal").ap()

        X = A.view(NC_, D)
        A.back(0)
        HTH, HTH_F, HTH_END = A.guarded(KD, T)
        A.back(NC_ * D)
        HT, HT_F, HT_END = A.guarded(KD, T)
        IDENT = A.view(P)
        TSUF = A.view(P)
        TINC = A.view(P)
        TSTR = A.view(P)
        ONES = A.view(P)
        VT = A.view(100)
        CTXT = A.view(36)
        SS = A.view(24)
        RL = A.view(24)
        RI = A.view(24)
        DP = A.view(8)
        CST = A.view(4)
        HCOL = A.view(4)
        G_MIX, G_MKV, G_SSM, G_MQ, G_FFN = (VT[:, 8 * i:8 * i + 8] for i in range(5))
        CB = VT[:, 40:52]
        CW = VT[:, 52:100].rearrange("p (j c) -> p j c", j=4)
        WR = A.view(KD, 20)
        ring = A.mark()
        RAW = [A.view(WT) for _ in range(NRAW)]
        HI = [A.view(WT) for _ in range(NHI)]
        A.back(ring)
        MSLOT = [A.view(WT) for _ in range(6)]
        A.back(ring)
        OSLOT = [A.view(2 * WT) for _ in range(3)]
        base = A.mark()

        XN = [A.view(D) for _ in range(2)]
        SQ = A.view(D)
        MT = A.view(KD, ML)
        YSBT = A.view(4, T)
        mix = A.mark()

        VEC = A.view(P)
        CTXR = A.view(P)
        KR = A.view(NC_, 512)
        VR = A.view(NC_, 512)
        PVR = A.view(4, 512)
        QT = A.view(4, T)
        KTA = A.view(4, 9 * P)
        att = A.mark()
        XS = A.view(NC_, D)
        MR = A.view(2, D)
        A.back(att + NC_ * D)
        PKR = A.view(4, 512)
        A.back(att)
        ZSB = [A.view(1280) for _ in range(3)]
        LB = [A.view(1280) for _ in range(2)]
        A.back(mix)

        XC = A.view(CONV_C, TS)
        ZS = A.view(KD, T)
        ssd = A.mark()
        XR = [A.view(584) for _ in range(3)]
        CV = [A.view(580) for _ in range(2)]
        UD, AD = A.view(T), A.view(T)
        TAIL = A.view(2, 3, CONV_C)
        TAILR = A.view(2, P)
        DTA, RST = A.view(TS), A.view(TS)
        ssd2 = A.mark()
        A.back(ssd)
        SEG = [A.view(8, P) for _ in range(2)]
        T1 = [A.view(4, P) for _ in range(2)]
        DX = A.view(4, P)
        assert A.at <= ssd + 3 * 584 + 2 * 580 + 2 * T
        HS = A.view(2, 2, 512)
        assert A.at <= ssd2
        A.back(ssd2)
        DTT, CUM, ECM = (A.view(TS) for _ in range(3))
        SELP = A.view(NH, HD)
        DIAG = A.view(NC_, NH)
        CR, DR, TE, CD, WRW = (A.view(NC_, NH) for _ in range(5))
        H0R = HO = A.view(8, P)
        A.back(base)
        XD = [A.view(512) for _ in range(2)]
        XW = [A.view(512) for _ in range(2)]
        BROW = [A.view(P) for _ in range(2)]
        CBM = [A.view(P) for _ in range(2)]
        ECS = A.view(512)
        assert A.at <= base + 3 * D
        A.back(mix)

        MG, MG_F, MG_END = A.guarded(KD, T)
        GS = [A.view(T) for _ in range(2)]
        GB = [A.view(T) for _ in range(2)]
        assert A.at <= mix + CONV_C * TS
        A.back(mix)
        RB = A.view(T)
        SQT = [A.view(T) for _ in range(2)]
        A.back(ssd)
        MGH, MGH_F, MGH_END = A.guarded(KD, T)
        ZSH = A.view(KD, T)
        M1 = [A.view(T)]
        A.back(base)
        YSBTH = A.view(4, T)
        M1.append(A.view(T))
        A.back(mix)

        A.back(mix - 4 * T)
        OT, OT_F, OT_END = A.guarded(KD, T)
        HTH2 = OT
        QM, OTH_F, OTH_END = A.guarded(KD, T)
        OTH = QM
        MKV = A.view(2, 2 * D)
        MC = A.view(2, 2, D)
        late = A.mark()
        KM = A.view(2, KD, ML)
        MTH = A.view(KD, ML)
        A.back(late + 2 * KD * ML)
        PX = [A.view(ML) for _ in range(2)]
        PT = [A.view(2, T) for _ in range(2)]
        NM = A.view(20)
        RS = A.view(20)
        RR = A.view(20)
        A.back(late)
        XNR = A.view(NC_, D)

        A.back(base)
        MSLOT += [A.view(WT) for _ in range(NMRAW + NMHI - 6)]
        XG = [A.view(D) for _ in range(NXG)]
        GT = [A.view(KD, P) for _ in range(2)]
        GTH = [A.view(KD, P) for _ in range(2)]
        HET = [A.view(4, P) for _ in range(2)]
        IOTA = A.half(P)
        ECAP = A.view(NE)
        W4 = A.view(4)
        TW = A.half(NC_, NE, 5)
        LG = A.view(NC_, 20)
        MX, SM, PSEL, MA, MB, EX, DEN, GA, GB_, RF = (A.view(NC_) for _ in range(10))
        E4, EQ, OHG, LSEL, OH1, L2, OH2 = (A.view(NC_, 4) for _ in range(7))
        TSTR_B, ONES_B = A.half(P), A.half(P)
        MK = A.half(NC_, NE)
        assert A.at <= late
        A.back(late)
        A.view(NC_, D)
        YO = [A.view(D) for _ in range(2)]
        S1, S2 = A.view(NC_, NE), A.view(NC_, NE)
        A.back(late)
        NF = A.view(D)
        GM = [A.half(NC_, P) for _ in range(2)]
        POSB = A.half(NC_, NE)
        SG, HE = A.view(FF), A.view(FF)
        HETH = [A.view(4, P) for _ in range(2)]
        CNT = A.view(NE)
        TMP, TMP2, DW, POSP, POSM = (A.view(NC_, NE) for _ in range(5))
        R1F, R2F = A.view(NC_), A.view(NC_)
        R12 = A.view(2, NC_)
        GATE = A.view(NE)
        GATE2 = A.view(NE)
        IDX = A.view(NE)
        FLAG = A.view(2)
        PC = A.view(NC_)
        TWO = A.half(NC_, 5)
        SLOTO = A.view(5)
        GATEO = A.view(2)
        IDXO = A.view(1)
        assert A.at <= late + NC_ * D
        x_loaded = [sem(f"x_loaded{i}") for i in range(NC_)]
        mem_loaded = [sem(f"mem_loaded{i}") for i in range(2)]
        vec_loaded = sem("vec_loaded")
        past_loaded = sem("past_loaded")
        ring_loaded = [sem(f"ring_loaded{i}") for i in range(NRAW)]
        wh_ready, wl_ready = sem("wh_ready"), sem("wl_ready")
        ah_ready, al_ready = sem("ah_ready"), sem("al_ready")
        state_loaded = sem("state_loaded")
        memc_loaded = sem("memc_loaded")
        out_stored = sem("out_stored")
        late_stored = sem("late_stored")
        const0 = sem("const0")
        consts = sem("consts")
        vec_psum = sem("vec_psum")
        vec_ready = sem("vec_ready")
        dp_psum = sem("dp_psum")
        ss_ready, rl_ready, ri_ready, xn_ready, tp_psum, ht_ready = (
            sem(n) for n in ("ss_ready", "rl_ready", "ri_ready", "xn_ready", "tp_psum", "ht_ready"))
        N_A, N_G, N_I, N_F = 0, 7, 12, 17
        kv_psum, kv_rows = sem("kv_psum"), sem("kv_rows")
        q_psum, q_ready = sem("q_psum"), sem("q_ready")
        kt_psum, kt_ready = sem("kt_psum"), sem("kt_ready")
        z_psum, z_abs, z_copied, z_exp, l_ready = (sem(n) for n in ("z_psum", "z_abs", "z_copied", "z_exp", "l_ready"))
        sp_raw, sp_ready, s_psum, u_ready, w_raw, w_ready, pv_psum, ysb_ready = (
            sem(n) for n in ("sp_raw", "sp_ready", "s_psum", "u_ready", "w_raw", "w_ready", "pv_psum", "ysb_ready"))

        def cols(w, c0, n):
            return w.rearrange("(k p) n -> p k n", p=P)[:, :, c0:c0 + n]

        w_in = I["w_in"][0]
        tiles = []

        def add_tiles(w, c0, n, width=256):
            first = len(tiles)
            for c in range(0, n, width):
                tiles.append(([(0, cols(w, c0 + c, width))], width))
            return first

        W_K = add_tiles(w_in, C_K, 512)
        W_V = add_tiles(w_in, C_V, 512)
        W_Q = add_tiles(w_in, C_Q, 512)
        W_X = add_tiles(w_in, C_X, CONV_C * P)
        W_Z = add_tiles(w_in, C_Z, D)
        W_DT = add_tiles(w_in, C_DT, P, P)
        W_M = len(tiles)
        for c in range(0, D, P):
            tiles.append(([(0, cols(w_in, C_GS + c, P)), (8, cols(w_in, C_GB + c, P))], P))
            tiles.append(([(0, cols(I["w_ssm_br"][0], c, P)), (8, cols(I["w_sb_br"][0], c, P))], P))
        W_O = add_tiles(I["w_out"][0], 0, D)
        W_KV = add_tiles(I["w_mem_kv"][0], 0, 2 * D)
        W_MQ = add_tiles(I["w_mem_q"][0], 0, D)
        W_MO = add_tiles(I["w_mem_o"][0], 0, D)
        landed, tot = [], [0] * NRAW
        for n, (parts, _) in enumerate(tiles):
            tot[n % NRAW] += 16 * len(parts)
            landed.append(tot[n % NRAW])

        def tile_words(n):
            parts, width = tiles[n]
            return width * sum(src.shape[1] for _, src in parts)

        def tile_view(buf, n):
            return buf[:, 0:tile_words(n)].rearrange("p (k n) -> p k n", n=tiles[n][1])

        def w_hi(n):
            return r32(tile_view(HI[n % NHI], n))

        def w_lo(n):
            return r32(tile_view(RAW[n % NRAW], n))

        def split_high(act, n):
            if n >= NHI:
                act.wait_ge(*retire[n - NHI])
            act.wait_ge(ring_loaded[n % NRAW], landed[n])
            nc.scalar.copy(w_hi(n), tile_view(RAW[n % NRAW], n)).then_inc(wh_ready, 1)

        def split_low(dve, n):
            dve.wait_ge(wh_ready, n + 1)
            raw = tile_view(RAW[n % NRAW], n)
            nc.vector.tensor_tensor(r32(raw), raw, w_hi(n), ALU.subtract).then_inc(wl_ready, 1)

        A_HT, A_YSB, A_ZS, A_MG, A_MT, A_HT2, A_OT = 0, 5, 6, 14, 22, 23, 28

        def act_high(hi, src):
            nc.scalar.copy(r32(hi), src).then_inc(ah_ready, 1)

        def act_low(dve, count, src, hi):
            dve.wait_ge(ah_ready, count)
            nc.vector.tensor_tensor(r32(src), src, r32(hi), ALU.subtract).then_inc(al_ready, 1)

        xb_psum, xr_ready, conv_done, xc_ready = (sem(n) for n in ("xb_psum", "xr_ready", "conv_done", "xc_ready"))
        zt_psum, zt_ready = sem("zt_psum"), sem("zt_ready")
        dt_psum = sem("dt_psum")
        dve_dt, act_dt = sem("dve_dt"), sem("act_dt")
        pads = sem("pads")
        tail_rows = sem("tail_rows")
        pre_psum, pre_dve, pre_act = sem("pre_psum"), sem("pre_dve"), sem("pre_act")
        (ssd_tr, sx_done, cumb_psum, seg_done, e_ready, m_ready, ec_psum, ec_done, inter_psum, t1_done,
         intra_psum, t2_done, st_psum, h_dec, h_ready, dx_ready, t3_done, yz_done) = (
            sem(n) for n in ("ssd_tr", "sx_done", "cumb_psum", "seg_done", "e_ready", "m_ready", "ec_psum",
                             "ec_done", "inter_psum", "t1_done", "intra_psum", "t2_done", "st_psum", "h_dec",
                             "h_ready", "dx_ready", "t3_done", "yz_done"))
        so_psum, so_rows = sem("so_psum"), sem("so_rows")
        sq_ready, ssq_psum, rb_ln, rb_ready, yn_ready = (
            sem(n) for n in ("sq_ready", "ssq_psum", "rb_ln", "rb_ready", "yn_ready"))
        (gs_psum, gb_psum, br_psum, sb_psum, gs_ready, gb_ready, m1_done, m2_done, mg_ready) = (
            sem(n) for n in ("gs_psum", "gb_psum", "br_psum", "sb_psum", "gs_ready", "gb_ready", "m1_done",
                             "m2_done", "mg_ready"))
        wo_psum, x1_ready = sem("wo_psum"), sem("x1_ready")
        mkv_psum, mkv_rows, km_psum, km_ready = (sem(n) for n in ("mkv_psum", "mkv_rows", "km_psum", "km_ready"))
        mq_psum, mq_ready = sem("mq_psum"), sem("mq_ready")
        (ms_psum, nm_ready, px_ready, rr_ready, pn_ready, pt_psum, pt_ready, ot_psum, ot_ready) = (
            sem(n) for n in ("ms_psum", "nm_ready", "px_ready", "rr_ready", "pn_ready", "pt_psum", "pt_ready",
                             "ot_psum", "ot_ready"))
        mo_psum, x2_ready = sem("mo_psum"), sem("x2_ready")

        retire = {}
        for first, count, psum, groups in ((W_K, 4, kv_psum, NC_), (W_Q, 2, q_psum, 2), (W_X, 6, xb_psum, 2),
                                           (W_Z, 4, zt_psum, 2), (W_DT, 1, dt_psum, 1), (W_O, 4, wo_psum, NC_),
                                           (W_KV, 8, mkv_psum, 2), (W_MQ, 4, mq_psum, 2), (W_MO, 4, mo_psum, NC_)):
            for j in range(count):
                retire[first + j] = (psum, groups * (j + 1))
        for c in range(KD):
            retire[W_M + 2 * c] = (gb_psum, c + 1)
            retire[W_M + 2 * c + 1] = (sb_psum, c + 1)

        conv_step = sem("conv_step")
        wr_loaded, hn_stored = sem("wr_loaded"), sem("hn_stored")
        lg_psum, route, route_exp, pos_psum, g_ready, g_psum = (
            sem(n) for n in ("lg_psum", "route", "route_exp", "pos_psum", "g_ready", "g_psum"))
        route_const, idx_ready, nf_loaded = sem("route_const"), sem("idx_ready"), sem("nf_loaded")
        mring_loaded = [sem(f"mring_loaded{i}") for i in range(NMRAW)]
        xg_loaded = [sem(f"xg_loaded{i}") for i in range(NXG)]
        y_stored = [sem(f"y_stored{i}") for i in range(2)]
        (gt_psum, gt_ready, ew_used, sg_ready, he_ready, het_psum, het_ready, yo_ready) = (
            sem(n) for n in ("gt_psum", "gt_ready", "ew_used", "sg_ready", "he_ready", "het_psum", "het_ready",
                             "yo_ready"))
        fin_loaded = [sem(f"fin_loaded{i}") for i in range(2)]
        y1_sum, x3_ready, fin_ready = (sem(n) for n in ("y1_sum", "x3_ready", "fin_ready"))
        KV_STORES = 4
        MIX_STORES = 8
        stored = [0]

        U_ = 10
        OFF = [0, 512, 1024, 896]

        def keycols(u, kc):
            if u < SBH:
                return OFF[kc], LP - kc * P
            return kc * 256, 256

        def out_dma(eng, dst, src, done=out_stored):
            eng.dma_start(dst, src).then_inc(done, 16)
            if done is out_stored:
                stored[0] += 1

        def norm_stat(i, src, n, scratch):
            sl = slice(i, i + 1)
            nc.scalar.activation(scratch[:n, :], src, ACT.Square, accum_out=SS[:n, sl]).then_inc(ss_ready, 1)
            nc.scalar.wait_ge(ss_ready, i + 1)
            nc.scalar.activation(RL[:n, sl], SS[:n, sl], ACT.Ln, scale=1.0 / D, bias=CST[:n, 0:1]).then_inc(rl_ready, 1)
            nc.scalar.wait_ge(rl_ready, i + 1)
            nc.scalar.activation(RI[:n, sl], RL[:n, sl], ACT.Exp, scale=-0.5).then_inc(ri_ready, 1)

        def norm_scale(dve, i, src, n, dst, reused):
            dve.wait_ge(ri_ready, i + 1)
            if reused:
                dve.wait_ge(tp_psum, i - 1)
            nc.vector.tensor_scalar(dst, src, RI[:n, i:i + 1], None, ALU.mult).then_inc(xn_ready, 1)

        def norm_banks(i, b0):
            return bank(b0 + 2 * (i % 2), 2).rearrange("p (c n) -> p c n", c=KD)

        def norm_turn(pe, i, src, n, b0):
            pe.wait_ge(xn_ready, i + 1)
            if i >= 2:
                pe.wait_ge(ht_ready, i - 1)
            for c in range(KD):
                last = nc.tensor.transpose(norm_banks(i, b0)[:, c, 0:n], src[:, c * P:(c + 1) * P], IDENT[:n, :n])
            last.then_inc(tp_psum, 1)

        def norm_gain(dve, i, gain, n, b0, dst):
            dve.wait_ge(tp_psum, i + 1)
            nc.vector.tensor_tensor(dst, norm_banks(i, b0)[:, :, 0:n], bc(gain.unsqueeze(2), [P, KD, n]),
                                    ALU.mult).then_inc(ht_ready, 1)

        srcA = [(XS[:n, m, :], n) for m, (_, n) in enumerate(CH)] + [(MR[:, m, :], P) for m in range(2)]
        dstA = [HT[:, :, t0:t0 + n] for t0, n in CH] + [MT[:, :, m * P:(m + 1) * P] for m in range(2)]

        def rstep(dve, n, ins):
            ins.then_inc(route, 1)
            dve.wait_ge(route, n)

        def route_dve(dve):
            k = [0]

            def go(ins):
                k[0] += 1
                rstep(dve, k[0], ins)

            v = nc.vector
            b3 = lambda a: bc(a.unsqueeze(2), [P, NC_, 4])
            g4 = lambda a: a.rearrange("p c (g k) -> p c g k", g=4)
            dve.wait_ge(mo_psum, 1)
            go(v.memset(LG, 0.0))
            go(v.tensor_copy(TSTR_B, TSTR))
            go(v.tensor_copy(ONES_B, ONES))
            dve.wait_ge(lg_psum, 1)
            go(v.tensor_copy(LG[:, 0:4, :], bank(0)[:, 0:128].rearrange("p (c n) -> p c n", c=4)[:, :, 0:20]))
            go(v.tensor_copy(LG[:LS, 4, :], bank(0)[:LS, 128:148]))
            lgg = LG[:, :, 0:4]
            dve.wait_ge(route_const, 4)
            go(v.tensor_reduce(MX, lgg, AX.X, ALU.max))
            go(v.tensor_tensor(E4, lgg, b3(MX), ALU.subtract))
            assert k[0] == route_group
            go(v.tensor_tensor(EQ, lgg, b3(MX), ALU.is_equal))

            def first_largest(eq, oh):
                go(v.tensor_tensor(eq, eq, bc(W4.unsqueeze(1), [P, NC_, 4]), ALU.mult))
                go(v.tensor_reduce(RF, eq, AX.X, ALU.max))
                go(v.tensor_tensor(oh, eq, b3(RF), ALU.is_equal))

            first_largest(EQ, OHG)
            le = LG[:, :, 4:20]
            for g in range(4):
                if g == 0:
                    go(v.tensor_tensor(LSEL, le[:, :, 0:4], bc(OHG[:, :, 0:1], [P, NC_, 4]), ALU.mult))
                else:
                    go(v.tensor_tensor(OH2, le[:, :, 4 * g:4 * g + 4], bc(OHG[:, :, g:g + 1], [P, NC_, 4]), ALU.mult))
                    go(v.tensor_tensor(LSEL, LSEL, OH2, ALU.add))
            go(v.tensor_reduce(MA, LSEL, AX.X, ALU.max))
            go(v.tensor_tensor(EQ, LSEL, b3(MA), ALU.is_equal))
            first_largest(EQ, OH1)
            go(v.scalar_tensor_tensor(out=L2, in0=OH1, scalar=-BIG, in1=LSEL, op0=ALU.mult, op1=ALU.add))
            go(v.tensor_reduce(MB, L2, AX.X, ALU.max))
            go(v.tensor_tensor(EQ, L2, b3(MB), ALU.is_equal))
            first_largest(EQ, OH2)
            go(v.tensor_tensor(EX, MB, MA, ALU.subtract))
            assert k[0] == route_diff
            for s_, oh in ((S1, OH1), (S2, OH2)):
                for g in range(4):
                    go(v.tensor_tensor(s_[:, :, 4 * g:4 * g + 4], oh, bc(OHG[:, :, g:g + 1], [P, NC_, 4]), ALU.mult))
                go(v.memset(s_[LS:, 4, :], 0.0))
            go(v.tensor_tensor(MK, S1, S2, ALU.add))
            route_steps["mask"] = k[0]
            dve.wait_ge(route_exp, 2)
            dve.wait_ge(hn_stored, 16 * NC_)
            dve.wait_ge(tp_psum, N_I + NC_)
            go(v.tensor_reduce(SM, E4, AX.X, ALU.add))
            go(v.reciprocal(PSEL, SM))
            go(v.tensor_scalar(DEN, EX, 1.0, None, ALU.add))
            go(v.reciprocal(GA, DEN))
            go(v.tensor_tensor(GA, GA, PSEL, ALU.mult))
            go(v.tensor_tensor(GB_, GA, EX, ALU.mult))
            b16 = lambda a: bc(a.unsqueeze(2), [P, NC_, NE])
            go(v.tensor_tensor(DW, S1, b16(GA), ALU.mult))
            go(v.tensor_tensor(TMP, S2, b16(GB_), ALU.mult))
            go(v.tensor_tensor(DW, DW, TMP, ALU.add))
            go(v.tensor_copy(TW[:, :, :, 2], DW))
            go(v.tensor_tensor(DW, DW, TW[:, :, :, 2], ALU.subtract))
            go(v.tensor_copy(TW[:, :, :, 3], DW))
            go(v.tensor_tensor(TW[:, :, :, 4], DW, TW[:, :, :, 3], ALU.subtract))
            dve.wait_ge(pos_psum, 1)
            go(v.tensor_copy(POSP, bank(1)[:, 0:80].rearrange("p (c e) -> p c e", c=NC_)))
            go(v.tensor_copy(CNT, bank(1)[:, 80:96]))
            go(v.scalar_tensor_tensor(out=POSM, in0=POSP, scalar=1.0, in1=MK, op0=ALU.add, op1=ALU.mult))
            go(v.tensor_scalar(POSM, POSM, -1.0, None, ALU.add))
            go(v.tensor_scalar(POSB, POSM, float(P), None, ALU.min))
            for e in range(NE):
                if e >= 2:
                    dve.wait_ge(g_psum, e - 1)
                nc.vector.tensor_tensor(GM[e % 2], bc(IOTA.unsqueeze(1), [P, NC_, P]),
                                        bc(POSB[:, :, e:e + 1], [P, NC_, P]), ALU.is_equal).then_inc(g_ready, 1)
            dve.wait_ge(g_psum, NE)
            slots = bank(2)[:, 0:5 * NE].rearrange("p (e n) -> p e n", e=NE)
            go(v.tensor_copy(GATE, slots[:, :, 2]))
            go(v.tensor_tensor(GATE2, GATE, slots[:, :, 3], ALU.add))
            v.tensor_tensor(GATE, GATE2, slots[:, :, 4], ALU.add).then_inc(idx_ready, 1)
            go(v.tensor_copy(TMP2[:, 0, :], slots[:, :, 0]))
            v.scalar_tensor_tensor(out=IDX.bitcast(U32), in0=TMP2[:, 0, :], scalar=float(P), in1=slots[:, :, 1],
                                   op0=ALU.mult, op1=ALU.add).then_inc(idx_ready, 1)

            def rows_step():
                go(v.tensor_scalar(TMP2, POSP, float(P), None, ALU.is_ge))
                for j in range(2, NC_):
                    go(v.scalar_tensor_tensor(out=TMP2, in0=POSP, scalar=float(P * j), in1=TMP2, op0=ALU.is_ge, op1=ALU.add))
                go(v.scalar_tensor_tensor(out=POSP, in0=TMP2, scalar=float((NE - 1) * P), in1=POSP, op0=ALU.mult, op1=ALU.add))
                go(v.tensor_tensor(POSP, POSP, bc(ECAP.unsqueeze(1), [P, NC_, NE]), ALU.add))
                for s_, r, i in ((S1, R1F, 0), (S2, R2F, 1)):
                    go(v.tensor_tensor(TMP, POSP, s_, ALU.mult))
                    go(v.tensor_reduce(r, TMP, AX.X, ALU.add))
                    go(v.tensor_copy(R12[:, i, :].bitcast(U32), r))
                go(v.tensor_reduce(FLAG[:, 0:1], CNT, AX.X, ALU.max))
                v.tensor_copy(FLAG[:, 1:2].bitcast(U32), FLAG[:, 0:1]).then_inc(idx_ready, 1)

            return rows_step

        route_steps = {}

        def router_scores(pe, m):
            t0, n = CH[m]
            if m == 0:
                pe.wait_ge(wr_loaded, 32)
                pe.wait_ge(x2_ready, 4 * NC_)
            pe.wait_ge(ht_ready, N_I + m + 1)
            for k in range(KD):
                last = nc.tensor.matmul(bank(0)[:n, 32 * m:32 * m + 20], HT[:, k, t0:t0 + n], WR[:, k, :],
                                        start=(k == 0), stop=(k == KD - 1))
            return last

        def route_pe(pe):
            router_scores(pe, NC_ - 1).then_inc(lg_psum, 1)
            pe.wait_ge(route, route_steps["mask"])
            for c in range(NC_ + 1):
                for c2 in range(min(c + 1, NC_)):
                    last = nc.tensor.matmul(bank(1)[:, 16 * c:16 * c + 16], TSTR_B if c2 == c else ONES_B, MK[:, c2, :],
                                            start=(c2 == 0), stop=(c2 == min(c, NC_ - 1)))
            last.then_inc(pos_psum, 1)
            for e in range(NE):
                pe.wait_ge(g_ready, e + 1)
                for c in range(NC_):
                    last = nc.tensor.matmul(bank(2)[:, 5 * e:5 * e + 5], GM[e % 2][:, c, :], TW[:, c, e, :],
                                            start=(c == 0), stop=(c == NC_ - 1))
                last.then_inc(g_psum, 1)
            pe.wait_ge(idx_ready, 2)

        E_TILES = []
        first_half = {}

        def expert_tiles(name, e):
            w = I[name][0, e].rearrange("(k p) f -> p k f", p=P)
            nk = w.shape[1] // 2
            first_half[name, e] = len(E_TILES)
            for h in range(2):
                E_TILES.append(w[:, h * nk:(h + 1) * nk, :])

        expert_tiles("w_gate_e", 0)
        for e in range(NE):
            expert_tiles("w_up_e", e)
            if e + 1 < NE:
                expert_tiles("w_gate_e", e + 1)
            expert_tiles("w_down_e", e)
        NT = len(E_TILES)

        def used(name, e):
            return first_half[name, e] + 2

        def e_view(buf, t):
            return buf.rearrange("p (k f) -> p k f", k=E_TILES[t].shape[1])

        def e_raw(t):
            return e_view(MSLOT[t % NMRAW], t)

        def e_hi(t):
            return r32(e_view(MSLOT[NMRAW + t % NMHI], t))

        def e_lo(t):
            return r32(e_raw(t))

        def expert_high(act, t):
            if t >= NT:
                return
            if t >= NMHI:
                act.wait_ge(ew_used, t - NMHI + 1)
            act.wait_ge(mring_loaded[t % NMRAW], 16 * (t // NMRAW + 1))
            nc.scalar.copy(e_hi(t), e_raw(t)).then_inc(wh_ready, 1)

        def expert_low(dve, t):
            if t >= NT:
                return
            dve.wait_ge(wh_ready, len(tiles) + t + 1)
            nc.vector.tensor_tensor(e_lo(t), e_raw(t), e_hi(t), ALU.subtract).then_inc(wl_ready, 1)

        A_E = A_OT + KD

        def a_tokens(e):
            return A_E + (1 if e == 0 else 2 * e)

        def a_hidden(e):
            return A_E + (2 * e + 3 if e + 1 < NE else 2 * e + 2)

        def experts_sp(sp):
            for m, (t0, n) in enumerate(CH):
                sp.wait_ge(xn_ready, N_I + m + 1)
                sp.dma_start(hn_rows[t0:t0 + n, :], XNR[:n, m, :]).then_inc(hn_stored, 16)
            sp.wait_ge(mo_psum, 4 * NC_)
            sp.wait_ge(hn_stored, 16 * NC_)
            sp.wait_ge(ht_ready, N_I + NC_)
            for t in range(NT):
                if t >= NMRAW:
                    sp.wait_ge(ew_used, t - NMRAW + 1)
                sp.dma_start(e_raw(t), E_TILES[t]).then_inc(mring_loaded[t % NMRAW], 16)
                if t == 20:
                    sp.dma_start(NF, I["norm_final"].rearrange("(a d) -> a d", a=1).to_broadcast([P, D])).then_inc(nf_loaded, 16)

        def turn_tokens(src):
            for c in range(KD):
                last = nc.tensor.transpose(bank(0, 2)[:, c * P:(c + 1) * P], src[:, c * P:(c + 1) * P], IDENT)
            return last

        def expert_rows(b, gt, w):
            for k in range(KD):
                last = nc.tensor.matmul(bank(b), gt[:, k, :], w[:, k, :], start=(k == 0), stop=(k == KD - 1))
            return last

        def turn_hidden(he):
            for c in range(4):
                last = nc.tensor.transpose(bank(4)[:, c * P:(c + 1) * P], he[:, c * P:(c + 1) * P], IDENT)
            return last

        def expert_down(het, w):
            for h in range(2):
                for c in range(4):
                    last = nc.tensor.matmul(bank(5 + h), het[:, c, :], w[:, c, 512 * h:512 * (h + 1)],
                                            start=(c == 0), stop=(c == 3))
            return last

        def half_rows(pe, t, b, gth, gtl, h):
            pe.wait_ge(wl_ready, len(tiles) + t + 1)
            for i in range(4):
                k = 4 * h + i
                for j, (a, w) in enumerate(((gth, e_hi(t)), (gth, e_lo(t)), (gtl, e_hi(t)))):
                    last = nc.tensor.matmul(bank(b), r32(a[:, k, :]), w[:, i, :], start=(k == 0 and j == 0),
                                            stop=(k == KD - 1 and j == 2))
            last.then_inc(ew_used, 1)

        def half_down(pe, t, heth, hetl, h):
            pe.wait_ge(wl_ready, len(tiles) + t + 1)
            for c in range(2):
                for i in range(2):
                    k = 2 * h + i
                    for j, (a, w) in enumerate(((heth, e_hi(t)), (heth, e_lo(t)), (hetl, e_hi(t)))):
                        last = nc.tensor.matmul(bank(5 + c), r32(a[:, k, :]), w[:, i, 512 * c:512 * (c + 1)],
                                                start=(k == 0 and j == 0), stop=(k == 3 and j == 2))
            last.then_inc(ew_used, 1)

        def experts_pe(pe):
            def turn(e):
                pe.wait_ge(xg_loaded[e % NXG], 16 * (e // NXG + 1))
                if e:
                    pe.wait_ge(gt_ready, e)
                turn_tokens(XG[e % NXG]).then_inc(gt_psum, 1)

            def rows(name, e, b):
                for h in range(2):
                    half_rows(pe, first_half[name, e] + h, b, GTH[e % 2], GT[e % 2], h)

            turn(0)
            pe.wait_ge(al_ready, a_tokens(0))
            rows("w_gate_e", 0, 2)
            for e in range(NE):
                if e + 1 < NE:
                    turn(e + 1)
                if e:
                    pe.wait_ge(he_ready, e)
                rows("w_up_e", e, 3)
                if e + 1 < NE:
                    pe.wait_ge(al_ready, a_tokens(e + 1))
                    pe.wait_ge(sg_ready, e + 1)
                    rows("w_gate_e", e + 1, 2)
                pe.wait_ge(he_ready, e + 1)
                if e:
                    pe.wait_ge(al_ready, a_hidden(e - 1))
                turn_hidden(HE).then_inc(het_psum, 1)
                pe.wait_ge(al_ready, a_hidden(e))
                if e:
                    pe.wait_ge(yo_ready, e)
                for h in range(2):
                    half_down(pe, first_half["w_down_e", e] + h, HETH[e % 2], HET[e % 2], h)

        def experts_act(act):
            def silu(e):
                act.wait_ge(ew_used, used("w_gate_e", e))
                if e:
                    act.wait_ge(he_ready, e)
                nc.scalar.activation(SG, bank(2), ACT.Silu).then_inc(sg_ready, 1)

            def tokens_high(e):
                act.wait_ge(gt_ready, e + 1)
                act_high(GTH[e % 2], GT[e % 2])

            tokens_high(0)
            expert_high(act, 4)
            silu(0)
            expert_high(act, 5)
            for e in range(NE):
                if e + 1 < NE:
                    tokens_high(e + 1)
                t = 6 + 6 * e
                for i in range(3):
                    expert_high(act, t + i)
                if e + 1 < NE:
                    silu(e + 1)
                act.wait_ge(het_psum, e + 1)
                act_high(HETH[e % 2], bank(4).rearrange("p (c n) -> p c n", c=4))
                for i in range(3, 5):
                    expert_high(act, t + i)
                act.wait_ge(ew_used, used("w_down_e", e))
                if e >= 2:
                    act.wait_ge(y_stored[e % 2], 16 * (e // 2))
                nc.scalar.activation(YO[e % 2], bank(5, 2), ACT.Copy, scale=GATE[:, e:e + 1]).then_inc(yo_ready, 1)
                act.wait_ge(yo_ready, e + 1)
                act.dma_start(y_rows[e * P:(e + 1) * P, :], YO[e % 2]).then_inc(y_stored[e % 2], 16)
                expert_high(act, t + 5)

        def experts_dve(dve, rows_step):
            def tokens(e):
                dve.wait_ge(gt_psum, e + 1)
                if e >= 2:
                    dve.wait_ge(ew_used, used("w_up_e", e - 2))
                gain_tokens(GT[e % 2]).then_inc(gt_ready, 1)

            tokens(0)
            for t in range(4):
                expert_low(dve, t)
                if t == 0:
                    act_low(dve, a_tokens(0), GT[0], GTH[0])
            expert_low(dve, 4)
            for e in range(NE):
                t = 6 + 6 * e
                if e + 1 < NE:
                    tokens(e + 1)
                expert_low(dve, t - 1)
                if e + 1 < NE:
                    act_low(dve, a_tokens(e + 1), GT[(e + 1) % 2], GTH[(e + 1) % 2])
                expert_low(dve, t)
                dve.wait_ge(sg_ready, e + 1)
                dve.wait_ge(ew_used, used("w_up_e", e))
                if e:
                    dve.wait_ge(het_psum, e)
                nc.vector.tensor_tensor(HE, bank(3), SG, ALU.mult).then_inc(he_ready, 1)
                expert_low(dve, t + 1)
                expert_low(dve, t + 2)
                dve.wait_ge(ah_ready, a_hidden(e))
                nc.vector.tensor_tensor(r32(HET[e % 2]), bank(4).rearrange("p (c n) -> p c n", c=4), r32(HETH[e % 2]),
                                        ALU.subtract).then_inc(al_ready, 1)
                expert_low(dve, t + 3)
                expert_low(dve, t + 4)
                if e == 1:
                    rows_step()

        def gain_tokens(dst):
            return nc.vector.tensor_tensor(dst, bank(0, 2).rearrange("p (c n) -> p c n", c=KD),
                                           bc(G_FFN.unsqueeze(2), [P, KD, P]), ALU.mult)

        def experts_pool(pool):
            for e in range(NE):
                if e >= NXG:
                    pool.wait_ge(gt_psum, e - NXG + 1)
                pool.indirect_dma_start(XG[e % NXG], None, hn_rows,
                                        bass.IndirectOffsetOnAxis(ap=IDX.bitcast(U32)[:, e:e + 1], axis=0)
                                        ).then_inc(xg_loaded[e % NXG], 16)

        def overflow(eng, body):
            eng.wait_ge(idx_ready, 3)
            count = eng.value_load(FLAG[0:1, 1:2].bitcast(U32), min_val=0, max_val=T)
            with eng.If(count > P):
                with eng.Fori(0, NE) as e:
                    for j in range(1, NC_):
                        body(e, j)
                        eng.wait_ge(y_stored[0], 16 * (NE // 2) + nth(e, j, 16))

        def nth(e, j, k=1):
            return e * (k * (NC_ - 1)) + k * j

        def oview(i):
            return OSLOT[i].rearrange("p (k f) -> p k f", f=FF if i < 2 else D)

        def ew(e, j, i):
            return NT + nth(e, j, 3) - 2 + i

        def overflow_sp(e):
            nc.sync.wait_ge(y_stored[0], 16 * (NE // 2) + nth(e, 0, 16))
            for i, name in enumerate(("w_gate_e", "w_up_e", "w_down_e")):
                nc.sync.dma_start(oview(i), I[name][0, bass.ds(e, 1)].rearrange("a (k p) f -> p (a k) f", p=P)
                                  ).then_inc(mring_loaded[0], 16)

        def overflow_pool(e, j):
            nc.gpsimd.wait_ge(idx_ready, 3 + nth(e, j, 4))
            nc.gpsimd.indirect_dma_start(XG[0], None, hn_rows, bass.IndirectOffsetOnAxis(ap=IDXO.bitcast(U32), axis=0)
                                         ).then_inc(xg_loaded[0], 16)

        def overflow_pe(e, j):
            pe = nc.tensor
            pe.wait_ge(g_ready, NE + nth(e, j, 3))
            for c in range(NC_):
                last = pe.matmul(bank(7)[:, 0:5], GM[0][:, c, :], TWO[:, c, :], start=(c == 0), stop=(c == NC_ - 1))
            last.then_inc(g_psum, 1)
            pe.wait_ge(xg_loaded[0], 16 * (NE // NXG) + nth(e, j, 16))
            turn_tokens(XG[0]).then_inc(gt_psum, 1)
            pe.wait_ge(gt_ready, NE + nth(e, j))
            pe.wait_ge(mring_loaded[0], 16 * (-(-NT // NMRAW)) + e * 48 + 48)
            expert_rows(2, GT[0], oview(0)).then_inc(ew_used, 1)
            expert_rows(3, GT[0], oview(1)).then_inc(ew_used, 1)
            pe.wait_ge(he_ready, NE + nth(e, j))
            turn_hidden(HE).then_inc(het_psum, 1)
            pe.wait_ge(het_ready, nth(e, j))
            expert_down(HET[0], oview(2)).then_inc(ew_used, 1)

        def overflow_dve(e, j):
            dve = nc.vector
            dve.tensor_scalar(PC.unsqueeze(2), POSM[:, :, bass.ds(e, 1)], -float(P * j), None, ALU.add).then_inc(g_ready, 1)
            dve.tensor_copy(TWO.unsqueeze(2), TW[:, :, bass.ds(e, 1), :]).then_inc(g_ready, 1)
            dve.wait_ge(g_ready, NE + nth(e, j, 3) - 1)
            dve.tensor_tensor(GM[0], bc(IOTA.unsqueeze(1), [P, NC_, P]), bc(PC.unsqueeze(2), [P, NC_, P]),
                              ALU.is_equal).then_inc(g_ready, 1)
            dve.wait_ge(g_psum, NE + nth(e, j))
            dve.tensor_copy(SLOTO, bank(7)[:, 0:5]).then_inc(idx_ready, 1)
            dve.wait_ge(idx_ready, nth(e, j, 4))
            dve.tensor_tensor(GATEO[:, 0:1], SLOTO[:, 2:3], SLOTO[:, 3:4], ALU.add).then_inc(idx_ready, 1)
            dve.wait_ge(idx_ready, 1 + nth(e, j, 4))
            dve.tensor_tensor(GATEO[:, 1:2], GATEO[:, 0:1], SLOTO[:, 4:5], ALU.add).then_inc(idx_ready, 1)
            dve.scalar_tensor_tensor(out=IDXO.bitcast(U32), in0=SLOTO[:, 0:1], scalar=float(P), in1=SLOTO[:, 1:2],
                                     op0=ALU.mult, op1=ALU.add).then_inc(idx_ready, 1)
            dve.wait_ge(gt_psum, NE + nth(e, j))
            gain_tokens(GT[0]).then_inc(gt_ready, 1)
            dve.wait_ge(sg_ready, NE + nth(e, j))
            dve.wait_ge(ew_used, ew(e, j, 1))
            dve.tensor_tensor(HE, bank(3), SG, ALU.mult).then_inc(he_ready, 1)
            dve.wait_ge(het_psum, NE + nth(e, j))
            dve.tensor_copy(HET[0], bank(4).rearrange("p (c n) -> p c n", c=4)).then_inc(het_ready, 1)

        def overflow_act(e, j):
            act = nc.scalar
            act.wait_ge(ew_used, ew(e, j, 0))
            act.activation(SG, bank(2), ACT.Silu).then_inc(sg_ready, 1)
            act.wait_ge(ew_used, ew(e, j, 2))
            act.wait_ge(idx_ready, 3 + nth(e, j, 4))
            act.activation(YO[0], bank(5, 2), ACT.Copy, scale=GATEO[:, 1:2]).then_inc(yo_ready, 1)
            act.wait_ge(yo_ready, NE + nth(e, j))
            act.dma_start(y_rows[bass.ds(e * P + NE * P * j, P), :], YO[0]).then_inc(y_stored[0], 16)

        def moe_sp(sp):
            experts_sp(sp)
            sp.wait_ge(ew_used, NT)
            sp.wait_ge(idx_ready, 3)
            count = sp.value_load(FLAG[0:1, 1:2].bitcast(U32), min_val=0, max_val=T)
            with sp.If(count > P):
                with sp.Fori(0, NE) as e:
                    overflow_sp(e)

        def moe_pool(pool):
            pool.wait_ge(mo_psum, 1)
            pool.iota(IOTA, [[1, P]], base=0, channel_multiplier=0, allow_small_or_imprecise_dtypes=True).then_inc(route_const, 1)
            pool.iota(ECAP, [[P, NE]], base=0, channel_multiplier=0, allow_small_or_imprecise_dtypes=True).then_inc(route_const, 1)
            for i in range(4):
                last = pool.memset(W4[:, i:i + 1], float(8 >> i))
            last.then_inc(route_const, 1)
            for c in range(NC_):
                pool.memset(TW[:, c, :, 0], float(c))
            pool.iota(TW[:, :, :, 1], [[0, NC_], [0, NE]], base=0, channel_multiplier=1,
                      allow_small_or_imprecise_dtypes=True).then_inc(route_const, 1)
            pool.wait_ge(idx_ready, 2)
            experts_pool(pool)
            pool.wait_ge(gt_psum, NE)
            pool.wait_ge(idx_ready, 3)
            count = pool.value_load(FLAG[0:1, 1:2].bitcast(U32), min_val=0, max_val=T)
            with pool.If(count > P):
                for e in range(NE):
                    for j in range(1, NC_):
                        overflow_pool(e, j)
                        pool.wait_ge(y_stored[0], 16 * (NE // 2) + nth(e, j, 16))
            for i in range(2):
                pool.wait_ge(y_stored[i], 16 * (NE // 2))
            with pool.If(count > P):
                gather_results(pool, y_rows)
            with pool.If(count <= P):
                gather_results(pool, y_rows[0:NE * P, :])
            for m, (t0, n) in enumerate(CH):
                pool.wait_ge(fin_ready, m + 1)
                dst = O["y_prompt"][0, t0:t0 + n, :] if m < 4 else O["y_sample"][0]
                out_dma(pool, dst, X[:n, m, :], late_stored)

        def gather_results(pool, rows):
            for m, (t0, n) in enumerate(CH):
                if m >= 2:
                    pool.wait_ge(x3_ready, m - 1)
                for i in range(2):
                    pool.indirect_dma_start(XG[2 * (m % 2) + i][:n, :], None, rows,
                                            bass.IndirectOffsetOnAxis(ap=R12.bitcast(U32)[:n, i, m:m + 1], axis=0)
                                            ).then_inc(fin_loaded[m % 2], 16)

        def moe_act(act):
            act.wait_ge(route, route_group)
            nc.scalar.activation(E4, E4, ACT.Exp).then_inc(route_exp, 1)
            act.wait_ge(route, route_diff)
            nc.scalar.activation(EX, EX, ACT.Exp).then_inc(route_exp, 1)
            for t in range(NMHI):
                expert_high(act, t)
            act.wait_ge(idx_ready, 2)
            experts_act(act)
            act.wait_ge(y_stored[0], 16 * (NE // 2))
            overflow(act, overflow_act)
            exp_and_ln()
            for m, (_, n) in enumerate(CH):
                act.wait_ge(x3_ready, m + 1)
                norm_stat(N_F + m, X[:n, m, :], n, SQ2)

        def moe_dve(dve):
            rows_step = route_dve(dve)
            experts_dve(dve, rows_step)
            overflow(dve, overflow_dve)
            dve.wait_ge(nf_loaded, 16)

            def finish(m):
                n = CH[m][1]
                dve.wait_ge(ri_ready, N_F + m + 1)
                nc.vector.scalar_tensor_tensor(out=X[:n, m, :], in0=X[:n, m, :], scalar=RI[:n, 17 + m:18 + m], in1=NF[:n, :],
                                               op0=ALU.mult, op1=ALU.mult).then_inc(fin_ready, 1)

            for m, (_, n) in enumerate(CH):
                dve.wait_ge(fin_loaded[m % 2], 32 * (m // 2 + 1))
                nc.vector.tensor_tensor(X[:n, m, :], X[:n, m, :], XG[2 * (m % 2)][:n, :], ALU.add).then_inc(y1_sum, 1)
                dve.wait_ge(y1_sum, m + 1)
                nc.vector.tensor_tensor(X[:n, m, :], X[:n, m, :], XG[2 * (m % 2) + 1][:n, :], ALU.add).then_inc(x3_ready, 1)
                if m:
                    finish(m - 1)
            finish(NC_ - 1)

        def moe_pe(pe):
            route_pe(pe)
            experts_pe(pe)
            overflow(pe, overflow_pe)

        route_group, route_diff = 7, 30
        SQ2 = GT[0].rearrange("p c n -> p (c n)")
        block = ctx.enter_context(nc.Block())

        @block.sync
        def _(sp):
            xr = I["x_prompt"][0].rearrange("(m p) d -> p m d", p=P)
            def load_rows(dst):
                for m in range(4):
                    sp.dma_start(dst[:, m, :], xr[:, m, :]).then_inc(x_loaded[m], 16)
                sp.dma_start(dst[:LS, 4, :], I["x_sample"][0]).then_inc(x_loaded[4], 16)

            def load(n):
                if n >= NRAW:
                    sp.wait_ge(*retire[n - NRAW])
                for k0, src in tiles[n][0]:
                    sp.dma_start(tile_view(RAW[n % NRAW], n)[:, k0:k0 + src.shape[1], :], src).then_inc(ring_loaded[n % NRAW], 16)

            load_rows(XS)
            load(0)
            load(1)
            for m in range(2):
                sp.dma_start(MR[:, m, :], I["mem_prompt"][0, m * P:(m + 1) * P, :]).then_inc(mem_loaded[m], 16)
            load(2)
            load(3)
            sp.dma_start(PVR, I["cache_sb_v"][0, 0].rearrange("(c p) h d -> p c (h d)", p=P)).then_inc(past_loaded, 16)
            sp.wait_ge(xn_ready, 7)
            sp.dma_start(PKR, I["cache_sb_k"][0, 0].rearrange("(c p) h d -> p c (h d)", p=P)).then_inc(past_loaded, 16)
            for n in range(4, W_X + 4):
                load(n)
            sp.wait_ge(ysb_ready, 5)
            sp.wait_ge(out_stored, 16 * KV_STORES)
            sp.dma_start(H0R, I["state_ssm"][0, 0].rearrange("h q n -> (h q) n").rearrange("(b p) n -> p b n", p=P)
                         ).then_inc(state_loaded, 16)
            for n in range(W_X + 4, W_O + 2):
                load(n)
            sp.wait_ge(gb_psum, KD)
            load_rows(X)
            for n in range(W_O + 2, W_KV + 5):
                load(n)
            sp.wait_ge(mg_ready, KD)
            sp.wait_ge(wo_psum, 4 * NC_)
            sp.dma_start(MC[:, 0], I["cache_mem_k"][0, 0].rearrange("(m p) h d -> p m (h d)", p=P)).then_inc(memc_loaded, 16)
            sp.dma_start(MC[:, 1], I["cache_mem_v"][0, 0].rearrange("(m p) h d -> p m (h d)", p=P)).then_inc(memc_loaded, 16)
            for n in range(W_KV + 5, len(tiles)):
                load(n)
            moe_sp(sp)
            sp.wait_ge(out_stored, 16 * MIX_STORES)
            sp.wait_ge(late_stored, 16 * (4 + NC_))

        @block.gpsimd
        def _(pool):
            rows = [("norm_mix", 0), ("norm_mem_kv", 8), ("ssm_norm", 16), ("norm_mem_q", 24), ("norm_ffn", 32),
                    ("conv_b", 40)]
            for name, r in rows:
                v = I[name][0].rearrange("(r p) -> r p", p=P)
                pool.dma_start(VEC[r:r + v.shape[0], :], v).then_inc(vec_loaded, 16)
            pool.dma_start(VEC[52:100, :], I["conv_w"][0].rearrange("j (c p) -> (j c) p", p=P)).then_inc(vec_loaded, 16)
            pool.dma_start(CTXR[0:36, :], I["state_conv"][0, 0].rearrange("j (c p) -> (j c) p", p=P)).then_inc(vec_loaded, 16)
            for i, name in enumerate(("dt_bias", "a_log", "d_skip")):
                pool.dma_start(HCOL[0:NH, i:i + 1], I[name].rearrange("a h -> h a")).then_inc(vec_loaded, 16)
            pool.dma_start(WR[:, :, 0:4], I["w_group_router"][0].rearrange("(k p) n -> p k n", p=P)).then_inc(wr_loaded, 16)
            pool.dma_start(WR[:, :, 4:20], I["w_expert_router"][0].rearrange("(k p) n -> p k n", p=P)).then_inc(wr_loaded, 16)
            for m in (IDENT, ):
                nc.gpsimd.memset(m, 0.0).then_inc(const0, 1)
            for m in (TSUF, TINC, TSTR):
                nc.gpsimd.memset(m, 1.0).then_inc(const0, 1)
            nc.gpsimd.memset(ONES, 1.0).then_inc(consts, 1)
            nc.gpsimd.memset(CST, EPS).then_inc(consts, 1)
            pool.wait_ge(const0, 4)
            for m, op, step, cm in ((IDENT, ALU.not_equal, -1, 1), (TSUF, ALU.is_ge, -1, 1),
                                    (TINC, ALU.is_ge, 1, -1), (TSTR, ALU.is_gt, 1, -1)):
                pool.affine_select(out=m, in_=m, compare_op=op, fill=1.0 if m is IDENT else 0.0, base=0,
                                   pattern=[[step, P]], channel_multiplier=cm).then_inc(consts, 1)
            for g, (name, rows_) in enumerate((("sb_k", KR), ("sb_v", VR))):
                pool.wait_ge(kv_rows, 10 * (g + 1))
                out_dma(pool, O[name + "_prompt"][0, 0].rearrange("(m p) h d -> p m (h d)", p=P), rows_[:, 0:4, :])
                out_dma(pool, O[name + "_sample"][0, 0].rearrange("p h d -> p (h d)"), rows_[:LS, 4, :])

            def mask(u, buf, done):
                if u < SBH:
                    for kc in range(4):
                        v = buf[:, OFF[kc]:OFF[kc] + P]
                        last = pool.affine_select(out=v, in_=v, compare_op=ALU.is_gt, fill=0.0, base=0,
                                                  pattern=[[1, P]], channel_multiplier=-1)
                else:
                    v = buf[:, 1024:1280].rearrange("p (h t) -> p h t", h=4)
                    last = pool.affine_select(out=v, in_=v, compare_op=ALU.is_gt, fill=0.0, base=0,
                                              pattern=[[0, 4], [1, LS]], channel_multiplier=-1)
                last.then_inc(done, 1)

            for u in range(U_ + 1):
                if u < U_:
                    pool.wait_ge(sp_raw, u + 1)
                    mask(u, LB[u % 2], sp_ready)
                if u >= 1:
                    pool.wait_ge(w_raw, u)
                    mask(u - 1, ZSB[(u - 1) % 3], w_ready)
            pool.wait_ge(ysb_ready, 5)
            pool.wait_ge(out_stored, 16 * KV_STORES)
            nc.gpsimd.memset(XC[:, :, T:TS], 0.0).then_inc(pads, 1)
            for s, name in ((0, "conv_prompt"), (1, "conv_sample")):
                pool.wait_ge(tail_rows, s + 1)
                out_dma(pool, O[name][0, 0].rearrange("j (c p) -> (j c) p", p=P), TAILR[0:36, s, :])
            pool.wait_ge(out_stored, 16 * stored[0])
            pool.wait_ge(dve_dt, 7)
            nc.gpsimd.memset(HS[:, 0], 0.0).then_inc(pads, 1)
            for v in range(10):
                c, g = divmod(v, 2)
                if v == 0:
                    pool.wait_ge(xc_ready, CONV_C)
                    pool.wait_ge(vec_ready, 4)
                if v >= 1:
                    pool.wait_ge(t3_done, v)
                nc.gpsimd.tensor_tensor(DX, XC[:, 4 * g:4 * g + 4, c * P:(c + 1) * P],
                                        bc(DP[:, 4 * g:4 * g + 4].unsqueeze(2), [P, 4, P]),
                                        ALU.mult).then_inc(dx_ready, 1)
            for s, name in ((0, "ssm_prompt"), (1, "ssm_sample")):
                pool.wait_ge(so_rows, s + 1)
                out_dma(pool, O[name][0, 0].rearrange("h q n -> (h q) n").rearrange("(b p) n -> p b n", p=P), HO)
            for t in range(4):
                pool.wait_ge(mkv_rows, 4 * (t + 1))
                name = ("mem_k_prompt", "mem_v_prompt")[t // 2]
                dst = O[name][0, 0].rearrange("(m p) h d -> p m (h d)", p=P)[:, :, 512 * (t % 2):512 * (t % 2) + 512]
                out_dma(pool, dst, MKV[:, :, 512 * t:512 * (t + 1)], late_stored)
            moe_pool(pool)

        def mem_out(act, h):
            for dc in range(2):
                act.wait_ge(ot_psum, 2 * h + dc + 1)
                nc.scalar.copy(OT[:, 2 * h + dc, :], bank(4 + 2 * dc, 2)[:, 0:T]).then_inc(ot_ready, 1)
                act.wait_ge(ot_ready, 2 * h + dc + 1)
                act_high(OTH[:, 2 * h + dc, :], OT[:, 2 * h + dc, :])

        def act_ht(i):
            t0, n = CH[i]
            nc.scalar.wait_ge(ht_ready, i + 1)
            act_high(HTH[:, :, t0:t0 + n], HT[:, :, t0:t0 + n])

        def exp_and_ln():
            nc.scalar.preload_act_table_set("natural_log_exp_and_others")

        @block.scalar
        def _(act):
            exp_and_ln()
            act.wait_ge(consts, 6)
            for i, (src, n) in enumerate(srcA):
                act.wait_ge(x_loaded[i] if i < NC_ else mem_loaded[i - NC_], 16)
                norm_stat(i, src, n, SQ)
                if i == 2:
                    split_high(act, 0)
                if i >= 3:
                    act_ht(i - 3)
            act_ht(4)
            split_high(act, 1)
            for i in range(20):
                t, m = divmod(i, 5)
                n = CH[m][1]
                act.wait_ge(kv_psum, i + 1)
                nc.scalar.copy((KR, VR)[t // 2][:n, m, 256 * (t % 2):256 * (t % 2) + 256], bank(4 + i % 4)[:n, 0:256]).then_inc(kv_rows, 1)
                if m == 4:
                    split_high(act, t + 2)
            split_high(act, W_X)
            split_high(act, W_X + 1)
            for b in range(9):
                act.wait_ge(kt_psum, b + 1)
                nc.scalar.copy(KTA[:, :, b * P:(b + 1) * P],
                               bank(4 + b % 4).rearrange("p (h n) -> p h n", h=4)).then_inc(kt_ready, 1)
            for u in range(U_ + 1):
                if u < U_:
                    act.wait_ge(z_copied, u + 1)
                    if u >= 2:
                        act.wait_ge(s_psum, u - 1)
                    lb = LB[u % 2]
                    nc.scalar.activation(lb, ZSB[u % 3], ACT.Abs).then_inc(z_abs, 1)
                    act.wait_ge(z_abs, u + 1)
                    nc.scalar.activation(lb, lb, ACT.Exp, scale=-1.0).then_inc(z_exp, 1)
                    act.wait_ge(z_exp, u + 1)
                    nc.scalar.activation(lb, lb, ACT.Ln, bias=1.0).then_inc(l_ready, 1)
                if u >= 1:
                    act.wait_ge(u_ready, u)
                    nc.scalar.activation(ZSB[(u - 1) % 3], ZSB[(u - 1) % 3], ACT.Exp).then_inc(w_raw, 1)
            act.wait_ge(ysb_ready, 5)
            act.wait_ge(out_stored, 16 * KV_STORES)
            for i in range(CONV_C + 1):
                if i < CONV_C:
                    act.wait_ge(xb_psum, i + 1)
                    if i >= 3:
                        act.wait_ge(conv_done, i - 2)
                    b = bank(2 * (i % 2), 2)
                    h = T // 2
                    nc.scalar.copy(XR[i % 3][:, 3:3 + h], b[:, 0:h])
                    nc.scalar.copy(XR[i % 3][:, 3 + h:515], b[:, 512:512 + LP - h])
                    nc.scalar.copy(XR[i % 3][:, 518:582], b[:, 512 + LP - h:512 + h]).then_inc(xr_ready, 1)
                    if i % 2:
                        split_high(act, W_X + 2 + i // 2)
                if i >= 1:
                    j = i - 1
                    act.wait_ge(conv_done, j + 1)
                    nc.scalar.activation(XC[:, j, 0:LP], CV[j % 2][:, 0:512], ACT.Silu)
                    nc.scalar.activation(XC[:, j, LP:T], CV[j % 2][:, 515:579], ACT.Silu).then_inc(xc_ready, 1)
            for i in range(KD):
                act.wait_ge(zt_psum, i + 1)
                nc.scalar.activation(halves(ZS[:, i, :]), pair(2 * (i % 2)), ACT.Silu).then_inc(zt_ready, 1)
                if i % 2:
                    split_high(act, W_Z + 2 + i // 2)
            exp_and_ln()
            act.wait_ge(dve_dt, 1)
            nc.scalar.activation(AD[0:NH, :], UD[0:NH, :], ACT.Abs).then_inc(act_dt, 1)
            act.wait_ge(act_dt, 1)
            nc.scalar.activation(AD[0:NH, :], AD[0:NH, :], ACT.Exp, scale=-1.0).then_inc(act_dt, 1)
            act.wait_ge(act_dt, 2)
            nc.scalar.activation(AD[0:NH, :], AD[0:NH, :], ACT.Ln, bias=1.0).then_inc(act_dt, 1)
            nc.scalar.activation(HCOL[0:NH, 3:4], HCOL[0:NH, 1:2], ACT.Exp).then_inc(act_dt, 1)
            split_high(act, W_M + 1)
            act.wait_ge(dve_dt, 6)
            nc.scalar.activation(ECM[0:NH, :], CUM[0:NH, :], ACT.Exp).then_inc(act_dt, 1)
            act.wait_ge(pre_dve, 4)
            nc.scalar.activation(TE, TE, ACT.Exp).then_inc(pre_act, 1)
            act.wait_ge(pre_psum, 2)
            nc.scalar.activation(CD, bank(7)[:, 160:240].rearrange("p (c h) -> p c h", c=NC_), ACT.Exp).then_inc(pre_act, 1)
            for v in range(10):
                act.wait_ge(ec_psum, v + 1)
                if v >= 1:
                    act.wait_ge(t1_done, v)
                nc.scalar.copy(ECS, bank(5)).then_inc(ec_done, 1)
                act.wait_ge(seg_done, v + 1)
                nc.scalar.activation(SEG[v % 2], SEG[v % 2], ACT.Exp).then_inc(e_ready, 1)
            for i in range(KD):
                act.wait_ge(yz_done, 10)
                if i >= 2:
                    act.wait_ge(ssq_psum, i - 1)
                nc.scalar.activation(SQT[i % 2], ZS[:, i, :], ACT.Square).then_inc(sq_ready, 1)
            act.wait_ge(ssq_psum, KD)
            nc.scalar.activation(RB, bank(0, 2)[:, 0:T], ACT.Ln, scale=1.0 / D, bias=CST[:, 0:1]).then_inc(rb_ln, 1)
            act.wait_ge(rb_ln, 1)
            nc.scalar.activation(RB, RB, ACT.Exp, scale=-0.5).then_inc(rb_ready, 1)
            act.wait_ge(intra_psum, 10)
            act_high(YSBTH, YSBT)
            act.wait_ge(out_stored, 16 * MIX_STORES)
            for i in range(KD):
                act.wait_ge(yn_ready, i + 1)
                act_high(ZSH[:, i, :], ZS[:, i, :])
            for c in range(KD):
                act.wait_ge(gs_psum, c + 1)
                if c >= 2:
                    act.wait_ge(m1_done, c - 1)
                nc.scalar.activation(halves(GS[c % 2]), pair(0), ACT.Sigmoid).then_inc(gs_ready, 1)
                act.wait_ge(gb_psum, c + 1)
                if c >= 2:
                    act.wait_ge(m2_done, c - 1)
                nc.scalar.activation(halves(GB[c % 2]), pair(2), ACT.Sigmoid).then_inc(gb_ready, 1)
                split_high(act, W_M + 2 * c + 2)
                if c < KD - 1:
                    split_high(act, W_M + 2 * c + 3)
                act.wait_ge(mg_ready, c + 1)
                act_high(MGH[:, c, :], MG[:, c, :])
            exp_and_ln()
            act_high(MTH, MT)
            for n in range(W_O + 1, W_KV + 2):
                split_high(act, n)
            for t in range(8):
                for m in range(2):
                    act.wait_ge(mkv_psum, 2 * t + m + 1)
                    nc.scalar.copy(MKV[:, m, 256 * t:256 * (t + 1)], bank((2 * t + m) % 4)[:, 0:256]).then_inc(mkv_rows, 1)
                split_high(act, W_KV + 2 + t)
                if t < NC_:
                    n = CH[t][1]
                    act.wait_ge(x1_ready, 3 * NC_ + t + 1)
                    norm_stat(N_G + t, X[:n, t, :], n, SQ)
                if 2 <= t < NC_ + 2:
                    t0, n = CH[t - 2]
                    act.wait_ge(ht_ready, N_G + t - 1)
                    act_high(HTH2[:, :, t0:t0 + n], HT[:, :, t0:t0 + n])
            for i in range(KD):
                act.wait_ge(mq_psum, i + 1)
                nc.scalar.mul(halves(QM[:, i, :]), pair(2 * (i % 2)), MHD ** -0.5).then_inc(mq_ready, 1)
                if i % 2:
                    split_high(act, W_MQ + 2 + i // 2)
            for a in range(20):
                h, m = divmod(a, 5)
                n = CH[m][1]
                act.wait_ge(nm_ready, a + 1)
                if a >= 2:
                    act.wait_ge(pt_psum, a - 1)
                nc.scalar.activation(PX[a % 2][:n, :], bank(a % 2)[:n, 0:ML], ACT.Exp, bias=NM[:n, a:a + 1],
                                     accum_out=RS[:n, a:a + 1]).then_inc(px_ready, 1)
                if m == 1 and h >= 1:
                    mem_out(act, h - 1)
            mem_out(act, MH - 1)
            split_high(act, W_MO + 2)
            split_high(act, W_MO + 3)
            for m, (_, n) in enumerate(CH):
                act.wait_ge(x2_ready, 3 * NC_ + m + 1)
                norm_stat(N_I + m, X[:n, m, :], n, SQ)
            moe_act(act)

        @block.vector
        def _(dve):
            nc.vector.memset(KR[LS:, 4, :], 0.0)
            nc.vector.memset(VR[LS:, 4, :], 0.0)
            nc.vector.memset(r32(HTH_END).bitcast(F32), 0.0)
            nc.vector.memset(r32(HT_END).bitcast(F32), 0.0)
            dve.wait_ge(vec_psum, 1)
            nc.vector.tensor_copy(VT, bank(7)[:, 0:100]).then_inc(vec_ready, 1)
            nc.vector.tensor_copy(CTXT, bank(7)[:, 128:164]).then_inc(vec_ready, 1)
            dve.wait_ge(vec_ready, 2)
            for i in range(len(srcA) + 1):
                if i == 3:
                    split_low(dve, 0)
                if i < len(srcA):
                    src, n = srcA[i]
                    norm_scale(dve, i, src, n, XN[i % 2][:n, :], i >= 2)
                if i >= 1:
                    norm_gain(dve, i - 1, G_MIX if i - 1 < NC_ else G_MKV, srcA[i - 1][1], 0, dstA[i - 1])
                if i >= 3:
                    t0, n = CH[i - 3]
                    act_low(dve, A_HT + i - 2, HT[:, :, t0:t0 + n], HTH[:, :, t0:t0 + n])
            for n in range(1, W_Q + 2):
                split_low(dve, n)
            for i in range(4):
                dve.wait_ge(q_psum, i + 1)
                nc.vector.tensor_scalar(halves(QT[:, i, :]), pair(2 * (i % 2)), HD ** -0.5, None,
                                        ALU.mult).then_inc(q_ready, 1)
                if i % 2:
                    split_low(dve, W_X + i // 2)

            def u_op(u):
                dve.wait_ge(s_psum, u + 1)
                nc.vector.tensor_tensor(ZSB[u % 3], ZSB[u % 3], ps[:, 1536:1536 + 1280], ALU.subtract).then_inc(u_ready, 1)

            def ysb_out(g):
                if g < 4:
                    dve.wait_ge(pv_psum, 2 * (g + 1))
                    nc.vector.tensor_copy(YSBT[:, g, 0:LP], bank(6 + g % 2)).then_inc(ysb_ready, 1)
                else:
                    dve.wait_ge(pv_psum, U_)
                    nc.vector.tensor_copy(YSBT[:, :, LP:T],
                                          bank(6 + g % 2)[:, 0:256].rearrange("p (h t) -> p h t", h=4)).then_inc(ysb_ready, 1)

            for u in range(U_ + 2):
                if u < U_:
                    dve.wait_ge(z_psum, u + 1)
                    if u >= 3:
                        dve.wait_ge(pv_psum, u - 2)
                    nc.vector.tensor_copy(ZSB[u % 3], ps[:, 0:1280]).then_inc(z_copied, 1)
                    dve.wait_ge(l_ready, u + 1)
                    dve.wait_ge(z_copied, u + 1)
                    nc.vector.scalar_tensor_tensor(out=LB[u % 2], in0=ZSB[u % 3], scalar=0.0, in1=LB[u % 2],
                                                   op0=ALU.max, op1=ALU.add).then_inc(sp_raw, 1)
                if 1 <= u <= U_:
                    u_op(u - 1)
                done = u - 2 + 1
                if u >= 2 and done % 2 == 0:
                    ysb_out(done // 2 - 1)

            dve.wait_ge(consts, 6)
            dve.wait_ge(out_stored, 16 * KV_STORES)
            for s in range(3):
                nc.vector.memset(XR[s][:, 0:3], 0.0)
            nc.vector.tensor_copy(SELP[0:NH], bc(IDENT[0:NH, 0:NH].unsqueeze(2), [NH, NH, HD])).then_inc(vec_ready, 1)
            for i in range(CONV_C):
                xr, cv = XR[i % 3], CV[i % 2]
                if i >= 2:
                    dve.wait_ge(xc_ready, i - 1)
                ctxv = CTXT.rearrange("p (j c) -> p j c", j=3)[:, :, i:i + 1]
                nc.vector.tensor_copy(xr[:, 515:518].unsqueeze(2), ctxv).then_inc(conv_step, 1)
                dve.wait_ge(xr_ready, i + 1)
                dve.wait_ge(conv_step, 4 * i + 1)
                nc.vector.tensor_copy(TAIL[:, 0, :, i:i + 1], xr[:, 512:515].unsqueeze(2))
                nc.vector.tensor_copy(TAIL[:, 1, :, i:i + 1], xr[:, 579:582].unsqueeze(2))
                nc.vector.tensor_scalar(cv[:, 0:579], xr[:, 0:579], CW[:, 0, i:i + 1], CB[:, i:i + 1],
                                        ALU.mult, ALU.add).then_inc(conv_step, 1)
                for j in range(1, 4):
                    dve.wait_ge(conv_step, 4 * i + 1 + j)
                    o = nc.vector.scalar_tensor_tensor(out=cv[:, 0:579], in0=xr[:, j:j + 579],
                                                       scalar=CW[:, j, i:i + 1], in1=cv[:, 0:579],
                                                       op0=ALU.mult, op1=ALU.add)
                    o.then_inc(conv_step if j < 3 else conv_done, 1)
                if i % 2:
                    split_low(dve, W_X + 2 + i // 2)
            for n in range(W_Z + 2, W_M + 1):
                split_low(dve, n)
            dve.wait_ge(dp_psum, 1)
            nc.vector.tensor_copy(DP, bank(7)[:, 240:248]).then_inc(vec_ready, 1)
            for s in range(2):
                dve.wait_ge(dp_psum, 3)
                nc.vector.tensor_copy(TAILR[0:36, s, :], bank(6)[0:36, P * s:P * (s + 1)]).then_inc(tail_rows, 1)
            dve.wait_ge(dt_psum, 1)
            nc.vector.tensor_scalar(halves(UD[0:NH, :]), pair(0, NH), HCOL[0:NH, 0:1], None, ALU.add).then_inc(dve_dt, 1)
            nc.vector.memset(DTT[0:NH, T:TS], 0.0)
            nc.vector.memset(RST[0:NH, :], 1.0).then_inc(dve_dt, 1)
            dve.wait_ge(dve_dt, 2)
            nc.vector.memset(RST[0:NH, :].rearrange("p (c t) -> p c t", t=P)[:, :, 0:1], 0.0).then_inc(dve_dt, 1)
            dve.wait_ge(act_dt, 3)
            nc.vector.scalar_tensor_tensor(out=DTT[0:NH, 0:T], in0=UD[0:NH, :], scalar=0.0, in1=AD[0:NH, :],
                                           op0=ALU.max, op1=ALU.add).then_inc(dve_dt, 1)
            dve.wait_ge(act_dt, 4)
            dve.wait_ge(dve_dt, 4)
            nc.vector.tensor_scalar(DTA[0:NH, :], DTT[0:NH, :], HCOL[0:NH, 3:4], -1.0, ALU.mult, ALU.mult).then_inc(dve_dt, 1)
            dve.wait_ge(dve_dt, 5)
            nc.vector.tensor_tensor_scan(CUM[0:NH, :], RST[0:NH, :], DTA[0:NH, :], 0.0, ALU.mult, ALU.add).then_inc(dve_dt, 1)
            dve.wait_ge(dve_dt, 6)
            last_cum = CUM[0:NH, :].rearrange("p (c t) -> p c t", t=P)[:, :, P - 1:P]
            nc.vector.tensor_tensor(DIAG[0:NH], bc(IDENT[0:NH, 0:NH].unsqueeze(1), [NH, NC_, NH]),
                                    bc(last_cum, [NH, NC_, NH]), ALU.mult).then_inc(dve_dt, 1)
            dve.wait_ge(pre_psum, 2)
            p7 = lambda a: bank(7)[:, a:a + 80].rearrange("p (c h) -> p c h", c=NC_)
            nc.vector.tensor_copy(CR, p7(0)).then_inc(pre_dve, 1)
            nc.vector.tensor_copy(DR, p7(80)).then_inc(pre_dve, 1)
            dve.wait_ge(pre_psum, 1)
            dve.wait_ge(pads, 2)
            nc.vector.tensor_copy(HS[:, 1], bank(1, 2).rearrange("p (g n) -> p g n", g=2)).then_inc(pre_dve, 1)
            dve.wait_ge(pre_dve, 3)
            nc.vector.tensor_tensor(TE, p7(160), CR, ALU.subtract).then_inc(pre_dve, 1)
            dve.wait_ge(pre_act, 2)
            nc.vector.tensor_tensor(WRW, DR, TE, ALU.mult).then_inc(pre_dve, 1)
            dve.wait_ge(pre_dve, 5)

            def xdt(v):
                c, g = divmod(v, 2)
                dve.wait_ge(ssd_tr, v + 1)
                if v >= 2:
                    dve.wait_ge(st_psum, v - 1)
                    dve.wait_ge(intra_psum, v - 1)
                nc.vector.tensor_copy(BROW[v % 2], bank(0)[:, 0:P])
                nc.vector.tensor_tensor(CBM[v % 2], bank(0)[:, P:2 * P], TINC, ALU.mult)
                xr = bank(7).rearrange("p (h q) -> p h q", h=8)
                for dst, w in ((XD, DR), (XW, WRW)):
                    last = nc.vector.tensor_tensor(dst[v % 2].rearrange("p (h q) -> p h q", h=8), xr,
                                                   bc(w[:, c, 8 * g:8 * g + 8].unsqueeze(2), [P, 8, HD]), ALU.mult)
                last.then_inc(sx_done, 1)

            def seg(v):
                c, g = divmod(v, 2)
                dve.wait_ge(cumb_psum, v + 1)
                if v >= 2:
                    dve.wait_ge(intra_psum, v - 1)
                b = bank(1, 2).rearrange("p (h t) -> p h t", h=8)
                for h in range(8):
                    last = nc.vector.tensor_scalar(SEG[v % 2][:, h, :], b[:, h, :], CR[:, c, 8 * g + h:8 * g + h + 1],
                                                   0.0, ALU.subtract, ALU.min)
                last.then_inc(seg_done, 1)

            for v in range(10):
                c, g = divmod(v, 2)
                sq = 0 if c < 4 else 1
                if v == 0:
                    xdt(0)
                    seg(0)
                dve.wait_ge(e_ready, v + 1)
                dve.wait_ge(sx_done, v + 1)
                nc.vector.tensor_tensor(SEG[v % 2], SEG[v % 2], bc(CBM[v % 2].unsqueeze(1), [P, 8, P]),
                                        ALU.mult).then_inc(m_ready, 1)
                dve.wait_ge(inter_psum, v + 1)
                dve.wait_ge(ec_done, v + 1)
                if v >= 2:
                    dve.wait_ge(yz_done, v - 1)
                nc.vector.tensor_tensor(T1[v % 2].rearrange("p j t -> p (j t)"), bank(4), ECS,
                                        ALU.mult).then_inc(t1_done, 1)
                hs = HS[:, sq, g, :].rearrange("p (h q) -> p h q", h=8)
                nc.vector.tensor_tensor(hs, hs, bc(CD[:, c, 8 * g:8 * g + 8].unsqueeze(2), [P, 8, HD]),
                                        ALU.mult).then_inc(h_dec, 1)
                dve.wait_ge(st_psum, v + 1)
                dve.wait_ge(h_dec, v + 1)
                nc.vector.tensor_tensor(HS[:, sq, g, :], HS[:, sq, g, :], bank(6), ALU.add).then_inc(h_ready, 1)
                if v < 9:
                    xdt(v + 1)
                    seg(v + 1)
                if v == 0:
                    split_low(dve, W_M + 1)
                dve.wait_ge(intra_psum, v + 1)
                dve.wait_ge(t1_done, v + 1)
                t1 = T1[v % 2]
                nc.vector.tensor_tensor(t1.rearrange("p j t -> p (j t)"), t1.rearrange("p j t -> p (j t)"), bank(3),
                                        ALU.add).then_inc(t2_done, 1)
                dve.wait_ge(t2_done, v + 1)
                dve.wait_ge(dx_ready, v + 1)
                nc.vector.tensor_tensor(t1, t1, DX, ALU.add).then_inc(t3_done, 1)
                dve.wait_ge(t3_done, v + 1)
                n = CH[c][1]
                zv = ZS[:, 4 * g:4 * g + 4, c * P:c * P + n]
                nc.vector.tensor_tensor(zv, zv, t1[:, :, 0:n], ALU.mult).then_inc(yz_done, 1)
            for s in range(2):
                dve.wait_ge(so_psum, s + 1)
                if s:
                    dve.wait_ge(out_stored, 16 * (KV_STORES + 3))
                nc.vector.tensor_copy(HO, bank(1, 2).rearrange("p (b n) -> p b n", b=8)).then_inc(so_rows, 1)
            dve.wait_ge(rb_ready, 1)
            dve.wait_ge(yz_done, 10)
            nc.vector.memset(r32(MG_END).bitcast(F32), 0.0)
            nc.vector.memset(r32(MGH_END).bitcast(F32), 0.0)
            for i in range(KD):
                nc.vector.scalar_tensor_tensor(out=ZS[:, i, :], in0=ZS[:, i, :], scalar=G_SSM[:, i:i + 1], in1=RB,
                                               op0=ALU.mult, op1=ALU.mult).then_inc(yn_ready, 1)
            act_low(dve, A_YSB + 1, YSBT, YSBTH)
            for i in range(KD):
                act_low(dve, A_ZS + i + 1, ZS[:, i, :], ZSH[:, i, :])
            for c in range(KD):
                split_low(dve, W_M + 2 * c + 2)
                dve.wait_ge(br_psum, c + 1)
                dve.wait_ge(gs_ready, c + 1)
                nc.vector.tensor_tensor(halves(M1[c % 2]), pair(4), halves(GS[c % 2]), ALU.mult).then_inc(m1_done, 1)
                dve.wait_ge(sb_psum, c + 1)
                dve.wait_ge(gb_ready, c + 1)
                nc.vector.tensor_tensor(halves(MG[:, c, :]), pair(6), halves(GB[c % 2]), ALU.mult).then_inc(m2_done, 1)
                dve.wait_ge(m1_done, c + 1)
                dve.wait_ge(m2_done, c + 1)
                nc.vector.tensor_tensor(MG[:, c, :], MG[:, c, :], M1[c % 2], ALU.add).then_inc(mg_ready, 1)
                if c < KD - 1:
                    split_low(dve, W_M + 2 * c + 3)
                act_low(dve, A_MG + c + 1, MG[:, c, :], MGH[:, c, :])
            def add_rows(psum, done, split):
                for i in range(4 * NC_):
                    t, m = divmod(i, NC_)
                    n = CH[m][1]
                    if psum is wo_psum and t == 0:
                        dve.wait_ge(x_loaded[m], 32)
                    dve.wait_ge(psum, i + 1)
                    xv = X[:n, m, 256 * t:256 * (t + 1)]
                    nc.vector.tensor_tensor(xv, xv, bank(i % 4)[:n, 0:256], ALU.add).then_inc(done, 1)
                    if m == NC_ - 1 and t < len(split):
                        split_low(dve, split[t])

            act_low(dve, A_MT + 1, MT, MTH)
            split_low(dve, W_O + 1)
            add_rows(wo_psum, x1_ready, [W_O + 2, W_O + 3, W_KV, W_KV + 1])
            for t in range(8):
                split_low(dve, W_KV + 2 + t)
                if t < NC_:
                    n = CH[t][1]
                    norm_scale(dve, N_G + t, X[:n, t, :], n, XN[t % 2][:n, :], t >= 2)
                if 1 <= t < NC_ + 1:
                    t0, n = CH[t - 1]
                    norm_gain(dve, N_G + t - 1, G_MQ, n, 4, HT[:, :, t0:t0 + n])
                if 2 <= t < NC_ + 2:
                    t0, n = CH[t - 2]
                    act_low(dve, A_HT2 + t - 1, HT[:, :, t0:t0 + n], HTH2[:, :, t0:t0 + n])
            dve.wait_ge(out_stored, 16 * MIX_STORES)
            for b in range(4):
                s, m = divmod(b, 2)
                dve.wait_ge(km_psum, b + 1)
                nc.vector.tensor_copy(KM[:, s, :, m * P:(m + 1) * P],
                                      bank(2 * (b % 2), 2).rearrange("p (c n) -> p c n", c=KD)).then_inc(km_ready, 1)
            for n in range(W_MQ + 2, W_MO + 2):
                split_low(dve, n)

            def pt_out(a):
                h, m = divmod(a, 5)
                t0, n = CH[m]
                dve.wait_ge(pt_psum, a + 1)
                if m == 0 and h >= 2:
                    dve.wait_ge(ot_psum, 2 * (h - 1))
                nc.vector.tensor_copy(PT[h % 2][:, :, t0:t0 + n],
                                      bank(2 + a % 2)[:, 0:256].rearrange("p (k n) -> p k n", k=2)[:, :, 0:n]
                                      ).then_inc(pt_ready, 1)

            nc.vector.memset(r32(OT_END).bitcast(F32), 0.0)
            nc.vector.memset(r32(OTH_END).bitcast(F32), 0.0)

            def out_low(h):
                for c in (2 * h, 2 * h + 1):
                    act_low(dve, A_OT + c + 1, OT[:, c, :], OTH[:, c, :])

            for a in range(20):
                n = CH[a % 5][1]
                if a % 5 == 3 and a >= 5:
                    out_low(a // 5 - 1)
                dve.wait_ge(ms_psum, a + 1)
                nc.vector.tensor_reduce(NM[:n, a:a + 1], bank(a % 2)[:n, 0:ML], AX.X, ALU.max, negate=True).then_inc(nm_ready, 1)
                if a >= 1:
                    pt_out(a - 1)
                dve.wait_ge(px_ready, a + 1)
                nc.vector.reciprocal(RR[:n, a:a + 1], RS[:n, a:a + 1]).then_inc(rr_ready, 1)
                dve.wait_ge(rr_ready, a + 1)
                nc.vector.tensor_scalar(PX[a % 2][:n, :], PX[a % 2][:n, :], RR[:n, a:a + 1], None, ALU.mult).then_inc(pn_ready, 1)
            pt_out(19)
            out_low(MH - 1)
            add_rows(mo_psum, x2_ready, [W_MO + 2, W_MO + 3])
            for m in range(NC_ + 1):
                if m < NC_:
                    n = CH[m][1]
                    norm_scale(dve, N_I + m, X[:n, m, :], n, XNR[:n, m, :], False)
                if m >= 1:
                    t0, n = CH[m - 1]
                    norm_gain(dve, N_I + m - 1, G_FFN, n, 4, HT[:, :, t0:t0 + n])
            moe_dve(dve)

        def passes(out, parts):
            for k, ((sh, sl), (mh, ml)) in enumerate(parts):
                for j, (a, b) in enumerate(((sh, mh), (sh, ml), (sl, mh))):
                    last = nc.tensor.matmul(out, a, b, start=(k == 0 and j == 0), stop=(k == len(parts) - 1 and j == 2))
            return last

        def tproj(b, n, c, high, low, nk=KD, k0=0):
            for h in range(2):
                t = slice(h * (T // 2), (h + 1) * (T // 2))
                last = passes(bank(b + h)[:, 0:T // 2], [((w_hi(n)[:, k0 + k, c:c + P], w_lo(n)[:, k0 + k, c:c + P]),
                                     (r32(high[:, k, t]), r32(low[:, k, t]))) for k in range(nk)])
            return last

        def rproj(b, n, m, high, low):
            st = lambda flat, k: r32(flat[:, k * T + m * P:k * T + m * P + P])
            return passes(bank(b)[:, 0:256], [((st(high, k), st(low, k)), (w_hi(n)[:, k, :], w_lo(n)[:, k, :]))
                                              for k in range(KD)])


        @block.tensor
        def _(pe):
            pe.wait_ge(consts, 6)
            pe.wait_ge(vec_loaded, 16 * 11)
            nc.tensor.transpose(bank(7)[:, 0:100], VEC[0:100, :], IDENT[0:100, 0:100])
            nc.tensor.transpose(bank(7)[:, 128:164], CTXR[0:36, :], IDENT[0:36, 0:36]).then_inc(vec_psum, 1)
            for i, (_, n) in enumerate(srcA):
                norm_turn(pe, i, XN[i % 2][:n, :], n, 0)
            pe.wait_ge(vec_ready, 2)
            for i in range(20):
                t, m = divmod(i, 5)
                if m == 0:
                    pe.wait_ge(wl_ready, t + 1)
                if t == 0:
                    pe.wait_ge(al_ready, A_HT + (m + 1 if m < 4 else 5))
                if i >= 4:
                    pe.wait_ge(kv_rows, i - 3)
                rproj(4 + i % 4, W_K + t, m, HTH_F, HT_F).then_inc(kv_psum, 1)
            for i in range(4):
                if i % 2 == 0:
                    pe.wait_ge(wl_ready, W_Q + i // 2 + 1)
                if i < 2:
                    pe.wait_ge(ht_ready, 7)
                else:
                    pe.wait_ge(q_ready, i - 1)
                tproj(2 * (i % 2), W_Q + i // 2, (i % 2) * P, HTH, HT).then_inc(q_psum, 1)
            pe.wait_ge(kv_rows, 20)
            pe.wait_ge(past_loaded, 32)
            for b in range(9):
                if b >= 4:
                    pe.wait_ge(kt_ready, b - 3)
                rows = KR[:, b, :] if b < 4 else PKR[:, b - 4, :] if b < 8 else KR[:, 4, :]
                for h in range(4):
                    last = nc.tensor.transpose(bank(4 + b % 4)[:, h * P:(h + 1) * P], rows[:, h * P:(h + 1) * P], IDENT)
                last.then_inc(kt_psum, 1)

            def scores(u):
                if u == 0:
                    pe.wait_ge(q_ready, 4)
                    pe.wait_ge(kt_ready, 9)
                else:
                    pe.wait_ge(z_copied, u)
                if u < SBH:
                    hp, lo = divmod(u, 2)
                    r = slice(64 * lo, 64 * lo + 64)
                    for kc in range(4):
                        o, n = keycols(u, kc)
                        last = nc.tensor.matmul(ps[:, o:o + n], KTA[r, hp, kc * P:(kc + 1) * P], QT[r, hp, kc * P:LP],
                                                start=True, stop=True)
                else:
                    for kc in range(5):
                        for j in range(4):
                            hp, lo = j, u - SBH
                            r = slice(64 * lo, 64 * lo + 64)
                            o = kc * 256 + j * 64
                            last = nc.tensor.matmul(ps[:, o:o + 64], KTA[r, hp, LP + kc * P:LP + (kc + 1) * P],
                                                    QT[r, hp, LP:T], start=True, stop=True)
                last.then_inc(z_psum, 1)

            def sums(u):
                pe.wait_ge(sp_ready, u + 1)
                if u >= 1:
                    pe.wait_ge(u_ready, u)
                nk = 4 if u < SBH else 5
                for kc in range(nk):
                    o, n = keycols(u, kc)
                    for j in range(kc, nk):
                        oj, nj = keycols(u, j)
                        last = nc.tensor.matmul(ps[:, 1536 + o + n - nj:1536 + o + n], TSUF if j == kc else ONES,
                                                LB[u % 2][:, oj:oj + nj], start=(j == kc), stop=(j == nk - 1))
                last.then_inc(s_psum, 1)

            def values(u):
                pe.wait_ge(w_ready, u + 1)
                g = u // 2
                if g >= 2 and u % 2 == 0:
                    pe.wait_ge(ysb_ready, g - 1)
                w = ZSB[u % 3]
                if u < SBH:
                    r = slice(64 * (u % 2), 64 * (u % 2) + 64)
                    for kc in range(4):
                        o, n = keycols(u, kc)
                        last = nc.tensor.matmul(bank(6 + g % 2)[r, kc * P:LP], VR[:, kc, u * HD:(u + 1) * HD], w[:, o:o + n],
                                                start=(kc == 0), stop=(kc == 3))
                else:
                    for j in range(4):
                        h = 2 * j + u - SBH
                        r = slice(64 * (h % 2), 64 * (h % 2) + 64)
                        for kc in range(5):
                            vv = PVR[:, kc, h * HD:(h + 1) * HD] if kc < 4 else VR[:, 4, h * HD:(h + 1) * HD]
                            last = nc.tensor.matmul(bank(6 + g % 2)[r, j * 64:j * 64 + 64], vv,
                                                    w[:, kc * 256 + j * 64:kc * 256 + j * 64 + 64],
                                                    start=(kc == 0), stop=(kc == 4))
                last.then_inc(pv_psum, 1)

            scores(0)
            for u in range(U_):
                if u + 1 < U_:
                    scores(u + 1)
                sums(u)
                if u >= 1:
                    values(u - 1)
            values(U_ - 1)

            for i in range(CONV_C):
                if i % 2 == 0:
                    pe.wait_ge(wl_ready, W_X + i // 2 + 1)
                if i == 0:
                    pe.wait_ge(z_copied, U_)
                    pe.wait_ge(u_ready, U_)
                if i >= 2:
                    pe.wait_ge(xr_ready, i - 1)
                tproj(2 * (i % 2), W_X + i // 2, (i % 2) * P, HTH, HT).then_inc(xb_psum, 1)
            for i in range(KD):
                if i % 2 == 0:
                    pe.wait_ge(wl_ready, W_Z + i // 2 + 1)
                if i < 2:
                    pe.wait_ge(xr_ready, CONV_C - 1 + i)
                else:
                    pe.wait_ge(zt_ready, i - 1)
                tproj(2 * (i % 2), W_Z + i // 2, (i % 2) * P, HTH, HT).then_inc(zt_psum, 1)
            pe.wait_ge(vec_ready, 3)
            pe.wait_ge(ysb_ready, 5)
            for j in range(8):
                last = nc.tensor.matmul(bank(7)[:, 240 + j:241 + j], SELP[0:NH, 2 * j:2 * j + 2, :].rearrange("p a b -> p (a b)"),
                                        HCOL[0:NH, 2:3], start=True, stop=True)
            last.then_inc(dp_psum, 1)
            pe.wait_ge(conv_done, CONV_C)
            for s in range(2):
                nc.tensor.transpose(bank(6)[0:36, P * s:P * (s + 1)], TAIL[:, s].rearrange("p j c -> p (j c)"),
                                    IDENT).then_inc(dp_psum, 1)
            pe.wait_ge(wl_ready, W_DT + 1)
            pe.wait_ge(zt_ready, 7)
            tproj(0, W_DT, 0, HTH, HT).then_inc(dt_psum, 1)
            pe.wait_ge(state_loaded, 16)
            pe.wait_ge(dve_dt, 1)
            pe.wait_ge(zt_ready, 8)
            for b in range(8):
                last = nc.tensor.transpose(bank(1, 2)[:, b * P:(b + 1) * P], H0R[:, b, :], IDENT)
            last.then_inc(pre_psum, 1)
            pe.wait_ge(dve_dt, 7)
            pe.wait_ge(vec_ready, 4)
            for c in range(NC_):
                nc.tensor.transpose(bank(7)[:, 16 * c:16 * c + 16], CUM[0:NH, c * P:(c + 1) * P], IDENT[0:NH, 0:NH])
                nc.tensor.transpose(bank(7)[:, 80 + 16 * c:96 + 16 * c], DTT[0:NH, c * P:(c + 1) * P], IDENT[0:NH, 0:NH])
            nc.tensor.matmul(bank(7)[:, 160:240], ONES[0:NH, :], DIAG[0:NH].rearrange("p c h -> p (c h)"),
                             start=True, stop=True).then_inc(pre_psum, 1)
            pe.wait_ge(pre_dve, 4)
            pe.wait_ge(pre_act, 2)
            pe.wait_ge(xc_ready, CONV_C)
            pe.wait_ge(act_dt, 5)
            pe.wait_ge(pads, 2)
            pe.wait_ge(tail_rows, 2)
            for v in range(10):
                c, g = divmod(v, 2)
                tk = slice(c * P, (c + 1) * P)
                sq = 0 if c < 4 else 1
                if v >= 1:
                    pe.wait_ge(sx_done, v)
                for j in range(4):
                    nc.tensor.transpose(bank(7)[:, j * P:(j + 1) * P], XC[:, 4 * g + j, tk], IDENT)
                nc.tensor.transpose(bank(0)[:, 0:P], XC[:, 8 + g, tk], IDENT)
                nc.tensor.matmul(bank(0)[:, P:2 * P], XC[:, 8 + g, tk], XC[:, 10 + g, tk], start=True, stop=True).then_inc(ssd_tr, 1)
                if v >= 1:
                    pe.wait_ge(seg_done, v)
                for h in range(8):
                    last = nc.tensor.matmul(bank(1, 2)[:, h * P:(h + 1) * P], bc(IDENT[0:NH, 8 * g + h:8 * g + h + 1], [NH, P]), CUM[0:NH, tk],
                                            start=True, stop=True)
                last.then_inc(cumb_psum, 1)
                if v >= 1:
                    pe.wait_ge(ec_done, v)
                for j in range(4):
                    a = 8 * g + 2 * j
                    last = nc.tensor.matmul(bank(5)[:, j * P:(j + 1) * P], SELP[0:NH, a:a + 2, :].rearrange("p a b -> p (a b)"),
                                            ECM[0:NH, tk], start=True, stop=True)
                last.then_inc(ec_psum, 1)
                if v >= 1:
                    pe.wait_ge(t1_done, v)
                if v >= 2:
                    pe.wait_ge(h_ready, v - 1)
                for j in range(4):
                    last = nc.tensor.matmul(bank(4)[:, j * P:(j + 1) * P], HS[:, sq, g, j * P:(j + 1) * P], XC[:, 10 + g, tk],
                                            start=True, stop=True)
                last.then_inc(inter_psum, 1)
                pe.wait_ge(sx_done, v + 1)
                if v >= 1:
                    pe.wait_ge(h_ready, v)
                nc.tensor.matmul(bank(6), BROW[v % 2], XW[v % 2], start=True, stop=True).then_inc(st_psum, 1)
                pe.wait_ge(m_ready, v + 1)
                if v >= 1:
                    pe.wait_ge(t2_done, v)
                for h in range(8):
                    r = slice(64 * (h % 2), 64 * (h % 2) + 64)
                    last = nc.tensor.matmul(bank(3)[r, (h // 2) * P:(h // 2 + 1) * P], XD[v % 2][:, h * HD:(h + 1) * HD],
                                            SEG[v % 2][:, h, :], start=True, stop=True)
                last.then_inc(intra_psum, 1)
            pe.wait_ge(h_ready, 10)
            for s in range(2):
                if s:
                    pe.wait_ge(so_rows, 1)
                for b in range(8):
                    last = nc.tensor.transpose(bank(1, 2)[:, b * P:(b + 1) * P],
                                               HS[:, s].rearrange("p g n -> p (g n)")[:, b * P:(b + 1) * P], IDENT)
                last.then_inc(so_psum, 1)
            pe.wait_ge(so_rows, 2)
            pe.wait_ge(sx_done, 10)
            for i in range(KD):
                pe.wait_ge(sq_ready, i + 1)
                nc.tensor.matmul(bank(0), ONES, SQT[i % 2][:, 0:LP], start=(i == 0), stop=(i == KD - 1))
                nc.tensor.matmul(bank(1)[:, 0:LS], ONES, SQT[i % 2][:, LP:T], start=(i == 0), stop=(i == KD - 1)).then_inc(ssq_psum, 1)
            for c in range(KD):
                na, nb = W_M + 2 * c, W_M + 2 * c + 1
                pe.wait_ge(wl_ready, na + 1)
                if c == 0:
                    pe.wait_ge(rb_ln, 1)
                    pe.wait_ge(t2_done, 10)
                    pe.wait_ge(h_ready, 10)
                else:
                    pe.wait_ge(gs_ready, c)
                tproj(0, na, 0, HTH, HT).then_inc(gs_psum, 1)
                if c:
                    pe.wait_ge(gb_ready, c)
                tproj(2, na, 0, HTH, HT, k0=KD).then_inc(gb_psum, 1)
                if c:
                    pe.wait_ge(m1_done, c)
                else:
                    pe.wait_ge(al_ready, A_ZS + KD)
                pe.wait_ge(wl_ready, nb + 1)
                tproj(4, nb, 0, ZSH, ZS).then_inc(br_psum, 1)
                if c:
                    pe.wait_ge(m2_done, c)
                tproj(6, nb, 0, YSBTH, YSBT, nk=4, k0=KD).then_inc(sb_psum, 1)
            pe.wait_ge(al_ready, A_MG + KD)
            for i in range(4 * NC_):
                t, m = divmod(i, NC_)
                if m == 0:
                    pe.wait_ge(wl_ready, W_O + t + 1)
                if i >= 4:
                    pe.wait_ge(x1_ready, i - 3)
                rproj(i % 4, W_O + t, m, MGH_F, MG_F).then_inc(wo_psum, 1)
            pe.wait_ge(x1_ready, 4 * NC_)
            pe.wait_ge(al_ready, A_MT + 1)
            for i in range(16):
                t, m = divmod(i, 2)
                if m == 0:
                    pe.wait_ge(wl_ready, W_KV + t + 1)
                if i >= 4:
                    pe.wait_ge(mkv_rows, i - 3)
                n = W_KV + t
                passes(bank(i % 4)[:, 0:256], [((r32(MTH[:, k, m * P:(m + 1) * P]), r32(MT[:, k, m * P:(m + 1) * P])),
                                                (w_hi(n)[:, k, :], w_lo(n)[:, k, :])) for k in range(KD)]).then_inc(mkv_psum, 1)
                if m == 1 and 1 <= t <= NC_:
                    n = CH[t - 1][1]
                    norm_turn(pe, N_G + t - 1, XN[(t - 1) % 2][:n, :], n, 4)
            pe.wait_ge(mkv_rows, 16)
            pe.wait_ge(memc_loaded, 32)
            for b in range(4):
                s, m = divmod(b, 2)
                if b >= 2:
                    pe.wait_ge(km_ready, b - 1)
                src = MKV[:, m, 0:D] if s == 0 else MC[:, 0, m, :]
                for c in range(KD):
                    last = nc.tensor.transpose(bank(2 * (b % 2), 2)[:, c * P:(c + 1) * P], src[:, c * P:(c + 1) * P], IDENT)
                last.then_inc(km_psum, 1)
            pe.wait_ge(al_ready, A_HT2 + NC_)
            for i in range(KD):
                if i % 2 == 0:
                    pe.wait_ge(wl_ready, W_MQ + i // 2 + 1)
                if i < 2:
                    pe.wait_ge(km_ready, 3 + i)
                else:
                    pe.wait_ge(mq_ready, i - 1)
                tproj(2 * (i % 2), W_MQ + i // 2, (i % 2) * P, HTH2, HT).then_inc(mq_psum, 1)
            pe.wait_ge(mq_ready, KD)

            def mscores(a):
                h, m = divmod(a, 5)
                t0, n = CH[m]
                if a >= 2:
                    pe.wait_ge(px_ready, a - 1)
                for j in range(2):
                    last = nc.tensor.matmul(bank(a % 2)[:n, 0:ML], QM[:, 2 * h + j, t0:t0 + n],
                                            KM[:, 0 if m < 4 else 1, 2 * h + j, :], start=(j == 0), stop=(j == 1))
                last.then_inc(ms_psum, 1)

            def mvalues(h):
                pe.wait_ge(pt_ready, 5 * (h + 1))
                for dc in range(2):
                    if h >= 1:
                        pe.wait_ge(ot_ready, 2 * (h - 1) + dc + 1)
                    f = h * MHD + dc * P
                    for kc in range(2):
                        nc.tensor.matmul(bank(4 + 2 * dc), MKV[:, kc, D + f:D + f + P], PT[h % 2][:, kc, 0:LP],
                                         start=(kc == 0), stop=(kc == 1))
                    for kc in range(2):
                        last = nc.tensor.matmul(bank(5 + 2 * dc)[:, 0:LS], MC[:, 1, kc, f:f + P], PT[h % 2][:, kc, LP:T],
                                                start=(kc == 0), stop=(kc == 1))
                    last.then_inc(ot_psum, 1)

            mscores(0)
            for a in range(20):
                if a + 1 < 20:
                    mscores(a + 1)
                n = CH[a % 5][1]
                pe.wait_ge(pn_ready, a + 1)
                if a >= 2:
                    pe.wait_ge(pt_ready, a - 1)
                for kc in range(2):
                    last = nc.tensor.transpose(bank(2 + a % 2)[:, kc * P:kc * P + n], PX[a % 2][:n, kc * P:(kc + 1) * P],
                                               IDENT[:n, :n])
                last.then_inc(pt_psum, 1)
                if a % 5 == 0 and a >= 5:
                    mvalues(a // 5 - 1)
            mvalues(MH - 1)
            pe.wait_ge(al_ready, A_OT + KD)
            pe.wait_ge(px_ready, 20)
            pe.wait_ge(pt_ready, 20)
            for i in range(4 * NC_):
                t, m = divmod(i, NC_)
                if m == 0:
                    pe.wait_ge(wl_ready, W_MO + t + 1)
                if i >= 4:
                    pe.wait_ge(x2_ready, i - 3)
                rproj(i % 4, W_MO + t, m, OTH_F, OT_F).then_inc(mo_psum, 1)
            for i, (_, n) in enumerate(CH):
                norm_turn(pe, N_I + i, XNR[:n, i, :], n, 4)
                if i:
                    router_scores(pe, i - 1)
            moe_pe(pe)


_INS = ["x_prompt", "x_sample", "cache_sb_k", "cache_sb_v", "state_ssm", "state_conv", "cache_mem_k", "cache_mem_v",
        "mem_prompt", "norm_mix", "w_in", "conv_w", "conv_b", "dt_bias", "a_log", "d_skip", "ssm_norm", "w_ssm_br",
        "w_sb_br", "w_out", "norm_mem_q", "norm_mem_kv", "w_mem_q", "w_mem_kv", "w_mem_o", "norm_ffn",
        "w_group_router", "w_expert_router", "w_gate_e", "w_up_e", "w_down_e", "norm_final"]
_OUTS = [("y_prompt", (1, LP, D)), ("y_sample", (1, LS, D)),
         ("sb_k_prompt", (1, 1, LP, SBH, 64)), ("sb_v_prompt", (1, 1, LP, SBH, 64)),
         ("ssm_prompt", (1, 1, NH, HD, NS)), ("conv_prompt", (1, 1, 3, CONV_C * P)),
         ("mem_k_prompt", (1, 1, ML, MH, MHD)), ("mem_v_prompt", (1, 1, ML, MH, MHD)),
         ("sb_k_sample", (1, 1, LS, SBH, 64)), ("sb_v_sample", (1, 1, LS, SBH, 64)),
         ("ssm_sample", (1, 1, NH, HD, NS)), ("conv_sample", (1, 1, 3, CONV_C * P))]


def kernel(**inputs):
    import concourse.bacc as bacc
    from concourse.bass_utils import run_bass_kernel_spmd

    nc = bacc.Bacc("TRN2", target_bir_lowering=False, num_devices=1)
    arrays, ins = {}, {}
    for name in _INS:
        a = np.ascontiguousarray(inputs[name])
        arrays["in_" + name] = a
        ins[name] = nc.dram_tensor("in_" + name, a.shape, mybir.dt.from_np(a.dtype), kind="ExternalInput").ap()
    outs = {name: nc.dram_tensor("out_" + name, shape, F32, kind="ExternalOutput").ap() for name, shape in _OUTS}
    encoder_step(nc, ins, outs)
    r = run_bass_kernel_spmd(nc, [arrays], core_ids=[0])
    return tuple(r.results[0]["out_" + name] for name, _ in _OUTS)
```
